# Optimizing a Trainium2 kernel written in Bass

```python
import jax, jax.numpy as jnp
from jax import lax
import numpy as np

D_MODEL = 1024
BATCH = 1
SEQ = 512
DEPTH = 1

GRID_W = 64
CTX_LEN = 256
N_HEADS = 8
QK_NOPE_DIM = 64
QK_ROPE_DIM = 32
V_HEAD_DIM = 64
Q_LORA_RANK = 384
KV_LORA_RANK = 256
ROPE_THETA = 10000.0
CONV_DIM = 512
CONV_WIDTH = 3
D_FF = 2816
Q_BLOCK = 128
EPS = 1e-6
ATTN_DIM = N_HEADS * V_HEAD_DIM
KV_END = KV_LORA_RANK
KR_END = KV_END + QK_ROPE_DIM
Q_END = KR_END + Q_LORA_RANK
CX_END = Q_END + CONV_DIM
CB_END = CX_END + CONV_DIM
CC_END = CB_END + CONV_DIM
GA_END = CC_END + D_MODEL
GC_END = GA_END + D_MODEL
IN_COLS = GC_END

kernel_name = 'hybrid_mla_shortconv_convffn_dit_block'

def rmsnorm(x, g):
    xf = x.astype(jnp.float32)
    y = xf * lax.rsqrt(jnp.mean(xf * xf, axis=-1, keepdims=True) + EPS)
    return (y * g.astype(jnp.float32)).astype(x.dtype)

def modulate(h, shift, scale):
    return h * (1 + scale[:, None, :]) + shift[:, None, :]

def dwconv(x, w, b):
    T = x.shape[1]
    pad = CONV_WIDTH // 2
    xp = jnp.pad(x, ((0, 0), (pad, CONV_WIDTH - 1 - pad), (0, 0)))
    y = b
    for k in range(CONV_WIDTH):
        y = y + xp[:, k:k + T] * w[k]
    return y

def axial_angles(rows):
    row = jnp.repeat(jnp.arange(rows), GRID_W).astype(jnp.float32)
    col = jnp.tile(jnp.arange(GRID_W), rows).astype(jnp.float32)
    axis_dim = QK_ROPE_DIM // 2
    inv = ROPE_THETA ** (-jnp.arange(0, axis_dim, 2, dtype=jnp.float32) / axis_dim)
    return jnp.concatenate([row[:, None] * inv, col[:, None] * inv], axis=-1)

def rope2d(x, ang):
    nf = QK_ROPE_DIM // 4
    xr = x.reshape(*x.shape[:-1], 2, 2, nf)
    x1, x2 = xr[..., 0, :], xr[..., 1, :]
    a = ang.reshape(ang.shape[0], 1, 2, nf)
    cos, sin = jnp.cos(a).astype(x.dtype), jnp.sin(a).astype(x.dtype)
    out = jnp.stack([x1 * cos - x2 * sin, x1 * sin + x2 * cos], axis=-2)
    return out.reshape(x.shape)

def mla_kv(p, kv_norm_g, w_ukv, ang):
    B, T = p.shape[:2]
    ckv = rmsnorm(p[..., :KV_END], kv_norm_g)
    kv = (ckv @ w_ukv).reshape(B, T, N_HEADS, QK_NOPE_DIM + V_HEAD_DIM)
    k_nope, v = kv[..., :QK_NOPE_DIM], kv[..., QK_NOPE_DIM:]
    k_rope = p[..., KV_END:KR_END][:, :, None, :]
    if ang is not None:
        k_rope = rope2d(k_rope, ang)
    return k_nope, k_rope[:, :, 0], v

def mla_query(p, q_norm_g, w_uq, ang):
    B, T = p.shape[:2]
    cq = rmsnorm(p[..., KR_END:Q_END], q_norm_g)
    q = (cq @ w_uq).reshape(B, T, N_HEADS, QK_NOPE_DIM + QK_ROPE_DIM)
    q_nope, q_rope = q[..., :QK_NOPE_DIM], q[..., QK_NOPE_DIM:]
    if ang is not None:
        q_rope = rope2d(q_rope, ang)
    return q_nope, q_rope

def mla_attend(q_nope, q_rope, k_nope, k_rope, v):
    scale = (QK_NOPE_DIM + QK_ROPE_DIM) ** -0.5
    s = (jnp.einsum('bqhd,bkhd->bhqk', q_nope, k_nope)
         + jnp.einsum('bqhr,bkr->bhqk', q_rope, k_rope))
    pr = jax.nn.softmax(s.astype(jnp.float32) * scale, axis=-1).astype(v.dtype)
    return jnp.einsum('bhqk,bkhd->bqhd', pr, v)

def mla_latent(q_nope, q_rope, k_nope, k_rope, v):
    B, T = q_nope.shape[:2]
    nb = T // Q_BLOCK

    def blocks(a):
        return a.reshape(B, nb, Q_BLOCK, *a.shape[2:]).swapaxes(0, 1)

    o = lax.map(lambda qs: mla_attend(qs[0], qs[1], k_nope, k_rope, v), (blocks(q_nope), blocks(q_rope)))
    return o.swapaxes(0, 1).reshape(B, T, ATTN_DIM)

def gated_merge(p, o_attn, conv_w, conv_b, w_attn_out, w_conv_out, w_o):
    x_in = p[..., Q_END:CX_END]
    b_gate = p[..., CX_END:CB_END]
    c_gate = p[..., CB_END:CC_END]
    y_conv = (b_gate * dwconv(c_gate * x_in, conv_w, conv_b)) @ w_conv_out
    y_attn = o_attn @ w_attn_out
    g_attn = jax.nn.sigmoid(p[..., CC_END:GA_END])
    g_conv = jax.nn.sigmoid(p[..., GA_END:GC_END])
    return (g_attn * y_attn + g_conv * y_conv) @ w_o

def conv_ffn(h, w_up, conv_w, conv_b, w_down):
    u = dwconv(h @ w_up, conv_w, conv_b)
    gate, val = jnp.split(u, 2, axis=-1)
    return (jax.nn.silu(gate) * val) @ w_down

def trunk_layer(x, ctx, mod_lat, mod_ctx, ang, update_ctx, norm1_g, w_in, q_norm_g, kv_norm_g,
                w_uq, w_ukv, conv_w, conv_b, w_attn_out, w_conv_out, w_o, norm2_g, w_up,
                ffn_conv_w, ffn_conv_b, w_down):
    sh1, sc1, g1, sh2, sc2, g2 = jnp.split(mod_lat, 6, axis=-1)
    csh1, csc1, cg1, csh2, csc2, cg2 = jnp.split(mod_ctx, 6, axis=-1)
    h = modulate(rmsnorm(x, norm1_g), sh1, sc1)
    hc = modulate(rmsnorm(ctx, norm1_g), csh1, csc1)
    p = h @ w_in
    pc = hc @ w_in if update_ctx else hc @ w_in[:, :KR_END]
    kn_c, kr_c, v_c = mla_kv(pc, kv_norm_g, w_ukv, None)
    kn_l, kr_l, v_l = mla_kv(p, kv_norm_g, w_ukv, ang)
    qn, qr = mla_query(p, q_norm_g, w_uq, ang)
    o = mla_latent(qn, qr, jnp.concatenate([kn_c, kn_l], axis=1),
                   jnp.concatenate([kr_c, kr_l], axis=1), jnp.concatenate([v_c, v_l], axis=1))
    x = x + g1[:, None, :] * gated_merge(p, o, conv_w, conv_b, w_attn_out, w_conv_out, w_o)
    x = x + g2[:, None, :] * conv_ffn(modulate(rmsnorm(x, norm2_g), sh2, sc2), w_up, ffn_conv_w, ffn_conv_b, w_down)
    if update_ctx:
        qn_c, qr_c = mla_query(pc, q_norm_g, w_uq, None)
        oc = mla_attend(qn_c, qr_c, kn_c, kr_c, v_c).reshape(ctx.shape[0], ctx.shape[1], ATTN_DIM)
        ctx = ctx + cg1[:, None, :] * gated_merge(pc, oc, conv_w, conv_b, w_attn_out, w_conv_out, w_o)
        ctx = ctx + cg2[:, None, :] * conv_ffn(modulate(rmsnorm(ctx, norm2_g), csh2, csc2), w_up, ffn_conv_w, ffn_conv_b, w_down)
    return x, ctx

def setup_inputs(seed: int = 0) -> dict:
    key = jax.random.key(seed)
    ks = jax.random.split(key, 24)
    L, D = DEPTH, D_MODEL

    def nrm(k, shape, fan_in, gain=1.0):
        return jax.random.normal(k, shape, jnp.float32) * (gain * fan_in ** -0.5)

    def norm_gain(k, shape):
        return 1.0 + 0.05 * jax.random.normal(k, shape, jnp.float32)

    def bias(k, shape):
        return 0.02 * jax.random.normal(k, shape, jnp.float32)

    return {
        'x': jax.random.normal(ks[0], (BATCH, SEQ, D), jnp.float32),
        'c': jax.random.normal(ks[1], (BATCH, D), jnp.float32),
        'ctx': jax.random.normal(ks[2], (BATCH, CTX_LEN, D), jnp.float32),
        'c_ctx': jax.random.normal(ks[3], (D,), jnp.float32),
        'w_ada': nrm(ks[4], (L, D, 6 * D), D, 0.5),
        'b_ada': bias(ks[5], (L, 6 * D)),
        'norm1_g': norm_gain(ks[6], (L, D)),
        'w_in': nrm(ks[7], (L, D, IN_COLS), D),
        'q_norm_g': norm_gain(ks[8], (L, Q_LORA_RANK)),
        'kv_norm_g': norm_gain(ks[9], (L, KV_LORA_RANK)),
        'w_uq': nrm(ks[10], (L, Q_LORA_RANK, N_HEADS * (QK_NOPE_DIM + QK_ROPE_DIM)), Q_LORA_RANK),
        'w_ukv': nrm(ks[11], (L, KV_LORA_RANK, N_HEADS * (QK_NOPE_DIM + V_HEAD_DIM)), KV_LORA_RANK),
        'conv_w': nrm(ks[12], (L, CONV_WIDTH, CONV_DIM), CONV_WIDTH),
        'conv_b': bias(ks[13], (L, CONV_DIM)),
        'w_attn_out': nrm(ks[14], (L, ATTN_DIM, D), ATTN_DIM),
        'w_conv_out': nrm(ks[15], (L, CONV_DIM, D), CONV_DIM),
        'w_o': nrm(ks[16], (L, D, D), D),
        'norm2_g': norm_gain(ks[17], (L, D)),
        'w_up': nrm(ks[18], (L, D, 2 * D_FF), D),
        'ffn_conv_w': nrm(ks[19], (L, CONV_WIDTH, 2 * D_FF), CONV_WIDTH),
        'ffn_conv_b': bias(ks[20], (L, 2 * D_FF)),
        'w_down': nrm(ks[21], (L, D_FF, D), D_FF),
        'final_g': norm_gain(ks[22], (D,)),
    }

def reference(x, c, ctx, c_ctx, w_ada, b_ada, norm1_g, w_in, q_norm_g, kv_norm_g, w_uq, w_ukv,
              conv_w, conv_b, w_attn_out, w_conv_out, w_o, norm2_g, w_up, ffn_conv_w, ffn_conv_b,
              w_down, final_g):
    rows = x.shape[1] // GRID_W
    ang = axial_angles(rows)
    sc = jax.nn.silu(c)
    sc_ctx = jax.nn.silu(c_ctx)[None, :]
    for i in range(DEPTH):
        mod_lat = sc @ w_ada[i] + b_ada[i]
        mod_ctx = sc_ctx @ w_ada[i] + b_ada[i]
        x, ctx = trunk_layer(x, ctx, mod_lat, mod_ctx, ang, i < DEPTH - 1, norm1_g[i], w_in[i],
                             q_norm_g[i], kv_norm_g[i], w_uq[i], w_ukv[i], conv_w[i], conv_b[i],
                             w_attn_out[i], w_conv_out[i], w_o[i], norm2_g[i], w_up[i],
                             ffn_conv_w[i], ffn_conv_b[i], w_down[i])
    return rmsnorm(x, final_g)


_drawn_inputs = setup_inputs


def setup_inputs(seed=0):
    import zlib

    import numpy as np

    out = dict(_drawn_inputs(seed))
    spreads = {}
    factors = {'ctx': 8.0,
     'c_ctx': 4.159,
     'norm1_g': 3.045,
     'q_norm_g': 8.0,
     'kv_norm_g': 8.0,
     'w_uq': 4.16,
     'conv_b': 26.147,
     'norm2_g': 3.579,
     'ffn_conv_b': 8.0}
    for name, (base, spread) in spreads.items():
        noise = np.random.default_rng([zlib.crc32(name.encode()), seed]).standard_normal(out[name].shape)
        drawn = base * np.exp(spread * noise) if base else spread * noise
        out[name] = __import__('jax').numpy.asarray(drawn.astype(out[name].dtype))
    for name, factor in factors.items():
        out[name] = (out[name] * factor).astype(out[name].dtype)
    return out
```

```python
from contextlib import ExitStack

import numpy as np

import concourse.bass as bass
from concourse import mybir

F32 = mybir.dt.float32
F32R = mybir.dt.float32r
ACT = mybir.ActivationFunctionType
ALU = mybir.AluOpType
AX = mybir.AxisListType

P = 128
D = 1024
T = 512
C = 256
K = T + C
GRID_W = 64
HEADS = 8
NOPE, ROPE, VDIM = 64, 32, 64
QK = NOPE + ROPE
QR, KVR = 384, 256
CONV = 512
FF = 2816
EPS = 1e-6
THETA = 10000.0
KV_END = KVR
KR_END = KV_END + ROPE
Q_END = KR_END + QR
CX_END = Q_END + CONV
CB_END = CX_END + CONV
CC_END = CB_END + CONV
GA_END = CC_END + D
DT = D // P
QT, KVT, CT, FT = QR // P, KVR // P, CONV // P, FF // P
TT, CTT, KT = T // P, C // P, K // P
SCALE = float(QK) ** -0.5
SLOTS = 4
UNIT = 1024
BANK = 512

R_C, R_CC, R_BADA, R_N1, R_N2, R_FG = 0, 8, 16, 64, 72, 80
R_QG = 88
R_KVG = R_QG + QT
R_CB = R_KVG + KVT
R_CW = R_CB + CT
R_END0 = R_CW + 3 * CT
R_FW = P
R_FB = R_FW + 6 * FT
R_END = R_FB + 2 * FT

U_KV, U_KR, U_Q, U_V, U_UQ, U_N = 0, 2, 3, 6, 7, 11
U_CONV = 12
U_MERGE = U_CONV + 3 * CT
U_O = U_MERGE + 3 * DT
U_UP = U_O + DT
U_DOWN = U_UP + 2 * FT
U_ALL = U_DOWN + FT
CONV_SPLITS = (8, 14, 20, 26)


def build(nc, x, c, ctx, c_ctx, w_ada, b_ada, norm1_g, w_in, q_norm_g, kv_norm_g, w_uq, w_ukv, conv_w,
          conv_b, w_attn_out, w_conv_out, w_o, norm2_g, w_up, ffn_conv_w, ffn_conv_b, w_down, final_g,
          rope_tab, out):
    stack = ExitStack()
    with stack:
        def sem(name):
            return stack.enter_context(nc.semaphore(name))

        def sb(name, shape, dt=F32, scope=stack):
            return scope.enter_context(nc.sbuf_tensor(name, shape, dt))

        raw = sb("raw", [P, SLOTS, UNIT])
        whi = sb("whi", [P, SLOTS, UNIT], F32R)
        wlo = sb("wlo", [P, SLOTS, UNIT], F32R)
        hhi = sb("hhi", [P, DT, T], F32R)
        hlo = sb("hlo", [P, DT, T], F32R)
        work = sb("work", [P, 6, T])
        tab = sb("tab", [P, T])
        ident = sb("ident", [P, P])
        ones = sb("ones", [P, P])
        eps = sb("eps", [P, 1])
        prm = sb("prm", [P, R_END])
        mod = sb("mod", [P, 6 * DT])
        modc = sb("modc", [P, 2 * DT])
        gain = sb("gain", [P, 3, DT])
        cvec = sb("cvec", [P, DT, 2])
        small = sb("small", [P, 32])

        early = ExitStack()
        xt = sb("xt", [P, KT, D], scope=early)
        sb("gap0", [P, 2048], scope=early)
        chi = sb("chi", [P, DT, C], F32R, scope=early)
        clo = sb("clo", [P, DT, C], F32R, scope=early)
        rows1 = sb("rows1", [2, 2 * D], scope=early)
        xnT = sb("xnT", [P, DT, K], scope=early)
        ada1 = sb("ada1", [P, 3, 2 * D], scope=early)
        ht = sb("ht", [P, 2, K], scope=early)
        early.close()
        att = ExitStack()
        qhi = sb("qhi", [P, HEADS, T], F32R, scope=att)
        qlo = sb("qlo", [P, HEADS, T], F32R, scope=att)
        cq = ExitStack()
        cqhi = sb("cqhi", [P, QT, T], F32R, scope=cq)
        cqlo = sb("cqlo", [P, QT, T], F32R, scope=cq)
        cqraw = sb("cqraw", [P, QT, T], scope=cq)
        cq.close()
        pthi = sb("pthi", [P, KT, T], F32R, scope=att)
        ptlo = sb("ptlo", [P, KT, T], F32R, scope=att)
        ckhi = sb("ckhi", [P, KVT, K], F32R, scope=att)
        cklo = sb("cklo", [P, KVT, K], F32R, scope=att)
        khi = sb("khi", [P, 2, K], F32R, scope=att)
        klo = sb("klo", [P, 2, K], F32R, scope=att)
        vs = sb("vs", [P, KT, HEADS, 2 * VDIM], F32R, scope=att)
        pr = ExitStack()
        ckraw = sb("ckraw", [P, KVT, K], scope=pr)
        pr.close()
        prob = sb("prob", [P, 2, K], scope=att)
        att.close()
        mrg = ExitStack()
        sb("gap1", [P, 2 * HEADS * T], scope=mrg)
        zhi = sb("zhi", [P, CT, T], F32R, scope=mrg)
        zlo = sb("zlo", [P, CT, T], F32R, scope=mrg)
        mhi = sb("mhi", [P, DT, T], F32R, scope=mrg)
        mlo = sb("mlo", [P, DT, T], F32R, scope=mrg)
        ada2 = sb("ada2", [P, 2, D], scope=mrg)
        sb("gap2", [P, 1536], scope=mrg)
        x2 = ExitStack()
        x2T = sb("x2T", [P, DT, T], scope=x2)
        x2.close()
        adacc = sb("adacc", [P, 4 * D], scope=mrg)
        mrg.close()
        res = ExitStack()
        rows2 = sb("rows2", [1, 4 * D], scope=res)
        sb("gap3", [P, 4096], scope=res)
        xtok = sb("xtok", [P, TT, D], scope=res)
        res.close()
        ffn = ExitStack()
        fhi = sb("fhi", [P, FT, T], F32R, scope=ffn)
        flo = sb("flo", [P, FT, T], F32R, scope=ffn)
        ffn.close()
        fin = ExitStack()
        yo = sb("yo", [P, TT, D], scope=fin)
        fin.close()

        ps = stack.enter_context(nc.psum_tensor("ps", [P, 8, BANK], F32))

        def wide(bank):
            return ps[:, bank:bank + 2, :].rearrange("p b n -> p (b n)")[:, 0:K]

        raw_loaded = [sem(f"raw_loaded{s}") for s in range(SLOTS)]
        w_hi, w_lo, w_used = sem("w_hi"), sem("w_lo"), sem("w_used")
        S = {}

        def s(name):
            if name not in S:
                S[name] = sem(name)
            return S[name]

        def wait(e, semaphore, value):
            if not (isinstance(value, int) and value <= 0):
                e.wait_ge(semaphore, value)

        def col(t, at):
            return t[:, bass.ds(at, 1)] if not isinstance(at, int) else t[:, at:at + 1]

        def at1(t, i):
            if isinstance(i, int):
                return t[:, i, :]
            return t[:, bass.ds(i, 1), :].rearrange("p a n -> p (a n)")

        def rows_of(w, k0, k1, c0, n):
            cols = w[:, c0:c0 + n] if isinstance(c0, int) else w[:, bass.ds(c0, n)]
            return cols.rearrange("(k p) n -> p k n", p=P)[:, k0:k1, :]

        def load(sp, u, slot, pieces):
            wait(sp, w_lo, u - SLOTS + 1)
            if not isinstance(u, int):
                sp.sem_inc(s("load_turn"), 1)
            for dst, src in pieces:
                sp.dma_start(dst, src).then_inc(raw_loaded[slot], 16)

        def column_tile(slot, w, c0, kt=DT):
            view = raw[:, slot, 0:kt * P].rearrange("p (k n) -> p k n", n=P)
            h = kt // 2
            return [(view[:, 0:h, :], rows_of(w, 0, h, c0, P)), (view[:, h:kt, :], rows_of(w, h, kt, c0, P))]

        def merge_tile(slot, d):
            view = raw[:, slot, :].rearrange("p (k n) -> p k n", n=P)
            return [(view[:, 0:CT, :], rows_of(w_attn_out, 0, CT, d * P, P)),
                    (view[:, CT:2 * CT, :], rows_of(w_conv_out, 0, CT, d * P, P))]

        def down_tile(slot, k):
            r = w_down[k * P:(k + 1) * P, :] if isinstance(k, int) else w_down[bass.ds(k * P, P), :]
            return [(raw[:, slot, 0:512], r[:, 0:512]), (raw[:, slot, 512:1024], r[:, 512:1024])]

        def arrived(e, u, slot):
            e.wait_ge(raw_loaded[slot], 32 * ((u - slot) // SLOTS + 1) if isinstance(u, int) else (u - slot) * 8 + 32)

        def plain(t, slot, n=UNIT):
            return [t[:, slot, 0:n]]

        def headed_raw(slot, g):
            v = raw[:, slot, 0:g * QK].rearrange("p (g n) -> p g n", n=QK)
            r = v[:, :, NOPE:QK].rearrange("p g (a h j) -> p g a h j", a=2, h=2)
            return [v, r[:, :, :, 1, :], r[:, :, :, 0, :]]

        def headed(t, slot, g):
            v = t[:, slot, 0:g * P].rearrange("p (g n) -> p g n", n=P)
            r = v[:, :, QK:P].rearrange("p g (a h j) -> p g a h j", a=2, h=2)
            return [v[:, :, 0:QK], r[:, :, :, 0, :], r[:, :, :, 1, :]]

        def views(u, slot):
            if isinstance(u, int) and u == U_KR:
                return headed_raw(slot, DT), headed(whi, slot, DT), headed(wlo, slot, DT)
            if isinstance(u, int) and U_UQ <= u < U_UQ + 4:
                return headed_raw(slot, 2 * QT), headed(whi, slot, 2 * QT), headed(wlo, slot, 2 * QT)
            return plain(raw, slot), plain(whi, slot), plain(wlo, slot)

        def split_hi(act, u, slot):
            arrived(act, u, slot)
            wait(act, w_used, u - SLOTS + 1)
            rv, hv, _ = views(u, slot)
            for n, (r, h) in enumerate(zip(rv, hv)):
                ins = nc.scalar.activation(h, r, ACT.Copy)
            ins.then_inc(w_hi, 1)

        def split_lo(pool, u, slot):
            pool.wait_ge(w_hi, u + 1)
            rv, hv, lv = views(u, slot)
            for r, h, l in zip(rv, hv, lv):
                ins = nc.gpsimd.tensor_tensor(out=l, in0=r, in1=h.bitcast(F32), op=ALU.subtract)
            ins.then_inc(w_lo, 1)

        def used(e, u):
            e.wait_ge(w_used, u + 1)

        def query_ready(e, h):
            if h % 2 == 0:
                e.wait_ge(s("q_ps"), h // 2 + 1)
            else:
                used(e, U_UQ + h // 2)

        def keys_ready(e, pair, part):
            if (pair, part) == (HEADS // 2 - 1, 1):
                used(e, U_N)
            else:
                e.wait_ge(s("k_ps"), 2 * pair + part + 1)

        flat = work[:].rearrange("p a n -> p (a n)")
        sqk = [flat[:, m * K:(m + 1) * K] for m in range(2)]
        G = flat[:, 0:3 * P].rearrange("p (g n) -> p g n", n=P)

        def tile_of(t, slot, k, n=P):
            return t[:, slot, k * n:(k + 1) * n]

        def mm3(pe, o, l, r, start, stop):
            pe.matmul(o, l[0], r[0], start=start, stop=False)
            pe.matmul(o, l[0], r[1], start=False, stop=False)
            return pe.matmul(o, l[1], r[0], start=False, stop=stop)

        def project(pe, o, slot, hi, lo, kt=DT, k0=0, start=True, stop=True):
            for k in range(kt):
                last = mm3(pe, o, (tile_of(whi, slot, k0 + k), tile_of(wlo, slot, k0 + k)),
                           (hi[:, k, :], lo[:, k, :]), start and k == 0, stop and k == kt - 1)
            return last

        def x3_add(dve, d):
            dve.wait_ge(s("x3_sq"), d + 1)
            if d == 0:
                nc.vector.tensor_copy(work[:, 2, :], work[:, 0, :]).then_inc(s("x3_ssq"), 1)
            else:
                dve.wait_ge(s("x3_ssq"), d)
                nc.vector.tensor_tensor(out=work[:, 2, :], in0=work[:, 2, :], in1=work[:, d % 2, :], op=ALU.add).then_inc(s("x3_ssq"), 1)

        block = stack.enter_context(nc.Block())

        @block.sync
        def _(sp):
            for k in range(DT):
                wait(sp, s("ada1_used"), k - 2)
                sp.dma_start(ada1[:, k % 3, :], w_ada[k * P:(k + 1) * P, 0:2 * D]).then_inc(s(f"ada1_loaded{k % 3}"), 16)
            for m in range(2):
                load(sp, U_KV + m, m, column_tile(m, w_in, m * P))
            kr = raw[:, 2, 0:DT * QK].rearrange("p (k n) -> p k n", n=QK)
            load(sp, U_KR, 2, [(kr[:, k:k + 4, :], rows_of(w_in, k, k + 4, KR_END - QK, QK)) for k in (0, 4)])
            for m in range(QT):
                slot = (U_Q + m) % SLOTS
                load(sp, U_Q + m, slot, column_tile(slot, w_in, KR_END + m * P))
            ukv = w_ukv.rearrange("(k p) (h n) -> p k h n", p=P, n=NOPE + VDIM)
            slot = U_V % SLOTS
            load(sp, U_V, slot, [(raw[:, slot, k * 512:(k + 1) * 512].rearrange("p (h n) -> p h n", n=VDIM),
                                  ukv[:, k, :, NOPE:]) for k in range(KVT)])
            for m in range(4):
                slot = (U_UQ + m) % SLOTS
                view = raw[:, slot, 0:2 * QT * QK].rearrange("p (k h n) -> p k h n", k=QT, n=QK)
                load(sp, U_UQ + m, slot, [(view[:, :, h, :], rows_of(w_uq, 0, QT, (2 * m + h) * QK, QK)) for h in (0, 1)])
            slot = U_N % SLOTS
            load(sp, U_N, slot, [(raw[:, slot, k * 512:(k + 1) * 512].rearrange("p (h n) -> p h n", n=NOPE),
                                  ukv[:, k, :, 0:NOPE]) for k in range(KVT)])

            def load_ada2(n, k, g):
                wait(sp, s("ada2_used"), n - 1)
                if not isinstance(n, int):
                    sp.sem_inc(s("load_turn"), 1)
                rows = w_ada[k * P:(k + 1) * P, :] if isinstance(k, int) else w_ada[bass.ds(k * P, P), :]
                sp.dma_start(ada2[:, g % 2, :], rows[:, (2 + g) * D:(3 + g) * D]).then_inc(s(f"ada2_loaded{g % 2}"), 16)

            for j in range(CT):
                for n, end in enumerate((Q_END, CB_END, CX_END)):
                    u = U_CONV + 3 * j + n
                    load(sp, u, u % SLOTS, column_tile(u % SLOTS, w_in, end + j * P))
                    if (j, n) in ((2, 1), (3, 1)):
                        if j == 2:
                            sp.wait_ge(s("pv_ps"), HEADS)
                        for m in range(2):
                            load_ada2(2 * (j - 2) + m, 0, 2 * (j - 2) + m)

            def merge_loads(i):
                for n in range(12):
                    dd, what = n // 3, n % 3
                    d = 4 * i + dd
                    u = U_MERGE + 12 * i + n
                    slot = n % SLOTS
                    load(sp, u, slot, merge_tile(slot, d) if what == 2 else
                         column_tile(slot, w_in, (CC_END, GA_END)[what] + d * P))
                    load_ada2(4 + 12 * i + n, 1 + 3 * i + n // 4, n % 4)

            with sp.Fori(0, 2) as i:
                merge_loads(i)
            for d in range(SLOTS):
                load(sp, U_O + d, d, column_tile(d, w_o, d * P))
                load_ada2(4 * (DT - 1) + d, DT - 1, d)
            used(sp, U_O - 1)
            for t in range(TT):
                sp.dma_start(xtok[:, t, :], x[t * P:(t + 1) * P, :]).then_inc(s("xtok_loaded"), 16)
            for d in range(SLOTS, DT):
                load(sp, U_O + d, d - SLOTS, column_tile(d - SLOTS, w_o, d * P))
            with sp.Fori(0, FT // 2) as i:
                for n in range(4):
                    load(sp, U_UP + 4 * i + n, n, column_tile(n, w_up, (n % 2) * FF + (2 * i + n // 2) * P))
            with sp.Fori(0, FT // 4) as i:
                for n in range(4):
                    load(sp, U_DOWN + 4 * i + n, n, down_tile(n, 4 * i + n))
            for k in range(FT // 4 * 4, FT):
                load(sp, U_DOWN + k, k % 4, down_tile(k % 4, k))
            for t in range(TT):
                sp.wait_ge(s("y_tok_act"), t + 1)
                sp.wait_ge(s("y_tok_dve"), t + 1)
                sp.dma_start(out[t * P:(t + 1) * P, :], yo[:, t, :]).then_inc(s("stored"), 16)
            sp.wait_ge(s("stored"), 16 * TT)

        @block.gpsimd
        def _(pool):
            nc.gpsimd.memset(ident[:], 0.0).then_inc(s("consts"), 1)
            nc.gpsimd.memset(ones[:], 1.0).then_inc(s("consts"), 1)
            nc.gpsimd.memset(eps[:], EPS).then_inc(s("consts"), 1)
            pool.wait_ge(s("consts"), 3)
            nc.gpsimd.affine_select(out=ident[:], in_=ident[:], compare_op=ALU.not_equal, fill=1.0, base=0,
                                    pattern=[[-1, P]], channel_multiplier=1).then_inc(s("consts"), 1)
            pool.wait_ge(s("mods1"), 6)
            for k in range(DT):
                wait(pool, s("h_lo"), 2 * (k - 1))
                for lo, hi, g, m in ((0, T, 0, mod), (T, K, 1, modc)):
                    nc.gpsimd.tensor_scalar(ht[:, k % 2, lo:hi], xnT[:, k, lo:hi], gain[:, g, k:k + 1],
                                            m[:, k:k + 1], ALU.mult, ALU.add).then_inc(s("h_t"), 1)
            for u in range(U_CONV):
                split_lo(pool, u, u % SLOTS)
            for g in range(HEADS * TT):
                pool.wait_ge(s("rsum"), g + 1)
                nc.gpsimd.tensor_scalar(prob[:, g % 2, :], prob[:, g % 2, :], small[:, 20 + g % 2:21 + g % 2], None,
                                        ALU.mult).then_inc(s("p_norm"), 1)
                if g - 1 in CONV_SPLITS:
                    n = CONV_SPLITS.index(g - 1)
                    split_lo(pool, U_CONV + n, n)
            for u in range(U_CONV + 4, U_MERGE):
                split_lo(pool, u, u % SLOTS)
            with pool.Fori(0, (U_DOWN - U_MERGE) // 4) as i:
                for n in range(4):
                    split_lo(pool, U_MERGE + 4 * i + n, n)
            with pool.Fori(0, FT // 4) as i:
                for n in range(4):
                    split_lo(pool, U_DOWN + 4 * i + n, n)
            for k in range(FT // 4 * 4, FT):
                split_lo(pool, U_DOWN + k, k % 4)

        @block.scalar
        def _(act):

            def rows_to(g, r0, a, n):
                act.dma_start(G[r0:r0 + n, g, :], a).then_inc(s("prm_loaded"), 16)

            rows_to(0, R_C, c.rearrange("a (r n) -> (a r) n", n=P), 8)
            rows_to(0, R_CC, c_ctx.rearrange("(r n) -> r n", n=P), 8)
            rows_to(0, R_BADA, b_ada.rearrange("(r n) -> r n", n=P), 48)
            rows_to(0, R_N1, norm1_g.rearrange("(r n) -> r n", n=P), DT)
            rows_to(0, R_N2, norm2_g.rearrange("(r n) -> r n", n=P), DT)
            rows_to(0, R_FG, final_g.rearrange("(r n) -> r n", n=P), DT)
            rows_to(0, R_QG, q_norm_g.rearrange("(r n) -> r n", n=P), QT)
            rows_to(0, R_KVG, kv_norm_g.rearrange("(r n) -> r n", n=P), KVT)
            rows_to(0, R_CB, conv_b.rearrange("(r n) -> r n", n=P), CT)
            rows_to(0, R_CW, conv_w.rearrange("k (r n) -> (k r) n", n=P), 3 * CT)
            fw = ffn_conv_w.rearrange("k (r n) -> (k r) n", n=P)
            rows_to(1, 0, fw[0:P, :], P)
            rows_to(2, 0, fw[P:6 * FT, :], 6 * FT - P)
            rows_to(2, 6 * FT - P, ffn_conv_b.rearrange("(r n) -> r n", n=P), 2 * FT)
            for t in range(TT):
                act.dma_start(xt[:, t, :], x[t * P:(t + 1) * P, :]).then_inc(s(f"x_loaded{t}"), 16)
            for t in range(CTT):
                act.dma_start(xt[:, TT + t, :], ctx[t * P:(t + 1) * P, :]).then_inc(s(f"x_loaded{TT + t}"), 16)
            act.dma_start(tab[64:P, :], rope_tab).then_inc(s("tab_loaded"), 16)

            act.wait_ge(s("prm"), 2)
            nc.scalar.activation(cvec[:].rearrange("p k s -> p s k"), prm[:, 0:2 * DT].rearrange("p (s k) -> p s k", k=DT),
                                 ACT.Silu).then_inc(s("cvec"), 1)
            act.wait_ge(s("consts"), 4)
            for t in range(KT):
                act.wait_ge(s(f"x_loaded{t}"), 16)
                wait(act, s("x_ssq"), t)
                nc.scalar.activation(ht[:].rearrange("p a n -> p (a n)")[:, 0:D], xt[:, t, :], ACT.Square,
                                     accum_out=small[:, t:t + 1]).then_inc(s("x_ssq"), 1)
                act.wait_ge(s("x_ssq"), t + 1)
                nc.scalar.activation(small[:, 8 + t:9 + t], small[:, t:t + 1], ACT.Sqrt, bias=eps[:, 0:1],
                                     scale=1.0 / D).then_inc(s("x_rms"), 1)
                if t >= 1:
                    act.wait_ge(s("xT_ps"), t)
                    nc.scalar.activation(xnT[:, 4:8, (t - 1) * P:t * P], ps[:, 5 + 2 * ((t - 1) % 2), :]
                                         .rearrange("p (k n) -> p k n", n=P), ACT.Copy).then_inc(s("xT_act"), 1)
            t = KT
            act.wait_ge(s("xT_ps"), t)
            nc.scalar.activation(xnT[:, 4:8, (t - 1) * P:t * P], ps[:, 5 + 2 * ((t - 1) % 2), :]
                                 .rearrange("p (k n) -> p k n", n=P), ACT.Copy).then_inc(s("xT_act"), 1)
            act.wait_ge(s("ada1_used"), DT)
            nc.scalar.activation(rows1[:, 0:D], ps[0:2, 0:2, :].rearrange("p b n -> p (b n)"), ACT.Copy).then_inc(s("rows1_act"), 1)
            act.wait_ge(s("mods1"), 6)
            for k in range(DT):
                for hi, lo, to, g, m in ((T, 0, hhi, 0, mod), (K, T, chi, 1, modc)):
                    nc.scalar.activation(to[:, k, :], xnT[:, k, lo:hi], ACT.Identity, bias=m[:, k:k + 1],
                                         scale=gain[:, g, k:k + 1]).then_inc(s("h_hi"), 1)
                if k in (4, 6):
                    split_hi(act, (k - 4) // 2, (k - 4) // 2)
            split_hi(act, 2, 2)
            split_hi(act, 3, 3)

            for m in range(KVT):
                used(act, U_KV + m)
                nc.scalar.activation(ckraw[:, m, :], wide(2 * m), ACT.Copy).then_inc(s("p_raw"), 1)
                nc.scalar.activation(sqk[m], wide(2 * m), ACT.Square).then_inc(s("p_sq"), 1)
                split_hi(act, 4 + m, m)
            for m in range(QT):
                if m == 1:
                    act.wait_ge(s("kstat_ps"), 1)
                    nc.scalar.activation(sqk[1], wide(2), ACT.Sqrt, bias=eps[:, 0:1], scale=1.0 / KVR).then_inc(s("k_rms"), 1)
                    for mm in range(KVT):
                        act.wait_ge(s("ck_t"), mm + 1)
                        nc.scalar.activation(ckhi[:, mm, :], ckraw[:, mm, :], ACT.Copy).then_inc(s("ck_hi"), 1)
                used(act, U_Q + m)
                if m == 0:
                    act.wait_ge(s("kr"), 8)
                bank = (6, 7, 0)[m]
                nc.scalar.activation(cqraw[:, m, :], ps[:, bank, :], ACT.Copy).then_inc(s("p_raw"), 1)
                if m >= 1:
                    act.wait_ge(s("q_sum"), m)
                nc.scalar.activation(work[:, 3 + m % 2, :], ps[:, bank, :], ACT.Square).then_inc(s("p_sq"), 1)
                split_hi(act, 6 + m, (6 + m) % SLOTS)
            for kt in range(KT):
                if kt == 4:
                    act.wait_ge(s("qstat_ps"), 1)
                    nc.scalar.activation(work[:, 4, :], ps[:, 1, :], ACT.Sqrt, bias=eps[:, 0:1], scale=1.0 / QR).then_inc(s("q_rms"), 1)
                if kt < KT - 1:
                    act.wait_ge(s("v_ps"), kt + 1)
                else:
                    used(act, U_V)
                nc.scalar.activation(vs[:, kt, :, 0:VDIM], ps[:, 4 + kt % 4, :].rearrange("p (h n) -> p h n", n=VDIM),
                                     ACT.Copy).then_inc(s("v_hi"), 1)
            for m in range(QT):
                act.wait_ge(s("cq_t"), m + 1)
                nc.scalar.activation(cqhi[:, m, :], cqraw[:, m, :], ACT.Copy).then_inc(s("cq_hi"), 1)
            for h in range(HEADS):
                query_ready(act, h)
                if h == 0:
                    act.wait_ge(s("cq_lo"), QT)
                wait(act, s("q_lo"), h - 1)
                nc.scalar.activation(work[0:NOPE, h % 2, :], ps[0:NOPE, h % 4, :], ACT.Copy).then_inc(s("q_nope"), 1)
                act.wait_ge(s("q_rope"), 3 * h + 3)
                act.wait_ge(s("q_nope"), h + 1)
                nc.scalar.activation(qhi[0:QK, h, :], work[0:QK, h % 2, :], ACT.Copy).then_inc(s("q_hi"), 1)
                if h % 2 == 0 and 9 + h // 2 < U_CONV:
                    split_hi(act, 9 + h // 2, (9 + h // 2) % SLOTS)

            def keys_hi(pair, part):
                lo, hi = ((0, T), (T, K))[part]
                keys_ready(act, pair, part)
                wait(act, s("s_ps"), 8 * pair)
                for b in range(2):
                    nc.scalar.activation(khi[0:NOPE, b, lo:hi], ps[b * NOPE:(b + 1) * NOPE, 6, 0:hi - lo],
                                         ACT.Copy).then_inc(s("k_hi"), 1)

            keys_hi(0, 0)
            keys_hi(0, 1)

            def exps(g):
                act.wait_ge(s("nmax"), g + 1)
                wait(act, s("t_ps"), g - 1)
                nc.scalar.activation(prob[:, g % 2, :], wide(2 * (g % 2)), ACT.Exp, bias=small[:, 16 + g % 2:17 + g % 2],
                                     scale=SCALE, accum_out=small[:, 18 + g % 2:19 + g % 2]).then_inc(s("p_exp"), 1)

            exps(0)
            exps(1)
            for g in range(HEADS * TT):
                h, t = g // TT, g % TT
                act.wait_ge(s("t_ps"), g + 1)
                wait(act, s("pv_ps"), h)
                nc.scalar.activation(pthi[:, :, t * P:(t + 1) * P], wide(4).rearrange("p (k n) -> p k n", n=P),
                                     ACT.Copy).then_inc(s("pt_hi"), 1)
                if g + 2 < HEADS * TT:
                    exps(g + 2)
                if h % 2 == 1 and t == 1 and h < HEADS - 1:
                    keys_hi((h + 1) // 2, 0)
                    keys_hi((h + 1) // 2, 1)
                if g in CONV_SPLITS:
                    n = CONV_SPLITS.index(g)
                    split_hi(act, U_CONV + n, n)
                if t == TT - 1:
                    act.wait_ge(s("pv_ps"), h + 1)
                    wait(act, s("o_sum"), h)
                    nc.scalar.activation(work[0:VDIM, 0, :] if h % 2 == 0 else work[VDIM:P, 0, :], ps[VDIM:P, 7, :], ACT.Copy).then_inc(s("o_part"), 1)
                    act.wait_ge(s("o_sum"), h + 1)
                    r = slice((h % 2) * VDIM, (h % 2 + 1) * VDIM)
                    nc.scalar.activation(qhi[r, h // 2 * 2, :], work[r, 1, :], ACT.Copy).then_inc(s("o_hi"), 1)

            for j in range(CT):
                cx, y = work[:, 3 * (j % 2), :], work[:, 3 * (j % 2) + 2, :]
                used(act, U_CONV + 3 * j)
                wait(act, s("z_lo"), j - 1)
                if j == 0:
                    act.wait_ge(s("o_lo"), HEADS)
                nc.scalar.activation(cx, ps[:, 3 * (j % 2), :], ACT.Copy).then_inc(s("c_x"), 1)
                split_hi(act, U_CONV + 3 * j + 4, (3 * j + 4) % SLOTS)
                act.wait_ge(s("c_prod"), j + 1)
                nc.scalar.activation(y, work[:, 3 * (j % 2) + 1, :], ACT.Identity, bias=prm[:, R_CB + j:R_CB + j + 1],
                                     scale=prm[:, R_CW + CT + j:R_CW + CT + j + 1]).then_inc(s("c_mid"), 1)
                split_hi(act, U_CONV + 3 * j + 5, (3 * j + 5) % SLOTS)
                act.wait_ge(s("c_z"), j + 1)
                nc.scalar.activation(zhi[:, j, :], work[:, 3 * (j % 2), :], ACT.Copy).then_inc(s("z_hi"), 1)
                split_hi(act, U_CONV + 3 * j + 6, (3 * j + 6) % SLOTS)

            def merge_hi(i, first):
                for dd in range(4):
                    d = 4 * i + dd
                    b = 4 * (dd % 2)
                    for n in range(3):
                        m = 3 * dd + n
                        if n < 2:
                            used(act, U_MERGE + 3 * d + n)
                            if first and dd == 0:
                                act.wait_ge(s("z_lo"), CT)
                            if not (first and dd < 2):
                                act.wait_ge(s("m_lo"), d - 1)
                            nc.scalar.activation(work[:, 3 * (dd % 2) + n, :], ps[:, b + n, :], ACT.Sigmoid).then_inc(s("g_sig"), 1)
                        else:
                            act.wait_ge(s("m_sum"), d + 1)
                            nc.scalar.activation(at1(mhi, d), work[:, 3 * (dd % 2) + 2, :], ACT.Copy).then_inc(s("m_hi"), 1)
                        split_hi(act, U_MERGE + 12 * i + m + 4, m % SLOTS)

            merge_hi(0, True)
            with act.Fori(1, 2) as i:
                merge_hi(i, False)

            act.wait_ge(s("rows2_ps"), 4)
            nc.scalar.activation(rows2[:, 0:2 * D], ps[0:1, 0:4, :].rearrange("p b n -> p (b n)"), ACT.Copy).then_inc(s("rows2_act"), 1)
            for d in range(DT):
                act.wait_ge(s("xT2_ps"), d + 1)
                act.wait_ge(s("rows2_ps"), 8)
                nc.scalar.activation(x2T[:, d, :], ps[:, 4 + d % 4, :], ACT.Copy).then_inc(s("x2_in"), 1)
                act.wait_ge(s("x2_sum"), d + 1)
                wait(act, s("x2_ssq"), d - 1)
                nc.scalar.activation(work[:, d % 2, :], x2T[:, d, :], ACT.Square).then_inc(s("x2_sq"), 1)
                if d < 4:
                    split_hi(act, U_O + 4 + d, d)
                else:
                    split_hi(act, U_UP + d - 4, d - 4)
            act.wait_ge(s("x2stat_ps"), 1)
            nc.scalar.activation(work[:, 3, :], ps[:, 4, :], ACT.Sqrt, bias=eps[:, 0:1], scale=1.0 / D).then_inc(s("x2_rms"), 1)
            for k in range(DT):
                act.wait_ge(s("h2_t"), k + 1)
                nc.scalar.activation(hhi[:, k, :], work[:, k % 2, :], ACT.Identity,
                                     bias=mod[:, 3 * DT + k:3 * DT + k + 1]).then_inc(s("h2_hi"), 1)

            def up(i, first):
                for jj in range(2):
                    j = 2 * i + jj
                    for n in range(2):
                        used(act, U_UP + 2 * j + n)
                        if first and jj == 0:
                            act.wait_ge(s("h2_lo"), DT)
                        if not (first and jj < 2):
                            act.wait_ge(s("f_prod"), j - 1)
                        nc.scalar.activation(work[:, 3 * jj + n, :], ps[:, 2 * jj + n, :], ACT.Identity,
                                             bias=col(prm, R_FB + n * FT + j),
                                             scale=col(prm, R_FW + 2 * FT + n * FT + j)).then_inc(s("up_mid"), 1)
                        split_hi(act, U_UP + 4 * i + 2 * jj + n + 4, 2 * jj + n)
                    act.wait_ge(s("up_gate"), 2 * j + 2)
                    nc.scalar.activation(work[:, 3 * jj, :], work[:, 3 * jj, :], ACT.Silu).then_inc(s("up_silu"), 1)
                    act.wait_ge(s("f_prod"), j + 1)
                    nc.scalar.activation(at1(fhi, j), work[:, 3 * jj + 2, :], ACT.Copy).then_inc(s("f_hi"), 1)

            up(0, True)
            with act.Fori(1, FT // 2) as i:
                up(i, False)
            with act.Fori(0, (FT - 4) // 4) as i:
                for n in range(4):
                    split_hi(act, U_DOWN + 4 + 4 * i + n, n)
            for k in range(4 + (FT - 4) // 4 * 4, FT):
                split_hi(act, U_DOWN + k, k % 4)
            for d in range(DT):
                act.wait_ge(s("x3_sum"), d + 1)
                wait(act, s("x3_ssq"), d - 1)
                nc.scalar.activation(work[:, d % 2, :], x2T[:, d, :], ACT.Square).then_inc(s("x3_sq"), 1)
            act.wait_ge(s("x3stat_ps"), 1)
            nc.scalar.activation(work[:, 3, :], ps[:, 0, :], ACT.Sqrt, bias=eps[:, 0:1], scale=1.0 / D).then_inc(s("x3_rms"), 1)
            for t in range(TT):
                act.wait_ge(s("y_ps"), t + 1)
                nc.scalar.activation(yo[:, t, 0:512], ps[:, 2 * (t % 4), :], ACT.Copy).then_inc(s("y_tok_act"), 1)

        @block.vector
        def _(dve):
            dve.wait_ge(s("prm_ps"), 1)
            nc.vector.tensor_copy(prm[:, 0:R_END0], ps[:, 7, 0:R_END0]).then_inc(s("prm"), 1)
            nc.vector.tensor_copy(prm[:, R_FW:R_END], ps[:, 7, R_FW:R_END]).then_inc(s("prm"), 1)
            for t in range(KT):
                dve.wait_ge(s("x_rms"), t + 1)
                nc.vector.reciprocal(small[:, 24 + t:25 + t], small[:, 8 + t:9 + t]).then_inc(s("x_rinv"), 1)
                dve.wait_ge(s("x_rinv"), t + 1)
                nc.vector.tensor_scalar(xt[:, t, :], xt[:, t, :], small[:, 24 + t:25 + t], None, ALU.mult).then_inc(s("x_norm"), 1)
                if t >= 1:
                    dve.wait_ge(s("xT_ps"), t)
                    nc.vector.tensor_copy(xnT[:, 0:4, (t - 1) * P:t * P], ps[:, 4 + 2 * ((t - 1) % 2), :]
                                          .rearrange("p (k n) -> p k n", n=P)).then_inc(s("xT_dve"), 1)
            t = KT
            dve.wait_ge(s("xT_ps"), t)
            nc.vector.tensor_copy(xnT[:, 0:4, (t - 1) * P:t * P], ps[:, 4 + 2 * ((t - 1) % 2), :]
                                  .rearrange("p (k n) -> p k n", n=P)).then_inc(s("xT_dve"), 1)
            dve.wait_ge(s("ada1_used"), DT)
            nc.vector.tensor_copy(rows1[:, D:2 * D], ps[0:2, 2:4, :].rearrange("p b n -> p (b n)")).then_inc(s("rows1_dve"), 1)
            dve.wait_ge(s("cols1_ps"), 1)
            cols = ps[:, 4, 0:4 * DT].rearrange("p (m s) -> p s m", s=2)
            nc.vector.tensor_tensor(out=mod[:, 0:2 * DT], in0=cols[:, 0, :], in1=prm[:, R_BADA:R_BADA + 2 * DT], op=ALU.add).then_inc(s("mods1"), 1)
            nc.vector.tensor_tensor(out=modc[:], in0=cols[:, 1, :], in1=prm[:, R_BADA:R_BADA + 2 * DT], op=ALU.add).then_inc(s("mods1"), 1)
            dve.wait_ge(s("mods1"), 2)
            for g, m in ((0, mod), (1, modc)):
                nc.vector.scalar_tensor_tensor(out=gain[:, g, :], in0=m[:, DT:2 * DT], scalar=1.0, in1=prm[:, R_N1:R_N1 + DT],
                                               op0=ALU.add, op1=ALU.mult).then_inc(s("mods1"), 2)
            for k in range(DT):
                for n, (lo, hi, dst, src) in enumerate(((0, T, hlo, hhi), (T, K, clo, chi))):
                    dve.wait_ge(s("h_t"), 2 * k + n + 1)
                    dve.wait_ge(s("h_hi"), 2 * k + n + 1)
                    nc.vector.tensor_tensor(out=dst[:, k, :], in0=ht[:, k % 2, lo:hi], in1=src[:, k, :].bitcast(F32),
                                            op=ALU.subtract).then_inc(s("h_lo"), 1)
            dve.wait_ge(s("p_sq"), 2)
            nc.vector.tensor_tensor(out=sqk[0], in0=sqk[0], in1=sqk[1], op=ALU.add).then_inc(s("k_ssq"), 1)
            used(dve, U_KR)
            dve.wait_ge(s("tab_loaded"), 16)
            kr = work[NOPE:QK, 3:5, :].rearrange("p a n -> p (a n)")
            tmp = work[NOPE:QK, 5, :]
            nc.vector.tensor_tensor(out=kr[:, 0:T], in0=ps[NOPE:QK, 4, :], in1=tab[NOPE:QK, :], op=ALU.mult).then_inc(s("kr"), 1)
            nc.vector.tensor_tensor(out=tmp, in0=ps[QK:P, 4, :], in1=tab[QK:P, :], op=ALU.mult).then_inc(s("kr"), 1)
            nc.vector.tensor_copy(kr[:, T:K], ps[NOPE:QK, 5, 0:C]).then_inc(s("kr"), 1)
            dve.wait_ge(s("kr"), 3)
            nc.vector.tensor_tensor(out=kr[:, 0:T], in0=kr[:, 0:T], in1=tmp, op=ALU.add).then_inc(s("kr"), 1)
            dve.wait_ge(s("kr"), 4)
            for b in range(2):
                nc.vector.tensor_copy(khi[NOPE:QK, b, :], kr[:, 0:K]).then_inc(s("kr"), 1)
            dve.wait_ge(s("kr"), 6)
            for b in range(2):
                nc.vector.tensor_tensor(out=klo[NOPE:QK, b, :], in0=kr[:, 0:K], in1=khi[NOPE:QK, b, :].bitcast(F32),
                                        op=ALU.subtract).then_inc(s("kr"), 1)
            dve.wait_ge(s("k_rms"), 1)
            nc.vector.reciprocal(sqk[0], sqk[1]).then_inc(s("k_rinv"), 1)
            dve.wait_ge(s("k_rinv"), 1)
            for m in range(KVT):
                nc.vector.scalar_tensor_tensor(out=ckraw[:, m, :], in0=ckraw[:, m, :], scalar=prm[:, R_KVG + m:R_KVG + m + 1],
                                               in1=sqk[0], op0=ALU.mult, op1=ALU.mult).then_inc(s("ck_t"), 1)
            for m in range(KVT):
                dve.wait_ge(s("ck_hi"), m + 1)
                nc.vector.tensor_tensor(out=cklo[:, m, :], in0=ckraw[:, m, :], in1=ckhi[:, m, :].bitcast(F32),
                                        op=ALU.subtract).then_inc(s("ck_lo"), 1)
            dve.wait_ge(s("p_sq"), KVT + 1)
            nc.vector.tensor_copy(work[:, 5, :], work[:, 3, :]).then_inc(s("q_sum"), 1)
            for m in range(1, QT):
                dve.wait_ge(s("p_sq"), KVT + 1 + m)
                dve.wait_ge(s("q_sum"), m)
                nc.vector.tensor_tensor(out=work[:, 5, :], in0=work[:, 5, :], in1=work[:, 3 + m % 2, :], op=ALU.add).then_inc(s("q_sum"), 1)
            def value_lo(kt):
                dve.wait_ge(s("v_hi"), kt + 1)
                nc.vector.tensor_tensor(out=vs[:, kt, :, VDIM:], in0=ps[:, 4 + kt % 4, :].rearrange("p (h n) -> p h n", n=VDIM),
                                        in1=vs[:, kt, :, 0:VDIM].bitcast(F32), op=ALU.subtract).then_inc(s("v_lo"), 1)

            for kt in range(4):
                value_lo(kt)
            dve.wait_ge(s("q_rms"), 1)
            nc.vector.reciprocal(work[:, 3, :], work[:, 4, :]).then_inc(s("q_rinv"), 1)
            dve.wait_ge(s("q_rinv"), 1)
            for m in range(QT):
                nc.vector.scalar_tensor_tensor(out=cqraw[:, m, :], in0=cqraw[:, m, :], scalar=prm[:, R_QG + m:R_QG + m + 1],
                                               in1=work[:, 3, :], op0=ALU.mult, op1=ALU.mult).then_inc(s("cq_t"), 1)
            for kt in range(4, KT):
                value_lo(kt)
            for m in range(QT):
                dve.wait_ge(s("cq_hi"), m + 1)
                nc.vector.tensor_tensor(out=cqlo[:, m, :], in0=cqraw[:, m, :], in1=cqhi[:, m, :].bitcast(F32),
                                        op=ALU.subtract).then_inc(s("cq_lo"), 1)
            for h in range(HEADS):
                qv, r1, r2 = work[:, h % 2, :], work[NOPE:QK, 2 + 2 * (h % 2), :], work[NOPE:QK, 3 + 2 * (h % 2), :]
                query_ready(dve, h)
                wait(dve, s("q_rope"), 3 * h)
                if h == 0:
                    dve.wait_ge(s("cq_lo"), QT)
                nc.vector.tensor_tensor(out=r1, in0=ps[NOPE:QK, h % 4, :], in1=tab[NOPE:QK, :], op=ALU.mult).then_inc(s("q_rope"), 1)
                nc.vector.tensor_tensor(out=r2, in0=ps[QK:P, h % 4, :], in1=tab[QK:P, :], op=ALU.mult).then_inc(s("q_rope"), 1)
                dve.wait_ge(s("q_rope"), 3 * h + 2)
                wait(dve, s("q_lo"), h - 1)
                nc.vector.tensor_tensor(out=qv[NOPE:QK, :], in0=r1, in1=r2, op=ALU.add).then_inc(s("q_rope"), 1)
                dve.wait_ge(s("q_hi"), h + 1)
                nc.vector.tensor_tensor(out=qlo[0:QK, h, :], in0=qv[0:QK, :], in1=qhi[0:QK, h, :].bitcast(F32),
                                        op=ALU.subtract).then_inc(s("q_lo"), 1)

            def keys_lo(pair, part):
                lo, hi = ((0, T), (T, K))[part]
                for b in range(2):
                    dve.wait_ge(s("k_hi"), 4 * pair + 2 * part + b + 1)
                    nc.vector.tensor_tensor(out=klo[0:NOPE, b, lo:hi], in0=ps[b * NOPE:(b + 1) * NOPE, 6, 0:hi - lo],
                                            in1=khi[0:NOPE, b, lo:hi].bitcast(F32), op=ALU.subtract).then_inc(s("k_lo"), 1)

            keys_lo(0, 0)
            keys_lo(0, 1)

            def maxima(g):
                dve.wait_ge(s("s_ps"), g + 1)
                wait(dve, s("nmax"), g)
                nc.vector.reduce_max(small[:, 22:23], wide(2 * (g % 2)), AX.X).then_inc(s("smax"), 1)
                dve.wait_ge(s("smax"), g + 1)
                wait(dve, s("p_exp"), g - 1)
                nc.vector.tensor_scalar(small[:, 16 + g % 2:17 + g % 2], small[:, 22:23], -SCALE, None, ALU.mult).then_inc(s("nmax"), 1)

            def inverse(g):
                dve.wait_ge(s("p_exp"), g + 1)
                wait(dve, s("p_norm"), g - 1)
                nc.vector.reciprocal(small[:, 20 + g % 2:21 + g % 2], small[:, 18 + g % 2:19 + g % 2]).then_inc(s("rsum"), 1)

            maxima(0)
            maxima(1)
            inverse(0)
            for g in range(HEADS * TT):
                h, t = g // TT, g % TT
                if g + 1 < HEADS * TT:
                    inverse(g + 1)
                dve.wait_ge(s("pt_hi"), g + 1)
                nc.vector.tensor_tensor(out=ptlo[:, :, t * P:(t + 1) * P], in0=wide(4).rearrange("p (k n) -> p k n", n=P),
                                        in1=pthi[:, :, t * P:(t + 1) * P].bitcast(F32), op=ALU.subtract).then_inc(s("pt_lo"), 1)
                if g + 2 < HEADS * TT:
                    maxima(g + 2)
                if h % 2 == 1 and t == 1 and h < HEADS - 1:
                    keys_lo((h + 1) // 2, 0)
                    keys_lo((h + 1) // 2, 1)
                if t == TT - 1:
                    r = slice((h % 2) * VDIM, (h % 2 + 1) * VDIM)
                    dve.wait_ge(s("o_part"), h + 1)
                    wait(dve, s("o_lo"), h)
                    nc.vector.tensor_tensor(out=work[r, 1, :], in0=ps[0:VDIM, 7, :], in1=work[r, 0, :], op=ALU.add).then_inc(s("o_sum"), 1)
                    dve.wait_ge(s("o_hi"), h + 1)
                    nc.vector.tensor_tensor(out=qlo[r, h // 2 * 2, :], in0=work[r, 1, :], in1=qhi[r, h // 2 * 2, :].bitcast(F32),
                                            op=ALU.subtract).then_inc(s("o_lo"), 1)

            def ada2_add(n, k, g):
                gg = g * D
                if isinstance(n, int):
                    dve.wait_ge(s(f"ada2_loaded{g % 2}"), 16 * (n // 2 + 1))
                else:
                    dve.wait_ge(s(f"ada2_loaded{g % 2}"), (n - g % 2) * 8 + 16)
                cv = cvec[:, k, 0:1] if isinstance(k, int) else cvec[:, bass.ds(k, 1), 0:1].rearrange("p a b -> p (a b)")
                if isinstance(k, int) and k == 0:
                    nc.vector.tensor_scalar(adacc[:, gg:gg + D], ada2[:, g % 2, :], cv, None, ALU.mult).then_inc(s("ada2_used"), 1)
                else:
                    dve.wait_ge(s("ada2_used"), n - 3)
                    nc.vector.scalar_tensor_tensor(out=adacc[:, gg:gg + D], in0=ada2[:, g % 2, :], scalar=cv,
                                                   in1=adacc[:, gg:gg + D], op0=ALU.mult, op1=ALU.add).then_inc(s("ada2_used"), 1)

            for j in range(CT):
                b = 3 * (j % 2)
                cx, prod, y = (work[:, b + n, :] for n in range(3))
                used(dve, U_CONV + 3 * j + 1)
                dve.wait_ge(s("c_x"), j + 1)
                nc.vector.tensor_tensor(out=prod, in0=ps[:, b + 1, :], in1=cx, op=ALU.mult).then_inc(s("c_prod"), 1)
                dve.wait_ge(s("c_mid"), j + 1)
                nc.vector.scalar_tensor_tensor(out=y[:, 1:T], in0=prod[:, 0:T - 1], scalar=prm[:, R_CW + j:R_CW + j + 1],
                                               in1=y[:, 1:T], op0=ALU.mult, op1=ALU.add).then_inc(s("c_tap"), 1)
                dve.wait_ge(s("c_tap"), 2 * j + 1)
                nc.vector.scalar_tensor_tensor(out=y[:, 0:T - 1], in0=prod[:, 1:T], scalar=prm[:, R_CW + 2 * CT + j:R_CW + 2 * CT + j + 1],
                                               in1=y[:, 0:T - 1], op0=ALU.mult, op1=ALU.add).then_inc(s("c_tap"), 1)
                dve.wait_ge(s("c_tap"), 2 * j + 2)
                used(dve, U_CONV + 3 * j + 2)
                nc.vector.tensor_tensor(out=cx, in0=ps[:, b + 2, :], in1=y, op=ALU.mult).then_inc(s("c_z"), 1)
                dve.wait_ge(s("z_hi"), j + 1)
                nc.vector.tensor_tensor(out=zlo[:, j, :], in0=cx, in1=zhi[:, j, :].bitcast(F32), op=ALU.subtract).then_inc(s("z_lo"), 1)
                if j in (1, 3):
                    for m in range(4):
                        ada2_add(4 * (j // 2) + m, j // 2, m)

            def merge_lo(i, first):
                for dd in range(4):
                    d = 4 * i + dd
                    b, w = 4 * (dd % 2), 3 * (dd % 2)
                    for n in range(2):
                        used(dve, U_MERGE + 3 * d + 2)
                        dve.wait_ge(s("g_sig"), 2 * d + n + 1)
                        nc.vector.tensor_tensor(out=work[:, w + n, :], in0=ps[:, b + 2 + n, :], in1=work[:, w + n, :],
                                                op=ALU.mult).then_inc(s("m_prod"), 1)
                    dve.wait_ge(s("m_prod"), 2 * d + 2)
                    if not (first and dd < 2):
                        dve.wait_ge(s("m_lo"), d - 1)
                    nc.vector.tensor_tensor(out=work[:, w + 2, :], in0=work[:, w, :], in1=work[:, w + 1, :],
                                            op=ALU.add).then_inc(s("m_sum"), 1)
                    for m in range(3):
                        nn = 3 * dd + m
                        ada2_add(8 + 12 * i + nn, 2 + 3 * i + nn // 4, nn % 4)
                    dve.wait_ge(s("m_hi"), d + 1)
                    nc.vector.tensor_tensor(out=at1(mlo, d), in0=work[:, w + 2, :], in1=at1(mhi, d).bitcast(F32),
                                            op=ALU.subtract).then_inc(s("m_lo"), 1)

            merge_lo(0, True)
            with dve.Fori(1, 2) as i:
                merge_lo(i, False)

            dve.wait_ge(s("rows2_ps"), 8)
            nc.vector.tensor_copy(rows2[:, 2 * D:4 * D], ps[0:1, 4:8, :].rearrange("p b n -> p (b n)")).then_inc(s("rows2_dve"), 1)
            dve.wait_ge(s("cols2_ps"), 1)
            nc.vector.tensor_tensor(out=mod[:, 2 * DT:6 * DT], in0=ps[:, 0, 0:4 * DT], in1=prm[:, R_BADA + 2 * DT:R_BADA + 6 * DT],
                                    op=ALU.add).then_inc(s("mods2"), 4)
            dve.wait_ge(s("mods2"), 4)
            nc.vector.scalar_tensor_tensor(out=gain[:, 2, :], in0=mod[:, 4 * DT:5 * DT], scalar=1.0, in1=prm[:, R_N2:R_N2 + DT],
                                           op0=ALU.add, op1=ALU.mult).then_inc(s("mods2"), 1)
            for d in range(DT):
                used(dve, U_O + d)
                dve.wait_ge(s("x2_in"), d + 1)
                nc.vector.scalar_tensor_tensor(out=x2T[:, d, :], in0=ps[:, d % 4, :], scalar=mod[:, 2 * DT + d:2 * DT + d + 1],
                                               in1=x2T[:, d, :], op0=ALU.mult, op1=ALU.add).then_inc(s("x2_sum"), 1)
                dve.wait_ge(s("x2_sq"), d + 1)
                if d == 0:
                    nc.vector.tensor_copy(work[:, 2, :], work[:, 0, :]).then_inc(s("x2_ssq"), 1)
                else:
                    dve.wait_ge(s("x2_ssq"), d)
                    nc.vector.tensor_tensor(out=work[:, 2, :], in0=work[:, 2, :], in1=work[:, d % 2, :], op=ALU.add).then_inc(s("x2_ssq"), 1)
            dve.wait_ge(s("x2_rms"), 1)
            nc.vector.reciprocal(work[:, 4, :], work[:, 3, :]).then_inc(s("x2_rinv"), 1)
            dve.wait_ge(s("x2_rinv"), 1)
            def h2_t(k):
                wait(dve, s("h2_lo"), k - 1)
                nc.vector.scalar_tensor_tensor(out=work[:, k % 2, :], in0=x2T[:, k, :], scalar=gain[:, 2, k:k + 1],
                                               in1=work[:, 4, :], op0=ALU.mult, op1=ALU.mult).then_inc(s("h2_t"), 1)

            h2_t(0)
            for k in range(DT):
                if k + 1 < DT:
                    h2_t(k + 1)
                dve.wait_ge(s("h2_hi"), k + 1)
                nc.vector.scalar_tensor_tensor(out=hlo[:, k, :], in0=work[:, k % 2, :], scalar=mod[:, 3 * DT + k:3 * DT + k + 1],
                                               in1=hhi[:, k, :].bitcast(F32), op0=ALU.add, op1=ALU.subtract).then_inc(s("h2_lo"), 1)

            def up(i, first):
                for jj in range(2):
                    j = 2 * i + jj
                    for n in range(2):
                        u, p = work[:, 3 * jj + n, :], ps[:, 2 * jj + n, :]
                        dve.wait_ge(s("up_mid"), 2 * j + n + 1)
                        nc.vector.scalar_tensor_tensor(out=u[:, 1:T], in0=p[:, 0:T - 1], scalar=col(prm, R_FW + n * FT + j),
                                                       in1=u[:, 1:T], op0=ALU.mult, op1=ALU.add).then_inc(s("up_gate" if n == 0 else "up_val"), 1)
                        dve.wait_ge(s("up_gate" if n == 0 else "up_val"), 2 * j + 1)
                        nc.vector.scalar_tensor_tensor(out=u[:, 0:T - 1], in0=p[:, 1:T], scalar=col(prm, R_FW + 4 * FT + n * FT + j),
                                                       in1=u[:, 0:T - 1], op0=ALU.mult, op1=ALU.add).then_inc(s("up_gate" if n == 0 else "up_val"), 1)
                    dve.wait_ge(s("up_val"), 2 * j + 2)
                    dve.wait_ge(s("up_silu"), j + 1)
                    if not (first and jj < 2):
                        dve.wait_ge(s("f_lo"), j - 1)
                    nc.vector.tensor_tensor(out=work[:, 3 * jj + 2, :], in0=work[:, 3 * jj, :], in1=work[:, 3 * jj + 1, :],
                                            op=ALU.mult).then_inc(s("f_prod"), 1)
                    dve.wait_ge(s("f_hi"), j + 1)
                    nc.vector.tensor_tensor(out=at1(flo, j), in0=work[:, 3 * jj + 2, :], in1=at1(fhi, j).bitcast(F32),
                                            op=ALU.subtract).then_inc(s("f_lo"), 1)

            up(0, True)
            with dve.Fori(1, FT // 2) as i:
                up(i, False)
            for d in range(DT):
                if d < DT - 1:
                    dve.wait_ge(s("d_ps"), d + 1)
                else:
                    used(dve, U_ALL - 1)
                nc.vector.scalar_tensor_tensor(out=x2T[:, d, :], in0=ps[:, d, :], scalar=mod[:, 5 * DT + d:5 * DT + d + 1],
                                               in1=x2T[:, d, :], op0=ALU.mult, op1=ALU.add).then_inc(s("x3_sum"), 1)
                if d >= 1:
                    x3_add(dve, d - 1)
            x3_add(dve, DT - 1)
            dve.wait_ge(s("x3_rms"), 1)
            nc.vector.reciprocal(work[:, 4, :], work[:, 3, :]).then_inc(s("x3_rinv"), 1)
            dve.wait_ge(s("x3_rinv"), 1)
            for d in range(DT):
                nc.vector.scalar_tensor_tensor(out=x2T[:, d, :], in0=x2T[:, d, :], scalar=prm[:, R_FG + d:R_FG + d + 1],
                                               in1=work[:, 4, :], op0=ALU.mult, op1=ALU.mult).then_inc(s("y_t"), 1)
            for t in range(TT):
                dve.wait_ge(s("y_ps"), t + 1)
                nc.vector.tensor_copy(yo[:, t, 512:D], ps[:, 2 * (t % 4) + 1, :]).then_inc(s("y_tok_dve"), 1)

        @block.tensor
        def _(pe):
            pe.wait_ge(s("consts"), 4)
            pe.wait_ge(s("prm_loaded"), 16 * 13)
            pe.transpose(ps[:, 7, 0:R_END0], G[0:R_END0, 0, :], ident[0:R_END0, 0:R_END0])
            pe.transpose(ps[:, 7, P:2 * P], G[:, 1, :], ident[:])
            n = R_END - 2 * P
            pe.transpose(ps[:, 7, 2 * P:R_END], G[0:n, 2, :], ident[0:n, 0:n]).then_inc(s("prm_ps"), 1)
            pe.wait_ge(s("cvec"), 1)
            for k in range(DT):
                if k < KT:
                    pe.wait_ge(s("x_norm"), k + 1)
                    wait(pe, s("xT_dve"), k - 1)
                    wait(pe, s("xT_act"), k - 1)
                    for m in range(DT):
                        last = pe.transpose(ps[:, 4 + 2 * (k % 2) + m // 4, (m % 4) * P:(m % 4 + 1) * P],
                                            xt[:, k, m * P:(m + 1) * P], ident[:])
                    last.then_inc(s("xT_ps"), 1)
                pe.wait_ge(s(f"ada1_loaded{k % 3}"), 16 * (k // 3 + 1))
                for b in range(4):
                    last = pe.matmul(ps[0:2, b, :], cvec[:, k, :], ada1[:, k % 3, b * 512:(b + 1) * 512],
                                     start=k == 0, stop=k == DT - 1)
                last.then_inc(s("ada1_used"), 1)
            pe.wait_ge(s("rows1_act"), 1)
            pe.wait_ge(s("rows1_dve"), 1)
            pe.wait_ge(s("xT_dve"), KT)
            for m in range(2 * DT):
                last = pe.transpose(ps[:, 4, 2 * m:2 * m + 2], rows1[:, m * P:(m + 1) * P], ident[0:2, 0:2])
            last.then_inc(s("cols1_ps"), 1)

            def unit(u):
                pe.wait_ge(w_lo, u + 1)

            pe.wait_ge(s("h_lo"), 2 * DT)
            for n, u in enumerate((U_KV, U_KV + 1, U_KR)):
                unit(u)
                project(pe, ps[:, 2 * n + 1, 0:C], u % SLOTS, chi, clo)
                project(pe, ps[:, 2 * n, :], u % SLOTS, hhi, hlo).then_inc(w_used, 1)
            for m in range(QT):
                if m == 1:
                    pe.wait_ge(s("k_ssq"), 1)
                    pe.matmul(ps[:, 3, 0:C], ones[:], sqk[0][:, T:K], start=True, stop=True)
                    pe.matmul(ps[:, 2, :], ones[:], sqk[0][:, 0:T], start=True, stop=True).then_inc(s("kstat_ps"), 1)
                unit(U_Q + m)
                if m == 2:
                    pe.wait_ge(s("p_sq"), 1)
                project(pe, ps[:, (6, 7, 0)[m], :], (U_Q + m) % SLOTS, hhi, hlo).then_inc(w_used, 1)
            unit(U_V)
            pe.wait_ge(s("ck_lo"), KVT)
            slot = U_V % SLOTS
            for kt in range(KT):
                if kt == 0:
                    pe.wait_ge(s("kr"), 8)
                wait(pe, s("v_lo"), kt - 3)
                if kt == 3:
                    pe.wait_ge(s("q_sum"), QT)
                    pe.matmul(ps[:, 1, :], ones[:], work[:, 5, :], start=True, stop=True).then_inc(s("qstat_ps"), 1)
                for k in range(KVT):
                    last = mm3(pe, ps[:, 4 + kt % 4, :], (ckhi[:, k, kt * P:(kt + 1) * P], cklo[:, k, kt * P:(kt + 1) * P]),
                               (tile_of(whi, slot, k, 512), tile_of(wlo, slot, k, 512)), k == 0, k == KVT - 1)
                last.then_inc(s("v_ps") if kt < KT - 1 else w_used, 1)
            pe.wait_ge(s("cq_lo"), QT)
            for h in range(HEADS):
                unit(U_UQ + h // 2)
                wait(pe, s("q_rope"), 3 * (h - 3))
                wait(pe, s("q_nope"), h - 3)
                slot = (U_UQ + h // 2) % SLOTS
                for k in range(QT):
                    w = tuple(t[:, slot, (2 * k + h % 2) * P:(2 * k + h % 2 + 1) * P] for t in (whi, wlo))
                    last = mm3(pe, ps[:, h % 4, :], w, (cqhi[:, k, :], cqlo[:, k, :]), k == 0, k == QT - 1)
                last.then_inc(s("q_ps") if h % 2 == 0 else w_used, 1)

            def keys(pair, part):
                lo, hi = ((0, T), (T, K))[part]
                slot = U_N % SLOTS
                wait(pe, s("k_lo"), 4 * pair + 2 * part)
                for k in range(KVT):
                    w = tuple(t[:, slot, k * 512 + pair * P:k * 512 + (pair + 1) * P] for t in (whi, wlo))
                    last = mm3(pe, ps[:, 6, 0:hi - lo], w, (ckhi[:, k, lo:hi], cklo[:, k, lo:hi]), k == 0, k == KVT - 1)
                last.then_inc(w_used if (pair, part) == (HEADS // 2 - 1, 1) else s("k_ps"), 1)

            unit(U_N)
            pe.wait_ge(s("v_lo"), KT)
            keys(0, 0)
            keys(0, 1)

            def scores(g):
                h, t = g // TT, g % TT
                wait(pe, s("p_exp"), g - 1)
                pe.wait_ge(s("q_lo"), h + 1 if g else HEADS)
                pe.wait_ge(s("k_lo"), 4 * (h // 2) + 4)
                q = tuple(x_[0:QK, h, t * P:(t + 1) * P] for x_ in (qhi, qlo))
                for bank, lo, hi in ((1, T, K), (0, 0, T)):
                    last = mm3(pe, ps[:, 2 * (g % 2) + bank, 0:hi - lo], q,
                               (khi[0:QK, h % 2, lo:hi], klo[0:QK, h % 2, lo:hi]), True, True)
                last.then_inc(s("s_ps"), 1)

            def transposes(g):
                pe.wait_ge(s("p_norm"), g + 1)
                wait(pe, s("pt_lo"), g)
                for kt in range(KT):
                    last = pe.transpose(wide(4)[:, kt * P:(kt + 1) * P], prob[:, g % 2, kt * P:(kt + 1) * P], ident[:])
                last.then_inc(s("t_ps"), 1)

            scores(0)
            scores(1)
            for g in range(HEADS * TT):
                h, t = g // TT, g % TT
                transposes(g)
                if g + 2 < HEADS * TT:
                    scores(g + 2)
                if h % 2 == 1 and t == 1 and h < HEADS - 1:
                    keys((h + 1) // 2, 0)
                    keys((h + 1) // 2, 1)
                if t == TT - 1:
                    pe.wait_ge(s("pt_lo"), g + 1)
                    wait(pe, s("o_sum"), h)
                    for kt in range(KT):
                        for n, p_ in enumerate((pthi, ptlo)):
                            last = pe.matmul(ps[:, 7, :], vs[:, kt, h, :], p_[:, kt, :], start=kt == 0 and n == 0,
                                             stop=kt == KT - 1 and n == 1)
                    last.then_inc(s("pv_ps"), 1)

            for j in range(CT):
                for n in range(3):
                    u = U_CONV + 3 * j + n
                    unit(u)
                    wait(pe, s("c_z"), j - 1)
                    project(pe, ps[:, 3 * (j % 2) + n, :], u % SLOTS, hhi, hlo).then_inc(w_used, 1)

            def merge(i, first):
                for dd in range(4):
                    d, b = 4 * i + dd, 4 * (dd % 2)
                    if first and dd == 0:
                        pe.wait_ge(s("z_lo"), CT)
                        pe.wait_ge(s("o_lo"), HEADS)
                    if not (first and dd < 2):
                        pe.wait_ge(s("m_prod"), 2 * d - 2)
                    for n in range(2):
                        m = 3 * dd + n
                        pe.wait_ge(w_lo, U_MERGE + 12 * i + m + 1)
                        project(pe, ps[:, b + n, :], m % SLOTS, hhi, hlo).then_inc(w_used, 1)
                    m = 3 * dd + 2
                    slot = m % SLOTS
                    pe.wait_ge(w_lo, U_MERGE + 12 * i + m + 1)
                    for k in range(CT):
                        mm3(pe, ps[:, b + 2, :], (tile_of(whi, slot, k), tile_of(wlo, slot, k)),
                            (qhi[:, 2 * k, :], qlo[:, 2 * k, :]), k == 0, k == CT - 1)
                    project(pe, ps[:, b + 3, :], slot, zhi, zlo, kt=CT, k0=CT).then_inc(w_used, 1)

            merge(0, True)
            with pe.Fori(1, 2) as i:
                merge(i, False)

            pe.wait_ge(s("ada2_used"), 4 * DT)
            pe.wait_ge(s("m_prod"), 2 * DT)
            for b in range(8):
                pe.matmul(ps[0:1, b, :], ones[:, 0:1], adacc[:, b * 512:(b + 1) * 512], start=True, stop=True).then_inc(s("rows2_ps"), 1)
            pe.wait_ge(s("rows2_act"), 1)
            pe.wait_ge(s("rows2_dve"), 1)
            for m in range(4 * DT):
                last = pe.transpose(ps[:, 0, m:m + 1], rows2[:, m * P:(m + 1) * P], ident[0:1, 0:1])
            last.then_inc(s("cols2_ps"), 1)

            pe.wait_ge(s("m_lo"), DT)
            for d in range(DT):
                unit(U_O + d)
                if d == 0:
                    pe.wait_ge(s("mods2"), 4)
                wait(pe, s("x2_sum"), d - 3)
                project(pe, ps[:, d % 4, :], d % SLOTS, mhi, mlo).then_inc(w_used, 1)
                if d == 0:
                    pe.wait_ge(s("xtok_loaded"), 16 * TT)
                wait(pe, s("x2_in"), d - 3)
                for t in range(TT):
                    last = pe.transpose(ps[:, 4 + d % 4, t * P:(t + 1) * P], xtok[:, t, d * P:(d + 1) * P], ident[:])
                last.then_inc(s("xT2_ps"), 1)
            pe.wait_ge(s("x2_ssq"), DT)
            pe.matmul(ps[:, 4, :], ones[:], work[:, 2, :], start=True, stop=True).then_inc(s("x2stat_ps"), 1)

            def up(i, first):
                for jj in range(2):
                    j = 2 * i + jj
                    for n in range(2):
                        m = 2 * jj + n
                        pe.wait_ge(w_lo, U_UP + 4 * i + m + 1)
                        if not (first and jj < 2):
                            pe.wait_ge(s("up_gate" if n == 0 else "up_val"), 2 * j - 2)
                        project(pe, ps[:, m, :], m, hhi, hlo).then_inc(w_used, 1)

            pe.wait_ge(s("h2_lo"), DT)
            up(0, True)
            with pe.Fori(1, FT // 2) as i:
                up(i, False)

            def down(k, slot, start=False, stop=False):
                pe.wait_ge(w_lo, U_DOWN + k + 1)
                pe.wait_ge(s("f_lo"), k + 1)
                for n, m in enumerate((4, 5, 6, 7, 0, 1, 2, 3) if not stop else range(DT)):
                    if start and n == 4:
                        pe.wait_ge(s("up_val"), 2 * FT)
                    last = mm3(pe, ps[:, m, :], (tile_of(whi, slot, m), tile_of(wlo, slot, m)),
                               (at1(fhi, k), at1(flo, k)), start, stop)
                    if stop:
                        last.then_inc(s("d_ps") if m < DT - 1 else w_used, 1)
                if not stop:
                    last.then_inc(w_used, 1)

            for k in range(4):
                down(k, k, start=k == 0)
            with pe.Fori(1, (FT - 2) // 4) as i:
                for n in range(4):
                    down(4 * i + n, n)
            for k in range((FT - 2) // 4 * 4, FT):
                down(k, k % SLOTS, stop=k == FT - 1)

            pe.wait_ge(s("x3_ssq"), DT)
            pe.matmul(ps[:, 0, :], ones[:], work[:, 2, :], start=True, stop=True).then_inc(s("x3stat_ps"), 1)
            pe.wait_ge(s("y_t"), DT)
            for t in range(TT):
                for d in range(DT):
                    last = pe.transpose(ps[:, 2 * t + d // 4, (d % 4) * P:(d % 4 + 1) * P], x2T[:, d, t * P:(t + 1) * P], ident[:])
                last.then_inc(s("y_ps"), 1)


_SHARED = ["x", "c", "ctx", "c_ctx", "w_ada", "b_ada", "norm1_g", "w_in", "q_norm_g", "kv_norm_g", "w_uq", "w_ukv",
           "conv_w", "conv_b", "w_attn_out", "w_conv_out", "w_o", "norm2_g", "w_up", "ffn_conv_w", "ffn_conv_b",
           "w_down", "final_g"]


def rope_table():
    t = np.arange(T)
    axis = ROPE // 2
    inv = np.float32(THETA) ** (-np.arange(0, axis, 2, dtype=np.float32) / np.float32(axis))
    table = np.zeros((2, 2, 2, axis // 2, T), np.float32)
    for a, at in enumerate((t // GRID_W, t % GRID_W)):
        ang = (inv[:, None] * at[None, :].astype(np.float32)).astype(np.float32)
        table[0, a] = np.cos(ang)
        table[1, a, 0] = -np.sin(ang)
        table[1, a, 1] = np.sin(ang)
    return table.reshape(2 * ROPE, T)


def kernel(**inputs):
    import concourse.bacc as bacc
    from concourse.bass_utils import run_bass_kernel_spmd

    nc = bacc.Bacc("TRN2", target_bir_lowering=False, num_devices=1)
    arrays, args = {}, []
    for name in _SHARED:
        a = np.ascontiguousarray(inputs[name])
        if name in ("x", "ctx") or (a.ndim > 1 and name != "c"):
            a = a.reshape(a.shape[1:])
        arrays[name + "_dram"] = a
    arrays["rope_dram"] = rope_table()
    for name, a in arrays.items():
        args.append(nc.dram_tensor(name, a.shape, mybir.dt.from_np(a.dtype), kind="ExternalInput").ap())
    args.append(nc.dram_tensor("out_dram", (T, D), F32, kind="ExternalOutput").ap())
    build(nc, *args)
    r = run_bass_kernel_spmd(nc, [arrays], core_ids=[0])
    return r.results[0]["out_dram"].reshape(1, T, D)
```

```python
from contextlib import ExitStack

import numpy as np

import concourse.bass as bass
from concourse import mybir

F32 = mybir.dt.float32
F32R = mybir.dt.float32r
ACT = mybir.ActivationFunctionType
ALU = mybir.AluOpType
AX = mybir.AxisListType

P = 128
D = 1024
T = 512
C = 256
K = T + C
GRID_W = 64
HEADS = 8
NOPE, ROPE, VDIM = 64, 32, 64
QK = NOPE + ROPE
QR, KVR = 384, 256
CONV = 512
FF = 2816
EPS = 1e-6
THETA = 10000.0
KV_END = KVR
KR_END = KV_END + ROPE
Q_END = KR_END + QR
CX_END = Q_END + CONV
CB_END = CX_END + CONV
CC_END = CB_END + CONV
GA_END = CC_END + D
DT = D // P
QT, KVT, CT, FT = QR // P, KVR // P, CONV // P, FF // P
TT, CTT, KT = T // P, C // P, K // P
SCALE = float(QK) ** -0.5
SLOTS = 4
UNIT = 1024
BANK = 512

R_C, R_CC, R_BADA, R_N1, R_N2, R_FG = 0, 8, 16, 64, 72, 80
R_QG = 88
R_KVG = R_QG + QT
R_CB = R_KVG + KVT
R_CW = R_CB + CT
R_END0 = R_CW + 3 * CT
R_FW = P
R_FB = R_FW + 6 * FT
R_END = R_FB + 2 * FT

U_ADA = 0
U_Q = U_ADA + 2 * DT
U_KV = U_Q + QT
U_KR = U_KV + KVT
U_UQ = U_KR + 1
U_V = U_UQ + HEADS // 2
U_N = U_V + 1
U_CONV = U_N + 1
U_MERGE = U_CONV + 3 * CT
U_O = U_MERGE + 3 * DT
U_UP = U_O + DT
U_DOWN = U_UP + 2 * FT
U_ALL = U_DOWN + FT
CONV_SPLITS = (9, 13, 17, 21)


def build(nc, x, c, ctx, c_ctx, w_ada, b_ada, norm1_g, w_in, q_norm_g, kv_norm_g, w_uq, w_ukv, conv_w,
          conv_b, w_attn_out, w_conv_out, w_o, norm2_g, w_up, ffn_conv_w, ffn_conv_b, w_down, final_g,
          rope_tab, out):
    stack = ExitStack()
    with stack:
        def sem(name):
            return stack.enter_context(nc.semaphore(name))

        def sb(name, shape, dt=F32, scope=stack):
            return scope.enter_context(nc.sbuf_tensor(name, shape, dt))

        raw = sb("raw", [P, SLOTS, UNIT])
        whi = sb("whi", [P, SLOTS, UNIT], F32R)
        wlo = sb("wlo", [P, SLOTS, UNIT], F32R)
        hhi = sb("hhi", [P, DT, T], F32R)
        hlo = sb("hlo", [P, DT, T], F32R)
        work = sb("work", [P, 6, T])
        tab = sb("tab", [P, T])
        ident = sb("ident", [P, P])
        ones = sb("ones", [P, P])
        eps = sb("eps", [P, 1])
        prm = sb("prm", [P, R_END])
        mod = sb("mod", [P, 6 * DT])
        modc = sb("modc", [P, 2 * DT])
        gain = sb("gain", [P, 3, DT])
        cvec = sb("cvec", [P, DT, 2])
        small = sb("small", [P, 32])

        early = ExitStack()
        xt = sb("xt", [P, KT, D], scope=early)
        rows1 = sb("rows1", [4, 2 * D], scope=early)
        chl = sb("chl", [P, DT, P], F32R, scope=early)
        sb("gap0", [P, 3584], scope=early)
        chi = sb("chi", [P, DT, C], F32R, scope=early)
        clo = sb("clo", [P, DT, C], F32R, scope=early)
        xnT = sb("xnT", [P, DT, K], scope=early)
        ht = sb("ht", [P, 2, K], scope=early)
        early.close()
        att = ExitStack()
        qhi = sb("qhi", [P, HEADS, T], F32R, scope=att)
        qlo = sb("qlo", [P, HEADS, T], F32R, scope=att)
        cq = ExitStack()
        cqhi = sb("cqhi", [P, QT, T], F32R, scope=cq)
        cqlo = sb("cqlo", [P, QT, T], F32R, scope=cq)
        cqraw = sb("cqraw", [P, QT, T], scope=cq)
        qtmp = sb("qtmp", [P, T], scope=cq)
        cq.close()
        pthi = sb("pthi", [P, KT, T], F32R, scope=att)
        ptlo = sb("ptlo", [P, KT, T], F32R, scope=att)
        ckhi = sb("ckhi", [P, KVT, K], F32R, scope=att)
        cklo = sb("cklo", [P, KVT, K], F32R, scope=att)
        khi = sb("khi", [P, 2, K], F32R, scope=att)
        klo = sb("klo", [P, 2, K], F32R, scope=att)
        vs = sb("vs", [P, KT, HEADS, 2 * VDIM], F32R, scope=att)
        pr = ExitStack()
        ckraw = sb("ckraw", [P, KVT, K], scope=pr)
        pr.close()
        prob = sb("prob", [P, 2, K], scope=att)
        att.close()
        mrg = ExitStack()
        sb("gap1", [P, 2 * HEADS * T], scope=mrg)
        zhi = sb("zhi", [P, CT, T], F32R, scope=mrg)
        zlo = sb("zlo", [P, CT, T], F32R, scope=mrg)
        mhi = sb("mhi", [P, DT, T], F32R, scope=mrg)
        mlo = sb("mlo", [P, DT, T], F32R, scope=mrg)
        ada2 = sb("ada2", [P, 2, D], scope=mrg)
        sb("gap2", [P, 1536], scope=mrg)
        x2 = ExitStack()
        x2T = sb("x2T", [P, DT, T], scope=x2)
        x2.close()
        adacc = sb("adacc", [P, 4 * D], scope=mrg)
        mrg.close()
        res = ExitStack()
        rows2 = sb("rows2", [1, 4 * D], scope=res)
        sb("gap3", [P, 4096], scope=res)
        xtok = sb("xtok", [P, TT, D], scope=res)
        res.close()
        ffn = ExitStack()
        fhi = sb("fhi", [P, FT, T], F32R, scope=ffn)
        flo = sb("flo", [P, FT, T], F32R, scope=ffn)
        ffn.close()
        fin = ExitStack()
        yo = sb("yo", [P, TT, D], scope=fin)
        yT = sb("yT", [P, DT, T], scope=fin)
        fin.close()

        ps = stack.enter_context(nc.psum_tensor("ps", [P, 8, BANK], F32))

        def wide(bank):
            return ps[:, bank:bank + 2, :].rearrange("p b n -> p (b n)")[:, 0:K]

        raw_loaded = [sem(f"raw_loaded{s}") for s in range(SLOTS)]
        w_hi, w_lo, w_used = sem("w_hi"), sem("w_lo"), sem("w_used")
        S = {}

        def s(name):
            if name not in S:
                S[name] = sem(name)
            return S[name]

        def wait(e, semaphore, value):
            if not (isinstance(value, int) and value <= 0):
                e.wait_ge(semaphore, value)

        def col(t, at):
            return t[:, bass.ds(at, 1)] if not isinstance(at, int) else t[:, at:at + 1]

        def at1(t, i):
            if isinstance(i, int):
                return t[:, i, :]
            return t[:, bass.ds(i, 1), :].rearrange("p a n -> p (a n)")

        def rows_of(w, k0, k1, c0, n):
            cols = w[:, c0:c0 + n] if isinstance(c0, int) else w[:, bass.ds(c0, n)]
            return cols.rearrange("(k p) n -> p k n", p=P)[:, k0:k1, :]

        def load(sp, u, slot, pieces):
            wait(sp, w_lo, u - SLOTS + 1)
            if not isinstance(u, int):
                sp.sem_inc(s("load_turn"), 1)
            for dst, src in pieces:
                sp.dma_start(dst, src).then_inc(raw_loaded[slot], 16)

        def column_tile(slot, w, c0, kt=DT):
            view = raw[:, slot, 0:kt * P].rearrange("p (k n) -> p k n", n=P)
            h = kt // 2
            return [(view[:, 0:h, :], rows_of(w, 0, h, c0, P)), (view[:, h:kt, :], rows_of(w, h, kt, c0, P))]

        def merge_tile(slot, d):
            view = raw[:, slot, :].rearrange("p (k n) -> p k n", n=P)
            return [(view[:, 0:CT, :], rows_of(w_attn_out, 0, CT, d * P, P)),
                    (view[:, CT:2 * CT, :], rows_of(w_conv_out, 0, CT, d * P, P))]

        def down_tile(slot, k):
            r = w_down[k * P:(k + 1) * P, :] if isinstance(k, int) else w_down[bass.ds(k * P, P), :]
            return [(raw[:, slot, 0:512], r[:, 0:512]), (raw[:, slot, 512:1024], r[:, 512:1024])]

        def arrived(e, u, slot):
            e.wait_ge(raw_loaded[slot], 32 * ((u - slot) // SLOTS + 1) if isinstance(u, int) else (u - slot) * 8 + 32)

        def plain(t, slot, n=UNIT):
            return [t[:, slot, 0:n]]

        def headed_raw(slot, g):
            v = raw[:, slot, 0:g * QK].rearrange("p (g n) -> p g n", n=QK)
            r = v[:, :, NOPE:QK].rearrange("p g (a h j) -> p g a h j", a=2, h=2)
            return [v, r[:, :, :, 1, :], r[:, :, :, 0, :]]

        def headed(t, slot, g):
            v = t[:, slot, 0:g * P].rearrange("p (g n) -> p g n", n=P)
            r = v[:, :, QK:P].rearrange("p g (a h j) -> p g a h j", a=2, h=2)
            return [v[:, :, 0:QK], r[:, :, :, 0, :], r[:, :, :, 1, :]]

        def views(u, slot):
            if isinstance(u, int) and u == U_KR:
                return headed_raw(slot, DT), headed(whi, slot, DT), headed(wlo, slot, DT)
            if isinstance(u, int) and U_UQ <= u < U_UQ + 4:
                return headed_raw(slot, 2 * QT), headed(whi, slot, 2 * QT), headed(wlo, slot, 2 * QT)
            return plain(raw, slot), plain(whi, slot), plain(wlo, slot)

        def split_hi(act, u, slot):
            arrived(act, u, slot)
            wait(act, w_used, u - SLOTS + 1)
            rv, hv, _ = views(u, slot)
            for n, (r, h) in enumerate(zip(rv, hv)):
                ins = nc.scalar.activation(h, r, ACT.Copy)
            ins.then_inc(w_hi, 1)

        def split_lo(e, u, slot, engine=None):
            e.wait_ge(w_hi, u + 1)
            rv, hv, lv = views(u, slot)
            for r, h, l in zip(rv, hv, lv):
                ins = (engine or nc.gpsimd).tensor_tensor(out=l, in0=r, in1=h.bitcast(F32), op=ALU.subtract)
            ins.then_inc(w_lo, 1)

        def used(e, u):
            e.wait_ge(w_used, u + 1)

        def query_ready(e, h):
            if h % 2 == 0:
                e.wait_ge(s("q_ps"), h // 2 + 1)
            else:
                used(e, U_UQ + h // 2)

        def keys_ready(e, pair, part):
            if (pair, part) == (HEADS // 2 - 1, 1):
                used(e, U_N)
            else:
                e.wait_ge(s("k_ps"), 2 * pair + part + 1)

        flat = work[:].rearrange("p a n -> p (a n)")
        sqk = [flat[:, m * K:(m + 1) * K] for m in range(2)]


        def qval(h):
            return (work[:, 3, :], qtmp[:])[h % 2]

        def probs(g):
            if g % 3 < 2:
                return prob[:, g % 3, :]
            return flat[:, 2 * T:2 * T + K]

        kraw = flat[:, 2 * T + K:2 * T + 2 * K]

        def neg_max(g):
            return small[:, 14 + g % 4:15 + g % 4]

        def exp_sum(g, n=1):
            return small[:, 18 + g % 8:18 + g % 8 + n]

        inv_sum = small[:, 8:8 + TT]
        diag = work[:, 5, :]

        G = flat[:, 0:3 * P].rearrange("p (g n) -> p g n", n=P)

        def tile_of(t, slot, k, n=P):
            return t[:, slot, k * n:(k + 1) * n]

        def mm3(pe, o, l, r, start, stop):
            pe.matmul(o, l[0], r[0], start=start, stop=False)
            pe.matmul(o, l[0], r[1], start=False, stop=False)
            return pe.matmul(o, l[1], r[0], start=False, stop=stop)

        def project(pe, o, slot, hi, lo, kt=DT, k0=0, start=True, stop=True):
            for k in range(kt):
                last = mm3(pe, o, (tile_of(whi, slot, k0 + k), tile_of(wlo, slot, k0 + k)),
                           (hi[:, k, :], lo[:, k, :]), start and k == 0, stop and k == kt - 1)
            return last

        def x3_add(dve, d):
            dve.wait_ge(s("x3_sq"), d + 1)
            if d == 0:
                nc.vector.tensor_copy(work[:, 2, :], work[:, 0, :]).then_inc(s("x3_ssq"), 1)
            else:
                dve.wait_ge(s("x3_ssq"), d)
                nc.vector.tensor_tensor(out=work[:, 2, :], in0=work[:, 2, :], in1=work[:, d % 2, :], op=ALU.add).then_inc(s("x3_ssq"), 1)

        block = stack.enter_context(nc.Block())

        @block.sync
        def _(sp):
            for u in range(U_ADA, U_Q):
                k, at = (u - U_ADA) // 2, (u - U_ADA) % 2 * D
                load(sp, u, u % SLOTS, [(raw[:, u % SLOTS, n:n + 512], w_ada[k * P:(k + 1) * P, at + n:at + n + 512])
                                        for n in (0, 512)])
            for m in range(QT):
                u = U_Q + m
                load(sp, u, u % SLOTS, column_tile(u % SLOTS, w_in, KR_END + m * P))
            for m in range(KVT):
                u = U_KV + m
                load(sp, u, u % SLOTS, column_tile(u % SLOTS, w_in, m * P))
            kr = raw[:, U_KR % SLOTS, 0:DT * QK].rearrange("p (k n) -> p k n", n=QK)
            load(sp, U_KR, U_KR % SLOTS, [(kr[:, k:k + 4, :], rows_of(w_in, k, k + 4, KR_END - QK, QK)) for k in (0, 4)])
            for m in range(4):
                slot = (U_UQ + m) % SLOTS
                view = raw[:, slot, 0:2 * QT * QK].rearrange("p (k h n) -> p k h n", k=QT, n=QK)
                load(sp, U_UQ + m, slot, [(view[:, :, h, :], rows_of(w_uq, 0, QT, (2 * m + h) * QK, QK)) for h in (0, 1)])
            ukv = w_ukv.rearrange("(k p) (h n) -> p k h n", p=P, n=NOPE + VDIM)
            slot = U_V % SLOTS
            load(sp, U_V, slot, [(raw[:, slot, k * 512:(k + 1) * 512].rearrange("p (h n) -> p h n", n=VDIM),
                                  ukv[:, k, :, NOPE:]) for k in range(KVT)])
            slot = U_N % SLOTS
            load(sp, U_N, slot, [(raw[:, slot, k * 512:(k + 1) * 512].rearrange("p (h n) -> p h n", n=NOPE),
                                  ukv[:, k, :, 0:NOPE]) for k in range(KVT)])

            def load_ada2(n, k, g):
                wait(sp, s("ada2_used"), n - 1)
                if not isinstance(n, int):
                    sp.sem_inc(s("load_turn"), 1)
                rows = w_ada[k * P:(k + 1) * P, :] if isinstance(k, int) else w_ada[bass.ds(k * P, P), :]
                sp.dma_start(ada2[:, g % 2, :], rows[:, (2 + g) * D:(3 + g) * D]).then_inc(s(f"ada2_loaded{g % 2}"), 16)

            for j in range(CT):
                for n, end in enumerate((Q_END, CB_END, CX_END)):
                    u = U_CONV + 3 * j + n
                    load(sp, u, u % SLOTS, column_tile(u % SLOTS, w_in, end + j * P))
                    if (j, n) in ((2, 1), (3, 1)):
                        if j == 2:
                            sp.wait_ge(s("pv_ps"), 2 * HEADS)
                        for m in range(2):
                            load_ada2(2 * (j - 2) + m, 0, 2 * (j - 2) + m)

            def merge_loads(i):
                for n in range(12):
                    dd, what = n // 3, n % 3
                    d = 4 * i + dd
                    u = U_MERGE + 12 * i + n
                    slot = n % SLOTS
                    load(sp, u, slot, merge_tile(slot, d) if what == 2 else
                         column_tile(slot, w_in, (CC_END, GA_END)[what] + d * P))
                    load_ada2(4 + 12 * i + n, 1 + 3 * i + n // 4, n % 4)

            with sp.Fori(0, 2) as i:
                merge_loads(i)
            for d in range(SLOTS):
                load(sp, U_O + d, d, column_tile(d, w_o, d * P))
                load_ada2(4 * (DT - 1) + d, DT - 1, d)
            used(sp, U_O - 1)
            for t in range(TT):
                sp.dma_start(xtok[:, t, :], x[t * P:(t + 1) * P, :]).then_inc(s("xtok_loaded"), 16)
            for d in range(SLOTS, DT):
                load(sp, U_O + d, d - SLOTS, column_tile(d - SLOTS, w_o, d * P))
            with sp.Fori(0, FT // 2) as i:
                for n in range(4):
                    load(sp, U_UP + 4 * i + n, n, column_tile(n, w_up, (n % 2) * FF + (2 * i + n // 2) * P))
            with sp.Fori(0, FT // 4) as i:
                for n in range(4):
                    load(sp, U_DOWN + 4 * i + n, n, down_tile(n, 4 * i + n))
            for k in range(FT // 4 * 4, FT):
                load(sp, U_DOWN + k, k % 4, down_tile(k % 4, k))
            out_v = out.rearrange("(t p) d -> p t d", p=P)
            for n in range(2):
                sp.wait_ge(s("y_act"), TT * (n + 1))
                sp.wait_ge(s("y_dve"), 3 * (n + 1))
                sp.dma_start(out_v[:, :, n * 512:(n + 1) * 512], yo[:, :, n * 512:(n + 1) * 512]).then_inc(s("stored"), 16)
            sp.wait_ge(s("stored"), 32)

        @block.gpsimd
        def _(pool):
            nc.gpsimd.memset(ident[:], 0.0).then_inc(s("consts"), 1)
            nc.gpsimd.memset(ones[:], 1.0).then_inc(s("consts"), 1)
            nc.gpsimd.memset(eps[:], EPS).then_inc(s("consts"), 1)
            pool.wait_ge(s("consts"), 3)
            nc.gpsimd.affine_select(out=ident[:], in_=ident[:], compare_op=ALU.not_equal, fill=1.0, base=0,
                                    pattern=[[-1, P]], channel_multiplier=1).then_inc(s("consts"), 1)
            nc.gpsimd.memset(chl[:].bitcast(F32), 0.0).then_inc(s("chl_zero"), 1)
            pool.wait_ge(s("mods1"), 8)
            for n in range(2 * DT):
                k, (lo, hi, g, m) = n % DT, ((0, T, 0, mod), (T, K, 1, modc))[n // DT]
                wait(pool, s("h_lo"), n - 1)
                nc.gpsimd.tensor_scalar(ht[:, n % 2, lo:hi], xnT[:, k, lo:hi], gain[:, g, k:k + 1],
                                        m[:, k:k + 1], ALU.mult, ALU.add).then_inc(s("h_t"), 1)
                if n == 4:
                    pool.wait_ge(w_lo, U_Q)
                if n in (4, 8, 11, 14):
                    split_lo(pool, U_Q + (4, 8, 11, 14).index(n), (U_Q + (4, 8, 11, 14).index(n)) % SLOTS)
            for u in range(U_Q + 4, U_CONV):
                split_lo(pool, u, u % SLOTS)

            def keys_split(h):
                pool.wait_ge(s("k_raw"), h // 2 * 2 + 2)
                wait(pool, s("s_ps"), TT * (h - 1))
                src = kraw[h % 2 * NOPE:(h % 2 + 1) * NOPE, :]
                nc.gpsimd.tensor_scalar(khi[0:NOPE, h % 2, :], src, 1.0, None, ALU.mult).then_inc(s("k_hi"), 1)
                if h % 2 == 0:
                    pool.wait_ge(s("k_hi"), h + 1)
                    nc.gpsimd.tensor_tensor(out=klo[0:NOPE, 0, :], in0=src, in1=khi[0:NOPE, 0, :].bitcast(F32),
                                            op=ALU.subtract).then_inc(s("k_lo_even"), 1)

            def diagonals(h):
                pool.wait_ge(s("rsum"), h + 1)
                wait(pool, s("r_ps"), h)
                nc.gpsimd.tensor_tensor(out=diag.rearrange("p (t n) -> p t n", n=P), in0=ident[:].unsqueeze(1).to_broadcast([P, TT, P]),
                                        in1=inv_sum.unsqueeze(2).to_broadcast([P, TT, P]), op=ALU.mult).then_inc(s("diag"), 1)

            def output_lo(h):
                r = slice((h % 2) * VDIM, (h % 2 + 1) * VDIM)
                pool.wait_ge(s("o_hi"), h + 1)
                nc.gpsimd.tensor_tensor(out=qlo[r, h // 2 * 2, :], in0=work[r, 1, :], in1=qhi[r, h // 2 * 2, :].bitcast(F32),
                                        op=ALU.subtract).then_inc(s("o_lo"), 1)

            keys_split(0)
            pool.wait_ge(s("k_lo_even"), 1)
            keys_split(1)
            pool.wait_ge(s("k_hi"), 2)
            for h in range(HEADS):
                diagonals(h)
                pool.wait_ge(s("diag"), h + 1)
                if h + 2 < HEADS:
                    keys_split(h + 2)
                    if h % 2 == 1:
                        pool.wait_ge(s("k_hi"), h + 3)
                    else:
                        pool.wait_ge(s("k_lo_even"), h // 2 + 2)
                if h >= 1:
                    output_lo(h - 1)
                    pool.wait_ge(s("o_lo"), h)
                if 2 <= h < 6:
                    split_lo(pool, U_CONV + h - 2, h - 2)
                    pool.wait_ge(w_lo, U_CONV + h - 1)
            output_lo(HEADS - 1)
            pool.wait_ge(s("o_lo"), HEADS)
            for u in range(U_CONV + 4, U_MERGE):
                split_lo(pool, u, u % SLOTS)
            with pool.Fori(0, (U_DOWN - U_MERGE) // 4) as i:
                for n in range(4):
                    split_lo(pool, U_MERGE + 4 * i + n, n)
            with pool.Fori(0, FT // 4) as i:
                for n in range(4):
                    split_lo(pool, U_DOWN + 4 * i + n, n)
            for k in range(FT // 4 * 4, FT):
                split_lo(pool, U_DOWN + k, k % 4)

        @block.scalar
        def _(act):

            def rows_to(g, r0, a, n):
                act.dma_start(G[r0:r0 + n, g, :], a).then_inc(s("prm_loaded" if g == 0 else "prm_ffn_loaded"), 16)

            rows_to(0, R_C, c.rearrange("a (r n) -> (a r) n", n=P), 8)
            rows_to(0, R_CC, c_ctx.rearrange("(r n) -> r n", n=P), 8)
            rows_to(0, R_BADA, b_ada.rearrange("(r n) -> r n", n=P), 48)
            rows_to(0, R_N1, norm1_g.rearrange("(r n) -> r n", n=P), DT)
            rows_to(0, R_N2, norm2_g.rearrange("(r n) -> r n", n=P), DT)
            rows_to(0, R_FG, final_g.rearrange("(r n) -> r n", n=P), DT)
            rows_to(0, R_QG, q_norm_g.rearrange("(r n) -> r n", n=P), QT)
            rows_to(0, R_KVG, kv_norm_g.rearrange("(r n) -> r n", n=P), KVT)
            rows_to(0, R_CB, conv_b.rearrange("(r n) -> r n", n=P), CT)
            rows_to(0, R_CW, conv_w.rearrange("k (r n) -> (k r) n", n=P), 3 * CT)
            for t in range(TT):
                act.dma_start(xt[:, t, :], x[t * P:(t + 1) * P, :]).then_inc(s(f"x_loaded{t}"), 16)
            for t in range(CTT):
                act.dma_start(xt[:, TT + t, :], ctx[t * P:(t + 1) * P, :]).then_inc(s(f"x_loaded{TT + t}"), 16)
            fw = ffn_conv_w.rearrange("k (r n) -> (k r) n", n=P)
            rows_to(1, 0, fw[0:P, :], P)
            rows_to(2, 0, fw[P:6 * FT, :], 6 * FT - P)
            rows_to(2, 6 * FT - P, ffn_conv_b.rearrange("(r n) -> r n", n=P), 2 * FT)
            act.dma_start(tab[64:P, :], rope_tab).then_inc(s("tab_loaded"), 16)

            act.wait_ge(s("prm"), 1)
            nc.scalar.activation(cvec[:].rearrange("p k s -> p s k"), prm[:, 0:2 * DT].rearrange("p (s k) -> p s k", k=DT),
                                 ACT.Silu).then_inc(s("cvec"), 1)
            act.wait_ge(s("cvec"), 1)
            act.wait_ge(s("chl_zero"), 1)
            nc.scalar.activation(chl[:, :, 0:2], cvec[:], ACT.Copy).then_inc(s("chl_hi"), 1)
            act.wait_ge(s("consts"), 4)

            def xT_copy(t):
                act.wait_ge(s("xT_ps"), t + 1)
                nc.scalar.activation(xnT[:, 4:8, t * P:(t + 1) * P], ps[:, 5 + 2 * (t % 2), :]
                                     .rearrange("p (k n) -> p k n", n=P), ACT.Copy).then_inc(s("xT_act"), 1)

            for u in range(U_ADA, U_Q):
                split_hi(act, u, u % SLOTS)
                if u % 2 == 1 and u // 2 < KT:
                    t = u // 2
                    act.wait_ge(s(f"x_loaded{t}"), 16)
                    wait(act, s("x_ssq"), t)
                    nc.scalar.activation(ht[:].rearrange("p a n -> p (a n)")[:, 0:D], xt[:, t, :], ACT.Square,
                                         accum_out=small[:, t:t + 1]).then_inc(s("x_ssq"), 1)
                    act.wait_ge(s("x_ssq"), t + 1)
                    nc.scalar.activation(small[:, 8 + t:9 + t], small[:, t:t + 1], ACT.Sqrt, bias=eps[:, 0:1],
                                         scale=1.0 / D).then_inc(s("x_rms"), 1)
                if u % 2 == 1 and 1 <= u // 2 <= KT:
                    xT_copy(u // 2 - 1)
            split_hi(act, U_Q, U_Q % SLOTS)
            split_hi(act, U_Q + 1, (U_Q + 1) % SLOTS)
            used(act, U_Q - 1)
            nc.scalar.activation(rows1[:, 0:D], ps[0:4, 0:2, :].rearrange("p b n -> p (b n)"), ACT.Copy).then_inc(s("rows1_act"), 1)
            split_hi(act, U_Q + 2, (U_Q + 2) % SLOTS)
            act.wait_ge(s("mods1"), 8)
            for n in range(2 * DT):
                k, (lo, hi, to, g, m) = n % DT, ((0, T, hhi, 0, mod), (T, K, chi, 1, modc))[n // DT]
                nc.scalar.activation(to[:, k, :], xnT[:, k, lo:hi], ACT.Identity, bias=m[:, k:k + 1],
                                     scale=gain[:, g, k:k + 1]).then_inc(s("h_hi"), 1)
                if n == DT - 1:
                    split_hi(act, U_KV, U_KV % SLOTS)

            for m in range(QT):
                used(act, U_Q + m)
                nc.scalar.activation(work[:, 3 + m, :], ps[:, m, :], ACT.Square).then_inc(s("p_sq"), 1)
                nc.scalar.activation(cqraw[:, m, :], ps[:, m, :], ACT.Copy).then_inc(s("p_raw"), 1)
                split_hi(act, U_KV + 1 + m, (U_KV + 1 + m) % SLOTS)
            act.wait_ge(s("qstat_ps"), 1)
            nc.scalar.activation(work[:, 4, :], ps[:, 3, :], ACT.Sqrt, bias=eps[:, 0:1], scale=1.0 / QR).then_inc(s("q_rms"), 1)
            for m in range(KVT):
                used(act, U_KV + m)
                nc.scalar.activation(sqk[m], wide(4 + 2 * m), ACT.Square).then_inc(s("p_sq"), 1)
                nc.scalar.activation(ckraw[:, m, :], wide(4 + 2 * m), ACT.Copy).then_inc(s("p_raw"), 1)
                split_hi(act, U_UQ + 1 + m, (U_UQ + 1 + m) % SLOTS)
                if m == 0:
                    for mm in range(QT):
                        act.wait_ge(s("cq_t"), mm + 1)
                        nc.scalar.activation(cqhi[:, mm, :], cqraw[:, mm, :], ACT.Copy).then_inc(s("cq_hi"), 1)
            split_hi(act, U_UQ + 3, (U_UQ + 3) % SLOTS)
            act.wait_ge(s("kstat_ps"), 1)
            nc.scalar.activation(sqk[1], wide(2), ACT.Sqrt, bias=eps[:, 0:1], scale=1.0 / KVR).then_inc(s("k_rms"), 1)
            for h in range(HEADS):
                query_ready(act, h)
                wait(act, s("q_lo"), h - 1)
                nc.scalar.activation(qval(h)[0:NOPE, :], ps[0:NOPE, 4 + h % 4, :], ACT.Copy, scale=SCALE).then_inc(s("q_nope"), 1)
                act.wait_ge(s("q_rope"), 3 * h + 3)
                act.wait_ge(s("q_nope"), h + 1)
                nc.scalar.activation(qhi[0:QK, h, :], qval(h)[0:QK, :], ACT.Copy).then_inc(s("q_hi"), 1)
                if h in (1, 3):
                    split_hi(act, U_V + h // 2, (U_V + h // 2) % SLOTS)
                if h == 3:
                    for m in range(KVT):
                        act.wait_ge(s("ck_t"), m + 1)
                        nc.scalar.activation(ckhi[:, m, :], ckraw[:, m, :], ACT.Copy).then_inc(s("ck_hi"), 1)
            for kt in range(KT):
                if kt < KT - 1:
                    act.wait_ge(s("v_ps"), kt + 1)
                else:
                    used(act, U_V)
                nc.scalar.activation(vs[:, kt, :, 0:VDIM], ps[:, kt % 4, :].rearrange("p (h n) -> p h n", n=VDIM),
                                     ACT.Copy).then_inc(s("v_hi"), 1)

            def keys_raw(pair, part):
                lo, hi = ((0, T), (T, K))[part]
                keys_ready(act, pair, part)
                wait(act, s("k_lo_even"), pair)
                wait(act, s("k_lo_odd"), pair)
                nc.scalar.activation(kraw[:, lo:hi], ps[:, 6, 0:hi - lo], ACT.Copy).then_inc(s("k_raw"), 1)

            keys_raw(0, 0)
            keys_raw(0, 1)

            def exps(g):
                act.wait_ge(s("nmax"), g + 1)
                wait(act, s("t_ps"), g - 2)
                nc.scalar.activation(probs(g), wide(2 * (g % 2)), ACT.Exp, bias=neg_max(g), scale=1.0,
                                     accum_out=exp_sum(g)).then_inc(s("p_exp"), 1)

            def output_part(h):
                r = slice((h % 2) * VDIM, (h % 2 + 1) * VDIM)
                act.wait_ge(s("pv_ps"), 2 * h + 2)
                wait(act, s("o_sum"), h)
                nc.scalar.activation(work[r, 0, :], ps[VDIM:P, 7, :], ACT.Copy).then_inc(s("o_part"), 1)

            def output_hi(h):
                r = slice((h % 2) * VDIM, (h % 2 + 1) * VDIM)
                act.wait_ge(s("o_val"), h + 1)
                nc.scalar.activation(qhi[r, h // 2 * 2, :], work[r, 1, :], ACT.Copy).then_inc(s("o_hi"), 1)

            exps(0)
            exps(1)
            for g in range(HEADS * TT):
                h, t = g // TT, g % TT
                act.wait_ge(s("t_ps0"), g + 1)
                wait(act, s("pv_ps"), g // 2 - 1)
                nc.scalar.activation(pthi[:, 0:4, t * P:(t + 1) * P], ps[:, 4, :].rearrange("p (k n) -> p k n", n=P),
                                     ACT.Copy).then_inc(s("pt_hi"), 1)
                act.wait_ge(s("t_ps"), g + 1)
                nc.scalar.activation(pthi[:, 4:KT, t * P:(t + 1) * P], ps[:, 5, 0:K - 4 * P].rearrange("p (k n) -> p k n", n=P),
                                     ACT.Copy).then_inc(s("pt_hi"), 1)
                if g + 2 < HEADS * TT:
                    exps(g + 2)
                if t == 0 and h >= 1:
                    output_part(h - 1)
                if t == 2 and h >= 1:
                    output_hi(h - 1)
                if t >= 2 and h % 2 == 0 and h + 2 < HEADS:
                    keys_raw(h // 2 + 1, t - 2)
                if g in CONV_SPLITS:
                    n = CONV_SPLITS.index(g)
                    split_hi(act, U_CONV + n, n)
            output_part(HEADS - 1)
            output_hi(HEADS - 1)

            for j in range(CT):
                cx, y = work[:, 3 * (j % 2), :], work[:, 3 * (j % 2) + 2, :]
                used(act, U_CONV + 3 * j)
                wait(act, s("z_lo"), j - 1)
                if j == 0:
                    act.wait_ge(s("o_lo"), HEADS)
                nc.scalar.activation(cx, ps[:, 3 * (j % 2), :], ACT.Copy).then_inc(s("c_x"), 1)
                split_hi(act, U_CONV + 3 * j + 4, (3 * j + 4) % SLOTS)
                act.wait_ge(s("c_prod"), j + 1)
                nc.scalar.activation(y, work[:, 3 * (j % 2) + 1, :], ACT.Identity, bias=prm[:, R_CB + j:R_CB + j + 1],
                                     scale=prm[:, R_CW + CT + j:R_CW + CT + j + 1]).then_inc(s("c_mid"), 1)
                split_hi(act, U_CONV + 3 * j + 5, (3 * j + 5) % SLOTS)
                act.wait_ge(s("c_z"), j + 1)
                nc.scalar.activation(zhi[:, j, :], work[:, 3 * (j % 2), :], ACT.Copy).then_inc(s("z_hi"), 1)
                split_hi(act, U_CONV + 3 * j + 6, (3 * j + 6) % SLOTS)

            def merge_hi(i, first):
                for dd in range(4):
                    d = 4 * i + dd
                    b = 4 * (dd % 2)
                    for n in range(3):
                        m = 3 * dd + n
                        if n < 2:
                            used(act, U_MERGE + 3 * d + n)
                            if first and dd == 0:
                                act.wait_ge(s("z_lo"), CT)
                            if not (first and dd < 2):
                                act.wait_ge(s("m_lo"), d - 1)
                            nc.scalar.activation(work[:, 3 * (dd % 2) + n, :], ps[:, b + n, :], ACT.Sigmoid).then_inc(s("g_sig"), 1)
                        else:
                            act.wait_ge(s("m_sum"), d + 1)
                            nc.scalar.activation(at1(mhi, d), work[:, 3 * (dd % 2) + 2, :], ACT.Copy).then_inc(s("m_hi"), 1)
                        split_hi(act, U_MERGE + 12 * i + m + 4, m % SLOTS)

            merge_hi(0, True)
            with act.Fori(1, 2) as i:
                merge_hi(i, False)

            act.wait_ge(s("rows2_ps"), 4)
            nc.scalar.activation(rows2[:, 0:2 * D], ps[0:1, 4:8, :].rearrange("p b n -> p (b n)"), ACT.Copy).then_inc(s("rows2_act"), 1)
            act.wait_ge(s("rows2_ps"), 8)
            nc.scalar.activation(small[:, 30:31], eps[:, 0:1], ACT.Sqrt).then_inc(s("table"), 1)
            for d in range(DT):
                act.wait_ge(s("xT2_ps"), d + 1)
                nc.scalar.activation(x2T[:, d, :], ps[:, 4 + d % 4, :], ACT.Copy).then_inc(s("x2_in"), 1)
                act.wait_ge(s("x2_sum"), d + 1)
                wait(act, s("x2_ssq"), d - 1)
                nc.scalar.activation(work[:, d % 2, :], x2T[:, d, :], ACT.Square).then_inc(s("x2_sq"), 1)
                u = U_O + 4 + d
                split_hi(act, u, u % SLOTS)
            act.wait_ge(s("x2stat_ps"), 1)
            nc.scalar.activation(work[:, 3, :], ps[:, 4, :], ACT.Sqrt, bias=eps[:, 0:1], scale=1.0 / D).then_inc(s("x2_rms"), 1)
            for k in range(DT):
                act.wait_ge(s("h2_t"), k + 1)
                nc.scalar.activation(hhi[:, k, :], work[:, k % 2, :], ACT.Identity,
                                     bias=mod[:, 3 * DT + k:3 * DT + k + 1]).then_inc(s("h2_hi"), 1)

            def up(i, first):
                for jj in range(2):
                    j = 2 * i + jj
                    for n in range(2):
                        used(act, U_UP + 2 * j + n)
                        if first and jj == 0:
                            act.wait_ge(s("h2_lo"), DT)
                        if not (first and jj < 2):
                            act.wait_ge(s("f_prod"), j - 1)
                        nc.scalar.activation(work[:, 3 * jj + n, :], ps[:, 2 * jj + n, :], ACT.Identity,
                                             bias=col(prm, R_FB + n * FT + j),
                                             scale=col(prm, R_FW + 2 * FT + n * FT + j)).then_inc(s("up_mid"), 1)
                        split_hi(act, U_UP + 4 * i + 2 * jj + n + 4, 2 * jj + n)
                    act.wait_ge(s("up_gate"), 2 * j + 2)
                    nc.scalar.activation(work[:, 3 * jj, :], work[:, 3 * jj, :], ACT.Silu).then_inc(s("up_silu"), 1)
                    act.wait_ge(s("f_prod"), j + 1)
                    nc.scalar.activation(at1(fhi, j), work[:, 3 * jj + 2, :], ACT.Copy).then_inc(s("f_hi"), 1)

            up(0, True)
            with act.Fori(1, FT // 2) as i:
                up(i, False)
            with act.Fori(0, (FT - 4) // 4) as i:
                for n in range(4):
                    split_hi(act, U_DOWN + 4 + 4 * i + n, n)
            for k in range(4 + (FT - 4) // 4 * 4, FT):
                split_hi(act, U_DOWN + k, k % 4)
            nc.scalar.activation(small[:, 31:32], eps[:, 0:1], ACT.Sqrt).then_inc(s("table"), 1)
            for d in range(DT):
                act.wait_ge(s("x3_sum"), d + 1)
                wait(act, s("x3_ssq"), d - 1)
                nc.scalar.activation(work[:, d % 2, :], x2T[:, d, :], ACT.Square).then_inc(s("x3_sq"), 1)
                nc.scalar.activation(yT[:, d, :], x2T[:, d, :], ACT.Copy, scale=prm[:, R_FG + d:R_FG + d + 1]).then_inc(s("y_t"), 1)
            act.wait_ge(s("x3stat_ps"), 1)
            nc.scalar.activation(small[:, 0:TT], ps[:, 7, 0:TT], ACT.Sqrt, bias=eps[:, 0:1], scale=1.0 / D).then_inc(s("x3_rms"), 1)
            for d in (3, 7):
                act.wait_ge(s("x3_rinv"), 1)
                act.wait_ge(s("y_ps"), d + 1)
                for t in range(TT):
                    nc.scalar.activation(yo[:, t, d * P:(d + 1) * P], ps[:, d, t * P:(t + 1) * P], ACT.Copy,
                                         scale=small[:, 4 + t:5 + t]).then_inc(s("y_act"), 1)

        @block.vector
        def _(dve):
            dve.wait_ge(s("prm_ps"), 1)
            nc.vector.tensor_copy(prm[:, 0:R_END0], ps[:, 7, 0:R_END0]).then_inc(s("prm"), 1)
            dve.wait_ge(s("chl_hi"), 1)
            nc.vector.tensor_tensor(out=chl[:, :, 2:4], in0=cvec[:], in1=chl[:, :, 0:2].bitcast(F32), op=ALU.subtract).then_inc(s("chl_lo"), 1)

            def xT_copy(t):
                dve.wait_ge(s("xT_ps"), t + 1)
                nc.vector.tensor_copy(xnT[:, 0:4, t * P:(t + 1) * P], ps[:, 4 + 2 * (t % 2), :]
                                      .rearrange("p (k n) -> p k n", n=P)).then_inc(s("xT_dve"), 1)

            for u in range(U_ADA, U_Q):
                split_lo(dve, u, u % SLOTS, nc.vector)
                if u % 2 == 1 and u // 2 < KT:
                    t = u // 2
                    dve.wait_ge(s("x_rms"), t + 1)
                    nc.vector.reciprocal(small[:, 24 + t:25 + t], small[:, 8 + t:9 + t]).then_inc(s("x_rinv"), 1)
                    dve.wait_ge(s("x_rinv"), t + 1)
                    nc.vector.tensor_scalar(xt[:, t, :], xt[:, t, :], small[:, 24 + t:25 + t], None, ALU.mult).then_inc(s("x_norm"), 1)
                if u % 2 == 1 and 1 <= u // 2 <= KT:
                    xT_copy(u // 2 - 1)
            used(dve, U_Q - 1)
            nc.vector.tensor_copy(rows1[:, D:2 * D], ps[0:4, 2:4, :].rearrange("p b n -> p (b n)")).then_inc(s("rows1_dve"), 1)
            dve.wait_ge(s("cols1_ps"), 1)
            cols = ps[:, 4, 0:8 * DT].rearrange("p (m s) -> p s m", s=4)
            for n, m in enumerate((mod[:, 0:2 * DT], modc[:])):
                nc.vector.tensor_tensor(out=m, in0=cols[:, n, :], in1=prm[:, R_BADA:R_BADA + 2 * DT], op=ALU.add).then_inc(s("mods1"), 1)
            dve.wait_ge(s("mods1"), 2)
            for n, m in enumerate((mod[:, 0:2 * DT], modc[:])):
                nc.vector.tensor_tensor(out=m, in0=cols[:, 2 + n, :], in1=m, op=ALU.add).then_inc(s("mods1"), 1)
            dve.wait_ge(s("mods1"), 4)
            for g, m in ((0, mod), (1, modc)):
                nc.vector.scalar_tensor_tensor(out=gain[:, g, :], in0=m[:, DT:2 * DT], scalar=1.0, in1=prm[:, R_N1:R_N1 + DT],
                                               op0=ALU.add, op1=ALU.mult).then_inc(s("mods1"), 2)
            for n in range(2 * DT):
                k, (lo, hi, dst, src) = n % DT, ((0, T, hlo, hhi), (T, K, clo, chi))[n // DT]
                dve.wait_ge(s("h_t"), n + 1)
                dve.wait_ge(s("h_hi"), n + 1)
                nc.vector.tensor_tensor(out=dst[:, k, :], in0=ht[:, n % 2, lo:hi], in1=src[:, k, :].bitcast(F32),
                                        op=ALU.subtract).then_inc(s("h_lo"), 1)
            dve.wait_ge(s("prm_ffn_ps"), 1)
            nc.vector.tensor_copy(prm[:, R_FW:R_END], ps[:, 7, R_FW:R_END]).then_inc(s("prm_ffn"), 1)
            for m in range(1, QT):
                dve.wait_ge(s("p_sq"), m + 1)
                wait(dve, s("q_sum"), m - 1)
                nc.vector.tensor_tensor(out=work[:, 3, :], in0=work[:, 3, :], in1=work[:, 3 + m, :], op=ALU.add).then_inc(s("q_sum"), 1)
            dve.wait_ge(s("q_rms"), 1)
            nc.vector.reciprocal(work[:, 5, :], work[:, 4, :]).then_inc(s("q_rinv"), 1)
            dve.wait_ge(s("q_rinv"), 1)
            for m in range(QT):
                nc.vector.scalar_tensor_tensor(out=cqraw[:, m, :], in0=cqraw[:, m, :], scalar=prm[:, R_QG + m:R_QG + m + 1],
                                               in1=work[:, 5, :], op0=ALU.mult, op1=ALU.mult).then_inc(s("cq_t"), 1)
            for m in range(QT):
                dve.wait_ge(s("cq_hi"), m + 1)
                nc.vector.tensor_tensor(out=cqlo[:, m, :], in0=cqraw[:, m, :], in1=cqhi[:, m, :].bitcast(F32),
                                        op=ALU.subtract).then_inc(s("cq_lo"), 1)
            dve.wait_ge(s("p_sq"), QT + 2)
            nc.vector.tensor_tensor(out=sqk[0], in0=sqk[0], in1=sqk[1], op=ALU.add).then_inc(s("k_ssq"), 1)
            used(dve, U_KR)
            dve.wait_ge(s("tab_loaded"), 16)
            kr = work[NOPE:QK, 3:5, :].rearrange("p a n -> p (a n)")
            tmp = work[NOPE:QK, 5, :]
            nc.vector.tensor_tensor(out=kr[:, 0:T], in0=ps[NOPE:QK, 0, :], in1=tab[NOPE:QK, :], op=ALU.mult).then_inc(s("kr"), 1)
            nc.vector.tensor_tensor(out=tmp, in0=ps[QK:P, 0, :], in1=tab[QK:P, :], op=ALU.mult).then_inc(s("kr"), 1)
            nc.vector.tensor_copy(kr[:, T:K], ps[NOPE:QK, 1, 0:C]).then_inc(s("kr"), 1)
            dve.wait_ge(s("kr"), 3)
            nc.vector.tensor_tensor(out=kr[:, 0:T], in0=kr[:, 0:T], in1=tmp, op=ALU.add).then_inc(s("kr"), 1)
            dve.wait_ge(s("kr"), 4)
            for b in range(2):
                nc.vector.tensor_copy(khi[NOPE:QK, b, :], kr[:, 0:K]).then_inc(s("kr"), 1)
            dve.wait_ge(s("kr"), 6)
            for b in range(2):
                nc.vector.tensor_tensor(out=klo[NOPE:QK, b, :], in0=kr[:, 0:K], in1=khi[NOPE:QK, b, :].bitcast(F32),
                                        op=ALU.subtract).then_inc(s("kr"), 1)
            dve.wait_ge(s("kr"), 8)
            def value_lo(kt):
                dve.wait_ge(s("v_hi"), kt + 1)
                nc.vector.tensor_tensor(out=vs[:, kt, :, VDIM:], in0=ps[:, kt % 4, :].rearrange("p (h n) -> p h n", n=VDIM),
                                        in1=vs[:, kt, :, 0:VDIM].bitcast(F32), op=ALU.subtract).then_inc(s("v_lo"), 1)

            for h in range(HEADS):
                r1, r2 = work[NOPE:QK, 4, :], work[NOPE:QK, 5, :]
                query_ready(dve, h)
                wait(dve, s("q_rope"), 3 * h)
                for n, (r, at) in enumerate(((r1, NOPE), (r2, QK))):
                    nc.vector.scalar_tensor_tensor(out=r, in0=ps[at:at + ROPE, 4 + h % 4, :], scalar=SCALE, in1=tab[at:at + ROPE, :],
                                                   op0=ALU.mult, op1=ALU.mult).then_inc(s("q_rope"), 1)
                dve.wait_ge(s("q_rope"), 3 * h + 2)
                wait(dve, s("q_lo"), h - 1)
                nc.vector.tensor_tensor(out=qval(h)[NOPE:QK, :], in0=r1, in1=r2, op=ALU.add).then_inc(s("q_rope"), 1)
                dve.wait_ge(s("q_hi"), h + 1)
                nc.vector.tensor_tensor(out=qlo[0:QK, h, :], in0=qval(h)[0:QK, :], in1=qhi[0:QK, h, :].bitcast(F32),
                                        op=ALU.subtract).then_inc(s("q_lo"), 1)
                if h == 1:
                    dve.wait_ge(s("k_rms"), 1)
                    nc.vector.reciprocal(sqk[0], sqk[1]).then_inc(s("k_rinv"), 1)
                    dve.wait_ge(s("k_rinv"), 1)
                    for m in range(KVT):
                        nc.vector.scalar_tensor_tensor(out=ckraw[:, m, :], in0=ckraw[:, m, :], scalar=prm[:, R_KVG + m:R_KVG + m + 1],
                                                       in1=sqk[0], op0=ALU.mult, op1=ALU.mult).then_inc(s("ck_t"), 1)
                if h == 4:
                    for m in range(KVT):
                        dve.wait_ge(s("ck_hi"), m + 1)
                        nc.vector.tensor_tensor(out=cklo[:, m, :], in0=ckraw[:, m, :], in1=ckhi[:, m, :].bitcast(F32),
                                                op=ALU.subtract).then_inc(s("ck_lo"), 1)
            for kt in range(KT):
                value_lo(kt)

            def maxima(g):
                dve.wait_ge(s("s_ps"), g + 1)
                wait(dve, s("p_exp"), g - 3)
                nc.vector.reduce_max(neg_max(g), wide(2 * (g % 2)), AX.X, negate=True).then_inc(s("nmax"), 1)

            def inverse(h):
                dve.wait_ge(s("p_exp"), TT * (h + 1))
                wait(dve, s("diag"), h)
                nc.vector.reciprocal(inv_sum, exp_sum(TT * h, TT)).then_inc(s("rsum"), 1)

            def output_value(h):
                r = slice((h % 2) * VDIM, (h % 2 + 1) * VDIM)
                dve.wait_ge(s("o_part"), h + 1)
                wait(dve, s("o_lo"), h)
                nc.vector.tensor_tensor(out=work[r, 1, :], in0=ps[0:VDIM, 7, :], in1=work[r, 0, :], op=ALU.add).then_inc(s("o_sum"), 1)
                dve.wait_ge(s("o_sum"), h + 1)
                dve.wait_ge(s("r_ps"), h + 1)
                nc.vector.tensor_tensor(out=work[r, 1, :], in0=ps[r, 6, :], in1=work[r, 1, :], op=ALU.mult).then_inc(s("o_val"), 1)

            def keys_lo(h):
                dve.wait_ge(s("k_hi"), h + 1)
                nc.vector.tensor_tensor(out=klo[0:NOPE, 1, :], in0=kraw[NOPE:P, :], in1=khi[0:NOPE, 1, :].bitcast(F32),
                                        op=ALU.subtract).then_inc(s("k_lo_odd"), 1)

            maxima(0)
            keys_lo(1)
            maxima(1)
            for g in range(HEADS * TT):
                h, t = g // TT, g % TT
                if g + 2 < HEADS * TT:
                    maxima(g + 2)
                if t == 2:
                    inverse(h)
                dve.wait_ge(s("pt_hi"), 2 * g + 1)
                nc.vector.tensor_tensor(out=ptlo[:, 0:4, t * P:(t + 1) * P], in0=ps[:, 4, :].rearrange("p (k n) -> p k n", n=P),
                                        in1=pthi[:, 0:4, t * P:(t + 1) * P].bitcast(F32), op=ALU.subtract).then_inc(s("pt_lo0"), 1)
                dve.wait_ge(s("pt_hi"), 2 * g + 2)
                nc.vector.tensor_tensor(out=ptlo[:, 4:KT, t * P:(t + 1) * P],
                                        in0=ps[:, 5, 0:K - 4 * P].rearrange("p (k n) -> p k n", n=P),
                                        in1=pthi[:, 4:KT, t * P:(t + 1) * P].bitcast(F32), op=ALU.subtract).then_inc(s("pt_lo"), 1)
                if t == 0 and h >= 2 and h % 2 == 0:
                    keys_lo(h + 1)
                if t == 1 and h >= 1:
                    output_value(h - 1)
            output_value(HEADS - 1)

            def ada2_add(n, k, g):
                gg = g * D
                if isinstance(n, int):
                    dve.wait_ge(s(f"ada2_loaded{g % 2}"), 16 * (n // 2 + 1))
                else:
                    dve.wait_ge(s(f"ada2_loaded{g % 2}"), (n - g % 2) * 8 + 16)
                cv = cvec[:, k, 0:1] if isinstance(k, int) else cvec[:, bass.ds(k, 1), 0:1].rearrange("p a b -> p (a b)")
                if isinstance(k, int) and k == 0:
                    nc.vector.tensor_scalar(adacc[:, gg:gg + D], ada2[:, g % 2, :], cv, None, ALU.mult).then_inc(s("ada2_used"), 1)
                else:
                    dve.wait_ge(s("ada2_used"), n - 3)
                    nc.vector.scalar_tensor_tensor(out=adacc[:, gg:gg + D], in0=ada2[:, g % 2, :], scalar=cv,
                                                   in1=adacc[:, gg:gg + D], op0=ALU.mult, op1=ALU.add).then_inc(s("ada2_used"), 1)

            for j in range(CT):
                b = 3 * (j % 2)
                cx, prod, y = (work[:, b + n, :] for n in range(3))
                used(dve, U_CONV + 3 * j + 1)
                dve.wait_ge(s("c_x"), j + 1)
                nc.vector.tensor_tensor(out=prod, in0=ps[:, b + 1, :], in1=cx, op=ALU.mult).then_inc(s("c_prod"), 1)
                dve.wait_ge(s("c_mid"), j + 1)
                nc.vector.scalar_tensor_tensor(out=y[:, 1:T], in0=prod[:, 0:T - 1], scalar=prm[:, R_CW + j:R_CW + j + 1],
                                               in1=y[:, 1:T], op0=ALU.mult, op1=ALU.add).then_inc(s("c_tap"), 1)
                dve.wait_ge(s("c_tap"), 2 * j + 1)
                nc.vector.scalar_tensor_tensor(out=y[:, 0:T - 1], in0=prod[:, 1:T], scalar=prm[:, R_CW + 2 * CT + j:R_CW + 2 * CT + j + 1],
                                               in1=y[:, 0:T - 1], op0=ALU.mult, op1=ALU.add).then_inc(s("c_tap"), 1)
                dve.wait_ge(s("c_tap"), 2 * j + 2)
                used(dve, U_CONV + 3 * j + 2)
                nc.vector.tensor_tensor(out=cx, in0=ps[:, b + 2, :], in1=y, op=ALU.mult).then_inc(s("c_z"), 1)
                dve.wait_ge(s("z_hi"), j + 1)
                nc.vector.tensor_tensor(out=zlo[:, j, :], in0=cx, in1=zhi[:, j, :].bitcast(F32), op=ALU.subtract).then_inc(s("z_lo"), 1)
                if j in (1, 3):
                    for m in range(4):
                        ada2_add(4 * (j // 2) + m, j // 2, m)

            def merge_lo(i, first):
                for dd in range(4):
                    d = 4 * i + dd
                    b, w = 4 * (dd % 2), 3 * (dd % 2)
                    for n in range(2):
                        used(dve, U_MERGE + 3 * d + 2)
                        dve.wait_ge(s("g_sig"), 2 * d + n + 1)
                        nc.vector.tensor_tensor(out=work[:, w + n, :], in0=ps[:, b + 2 + n, :], in1=work[:, w + n, :],
                                                op=ALU.mult).then_inc(s("m_prod"), 1)
                    dve.wait_ge(s("m_prod"), 2 * d + 2)
                    if not (first and dd < 2):
                        dve.wait_ge(s("m_lo"), d - 1)
                    nc.vector.tensor_tensor(out=work[:, w + 2, :], in0=work[:, w, :], in1=work[:, w + 1, :],
                                            op=ALU.add).then_inc(s("m_sum"), 1)
                    for m in range(3):
                        nn = 3 * dd + m
                        ada2_add(8 + 12 * i + nn, 2 + 3 * i + nn // 4, nn % 4)
                    dve.wait_ge(s("m_hi"), d + 1)
                    nc.vector.tensor_tensor(out=at1(mlo, d), in0=work[:, w + 2, :], in1=at1(mhi, d).bitcast(F32),
                                            op=ALU.subtract).then_inc(s("m_lo"), 1)

            merge_lo(0, True)
            with dve.Fori(1, 2) as i:
                merge_lo(i, False)

            dve.wait_ge(s("rows2_ps"), 8)
            nc.vector.tensor_copy(rows2[:, 2 * D:4 * D], ps[0:1, 4:8, :].rearrange("p b n -> p (b n)")).then_inc(s("rows2_dve"), 1)
            dve.wait_ge(s("cols2_ps"), 1)
            nc.vector.tensor_tensor(out=mod[:, 2 * DT:6 * DT], in0=ps[:, 3, 0:4 * DT], in1=prm[:, R_BADA + 2 * DT:R_BADA + 6 * DT],
                                    op=ALU.add).then_inc(s("mods2"), 4)
            dve.wait_ge(s("mods2"), 4)
            nc.vector.scalar_tensor_tensor(out=gain[:, 2, :], in0=mod[:, 4 * DT:5 * DT], scalar=1.0, in1=prm[:, R_N2:R_N2 + DT],
                                           op0=ALU.add, op1=ALU.mult).then_inc(s("mods2"), 1)
            for d in range(DT):
                used(dve, U_O + d)
                dve.wait_ge(s("x2_in"), d + 1)
                nc.vector.scalar_tensor_tensor(out=x2T[:, d, :], in0=ps[:, d % 4, :], scalar=mod[:, 2 * DT + d:2 * DT + d + 1],
                                               in1=x2T[:, d, :], op0=ALU.mult, op1=ALU.add).then_inc(s("x2_sum"), 1)
                dve.wait_ge(s("x2_sq"), d + 1)
                if d == 0:
                    nc.vector.tensor_copy(work[:, 2, :], work[:, 0, :]).then_inc(s("x2_ssq"), 1)
                else:
                    dve.wait_ge(s("x2_ssq"), d)
                    nc.vector.tensor_tensor(out=work[:, 2, :], in0=work[:, 2, :], in1=work[:, d % 2, :], op=ALU.add).then_inc(s("x2_ssq"), 1)
            dve.wait_ge(s("x2_rms"), 1)
            nc.vector.reciprocal(work[:, 4, :], work[:, 3, :]).then_inc(s("x2_rinv"), 1)
            dve.wait_ge(s("x2_rinv"), 1)
            def h2_t(k):
                wait(dve, s("h2_lo"), k - 1)
                nc.vector.scalar_tensor_tensor(out=work[:, k % 2, :], in0=x2T[:, k, :], scalar=gain[:, 2, k:k + 1],
                                               in1=work[:, 4, :], op0=ALU.mult, op1=ALU.mult).then_inc(s("h2_t"), 1)

            h2_t(0)
            for k in range(DT):
                if k + 1 < DT:
                    h2_t(k + 1)
                dve.wait_ge(s("h2_hi"), k + 1)
                nc.vector.scalar_tensor_tensor(out=hlo[:, k, :], in0=work[:, k % 2, :], scalar=mod[:, 3 * DT + k:3 * DT + k + 1],
                                               in1=hhi[:, k, :].bitcast(F32), op0=ALU.add, op1=ALU.subtract).then_inc(s("h2_lo"), 1)

            def up(i, first):
                for jj in range(2):
                    j = 2 * i + jj
                    for n in range(2):
                        u, p = work[:, 3 * jj + n, :], ps[:, 2 * jj + n, :]
                        dve.wait_ge(s("up_mid"), 2 * j + n + 1)
                        nc.vector.scalar_tensor_tensor(out=u[:, 1:T], in0=p[:, 0:T - 1], scalar=col(prm, R_FW + n * FT + j),
                                                       in1=u[:, 1:T], op0=ALU.mult, op1=ALU.add).then_inc(s("up_gate" if n == 0 else "up_val"), 1)
                        dve.wait_ge(s("up_gate" if n == 0 else "up_val"), 2 * j + 1)
                        nc.vector.scalar_tensor_tensor(out=u[:, 0:T - 1], in0=p[:, 1:T], scalar=col(prm, R_FW + 4 * FT + n * FT + j),
                                                       in1=u[:, 0:T - 1], op0=ALU.mult, op1=ALU.add).then_inc(s("up_gate" if n == 0 else "up_val"), 1)
                    dve.wait_ge(s("up_val"), 2 * j + 2)
                    dve.wait_ge(s("up_silu"), j + 1)
                    if not (first and jj < 2):
                        dve.wait_ge(s("f_lo"), j - 1)
                    nc.vector.tensor_tensor(out=work[:, 3 * jj + 2, :], in0=work[:, 3 * jj, :], in1=work[:, 3 * jj + 1, :],
                                            op=ALU.mult).then_inc(s("f_prod"), 1)
                    dve.wait_ge(s("f_hi"), j + 1)
                    nc.vector.tensor_tensor(out=at1(flo, j), in0=work[:, 3 * jj + 2, :], in1=at1(fhi, j).bitcast(F32),
                                            op=ALU.subtract).then_inc(s("f_lo"), 1)

            up(0, True)
            with dve.Fori(1, FT // 2) as i:
                up(i, False)
            for d in range(DT):
                dve.wait_ge(s("d_ps"), d + 1)
                nc.vector.scalar_tensor_tensor(out=x2T[:, d, :], in0=ps[:, d, :], scalar=mod[:, 5 * DT + d:5 * DT + d + 1],
                                               in1=x2T[:, d, :], op0=ALU.mult, op1=ALU.add).then_inc(s("x3_sum"), 1)
                if d >= 1:
                    x3_add(dve, d - 1)
            x3_add(dve, DT - 1)
            dve.wait_ge(s("x3_rms"), 1)
            nc.vector.reciprocal(small[:, 4:4 + TT], small[:, 0:TT]).then_inc(s("x3_rinv"), 1)
            dve.wait_ge(s("x3_rinv"), 1)
            inv = small[:, 4:4 + TT].unsqueeze(2).to_broadcast([P, TT, P])
            for d in (0, 1, 2, 4, 5, 6):
                dve.wait_ge(s("y_ps"), d + 1)
                nc.vector.tensor_tensor(out=yo[:, :, d * P:(d + 1) * P], in0=ps[:, d, :].rearrange("p (t n) -> p t n", n=P),
                                        in1=inv, op=ALU.mult).then_inc(s("y_dve"), 1)

        @block.tensor
        def _(pe):
            pe.wait_ge(s("consts"), 4)
            pe.wait_ge(s("prm_loaded"), 16 * 10)
            pe.transpose(ps[:, 7, 0:R_END0], G[0:R_END0, 0, :], ident[0:R_END0, 0:R_END0]).then_inc(s("prm_ps"), 1)
            pe.wait_ge(s("chl_lo"), 1)

            def unit(u):
                pe.wait_ge(w_lo, u + 1)

            for u in range(U_ADA, U_Q):
                k, half = (u - U_ADA) // 2, (u - U_ADA) % 2
                unit(u)
                for b in range(2):
                    for w in (whi, wlo):
                        last = pe.matmul(ps[:, 2 * half + b, :], chl[:, k, :], tile_of(w, u % SLOTS, b, 512),
                                         start=k == 0 and w is whi, stop=k == DT - 1 and w is wlo)
                last.then_inc(w_used, 1)
                t = u // 2
                if u % 2 == 1 and t < KT:
                    pe.wait_ge(s("x_norm"), t + 1)
                    wait(pe, s("xT_dve"), t - 1)
                    wait(pe, s("xT_act"), t - 1)
                    for m in range(DT):
                        last = pe.transpose(ps[:, 4 + 2 * (t % 2) + m // 4, (m % 4) * P:(m % 4 + 1) * P],
                                            xt[:, t, m * P:(m + 1) * P], ident[:])
                    last.then_inc(s("xT_ps"), 1)
            pe.wait_ge(s("rows1_act"), 1)
            pe.wait_ge(s("rows1_dve"), 1)
            pe.wait_ge(s("xT_dve"), KT)
            for m in range(2 * DT):
                last = pe.transpose(ps[:, 4, 4 * m:4 * m + 4], rows1[:, m * P:(m + 1) * P], ident[0:4, 0:4])
            last.then_inc(s("cols1_ps"), 1)
            pe.wait_ge(s("xT_act"), KT)
            pe.wait_ge(s("prm_ffn_loaded"), 16 * 3)
            pe.transpose(ps[:, 7, P:2 * P], G[:, 1, :], ident[:])
            n = R_END - 2 * P
            pe.transpose(ps[:, 7, 2 * P:R_END], G[0:n, 2, :], ident[0:n, 0:n]).then_inc(s("prm_ffn_ps"), 1)

            for k in range(DT):
                pe.wait_ge(s("h_lo"), k + 1)
                for m in range(QT):
                    u = U_Q + m
                    if k == 0:
                        unit(u)
                    last = mm3(pe, ps[:, m, :], (tile_of(whi, u % SLOTS, k), tile_of(wlo, u % SLOTS, k)),
                               (hhi[:, k, :], hlo[:, k, :]), k == 0, k == DT - 1)
                    if k == DT - 1:
                        last.then_inc(w_used, 1)
            for n, u in enumerate((U_KV, U_KV + 1, U_KR)):
                bank = (4, 6, 0)[n]
                unit(u)
                if n == 0:
                    pe.wait_ge(s("h_lo"), 2 * DT)
                if n == 1:
                    pe.wait_ge(s("prm_ffn"), 1)
                    pe.wait_ge(s("q_sum"), QT - 1)
                    pe.matmul(ps[:, 3, :], ones[:], work[:, 3, :], start=True, stop=True).then_inc(s("qstat_ps"), 1)
                if n == 2:
                    pe.wait_ge(s("p_raw"), QT)
                project(pe, ps[:, bank + 1, 0:C], u % SLOTS, chi, clo)
                project(pe, ps[:, bank, :], u % SLOTS, hhi, hlo).then_inc(w_used, 1)
            pe.wait_ge(s("k_ssq"), 1)
            pe.wait_ge(s("q_rms"), 1)
            pe.matmul(ps[:, 3, 0:C], ones[:], sqk[0][:, T:K], start=True, stop=True)
            pe.matmul(ps[:, 2, :], ones[:], sqk[0][:, 0:T], start=True, stop=True).then_inc(s("kstat_ps"), 1)
            pe.wait_ge(s("cq_lo"), QT)
            pe.wait_ge(s("p_raw"), QT + KVT)
            for h in range(HEADS):
                unit(U_UQ + h // 2)
                wait(pe, s("q_rope"), 3 * (h - 3))
                wait(pe, s("q_nope"), h - 3)
                slot = (U_UQ + h // 2) % SLOTS
                for k in range(QT):
                    w = tuple(t[:, slot, (2 * k + h % 2) * P:(2 * k + h % 2 + 1) * P] for t in (whi, wlo))
                    last = mm3(pe, ps[:, 4 + h % 4, :], w, (cqhi[:, k, :], cqlo[:, k, :]), k == 0, k == QT - 1)
                last.then_inc(s("q_ps") if h % 2 == 0 else w_used, 1)

            def keys(pair, part):
                lo, hi = ((0, T), (T, K))[part]
                slot = U_N % SLOTS
                wait(pe, s("k_raw"), 2 * pair + part)
                wait(pe, s("o_val"), 2 * pair - 2)
                for k in range(KVT):
                    w = tuple(t[:, slot, k * 512 + pair * P:k * 512 + (pair + 1) * P] for t in (whi, wlo))
                    last = mm3(pe, ps[:, 6, 0:hi - lo], w, (ckhi[:, k, lo:hi], cklo[:, k, lo:hi]), k == 0, k == KVT - 1)
                last.then_inc(w_used if (pair, part) == (HEADS // 2 - 1, 1) else s("k_ps"), 1)

            unit(U_V)
            pe.wait_ge(s("ck_lo"), KVT)
            pe.wait_ge(s("k_rms"), 1)
            pe.wait_ge(s("kr"), 8)
            slot = U_V % SLOTS
            for kt in range(KT):
                wait(pe, s("v_lo"), kt - 3)
                for k in range(KVT):
                    last = mm3(pe, ps[:, kt % 4, :], (ckhi[:, k, kt * P:(kt + 1) * P], cklo[:, k, kt * P:(kt + 1) * P]),
                               (tile_of(whi, slot, k, 512), tile_of(wlo, slot, k, 512)), k == 0, k == KVT - 1)
                last.then_inc(s("v_ps") if kt < KT - 1 else w_used, 1)
            unit(U_N)
            pe.wait_ge(s("q_lo"), HEADS - 1)
            keys(0, 0)
            keys(0, 1)

            def scores(g):
                h, t = g // TT, g % TT
                wait(pe, s("p_exp"), g - 1)
                if g == 0:
                    pe.wait_ge(s("q_lo"), HEADS)
                    pe.wait_ge(s("v_lo"), KT)
                pe.wait_ge(s(("k_lo_even", "k_lo_odd")[h % 2]), h // 2 + 1)
                q = tuple(x_[0:QK, h, t * P:(t + 1) * P] for x_ in (qhi, qlo))
                for bank, lo, hi in ((1, T, K), (0, 0, T)):
                    last = mm3(pe, ps[:, 2 * (g % 2) + bank, 0:hi - lo], q,
                               (khi[0:QK, h % 2, lo:hi], klo[0:QK, h % 2, lo:hi]), True, True)
                last.then_inc(s("s_ps"), 1)

            def transposes(g):
                pe.wait_ge(s("p_exp"), g + 1)
                for half, lo, hi in ((0, 0, 4), (1, 4, KT)):
                    wait(pe, s("pt_lo" if half else "pt_lo0"), g)
                    for kt in range(lo, hi):
                        last = pe.transpose(ps[:, 4 + half, (kt - lo) * P:(kt - lo + 1) * P], probs(g)[:, kt * P:(kt + 1) * P], ident[:])
                    last.then_inc(s("t_ps" if half else "t_ps0"), 1)

            def output(h, half):
                pe.wait_ge(s("pt_lo"), TT * h + 2 * half + 2)
                wait(pe, s("o_val"), h)
                q = slice(half * 2 * P, (half + 1) * 2 * P)
                for kt in range(KT):
                    for n, p_ in enumerate((pthi, ptlo)):
                        last = pe.matmul(ps[:, 7, q], vs[:, kt, h, :], p_[:, kt, q], start=kt == 0 and n == 0,
                                         stop=kt == KT - 1 and n == 1)
                last.then_inc(s("pv_ps"), 1)

            def row_factors(h):
                pe.wait_ge(s("k_raw"), min(2 * (h // 2) + 4, HEADS))
                pe.wait_ge(s("diag"), h + 1)
                pe.matmul(ps[:, 6, :], ones[:], diag, start=True, stop=True).then_inc(s("r_ps"), 1)

            scores(0)
            scores(1)
            for g in range(HEADS * TT):
                h, t = g // TT, g % TT
                if g + 2 < HEADS * TT:
                    scores(g + 2)
                if t == 3:
                    output(h, 0)
                transposes(g)
                if t == 0 and h >= 1:
                    output(h - 1, 1)
                    row_factors(h - 1)
                if t >= 2 and h % 2 == 0 and h + 2 < HEADS:
                    keys(h // 2 + 1, t - 2)
            output(HEADS - 1, 1)
            row_factors(HEADS - 1)

            for j in range(CT):
                for n in range(3):
                    u = U_CONV + 3 * j + n
                    unit(u)
                    wait(pe, s("c_z"), j - 1)
                    project(pe, ps[:, 3 * (j % 2) + n, :], u % SLOTS, hhi, hlo).then_inc(w_used, 1)

            def merge(i, first):
                for dd in range(4):
                    d, b = 4 * i + dd, 4 * (dd % 2)
                    if first and dd == 0:
                        pe.wait_ge(s("z_lo"), CT)
                        pe.wait_ge(s("o_lo"), HEADS)
                    if not (first and dd < 2):
                        pe.wait_ge(s("m_prod"), 2 * d - 2)
                    for n in range(2):
                        m = 3 * dd + n
                        pe.wait_ge(w_lo, U_MERGE + 12 * i + m + 1)
                        project(pe, ps[:, b + n, :], m % SLOTS, hhi, hlo).then_inc(w_used, 1)
                    m = 3 * dd + 2
                    slot = m % SLOTS
                    pe.wait_ge(w_lo, U_MERGE + 12 * i + m + 1)
                    for k in range(CT):
                        mm3(pe, ps[:, b + 2, :], (tile_of(whi, slot, k), tile_of(wlo, slot, k)),
                            (qhi[:, 2 * k, :], qlo[:, 2 * k, :]), k == 0, k == CT - 1)
                    project(pe, ps[:, b + 3, :], slot, zhi, zlo, kt=CT, k0=CT).then_inc(w_used, 1)

            merge(0, True)
            with pe.Fori(1, 2) as i:
                merge(i, False)

            def mod_rows(b0):
                for b in range(b0, b0 + 4):
                    pe.matmul(ps[0:1, 4 + b % 4, :], ones[:, 0:1], adacc[:, b * 512:(b + 1) * 512], start=True, stop=True).then_inc(s("rows2_ps"), 1)

            pe.wait_ge(s("m_lo"), DT)

            def residual_in(d):
                wait(pe, s("x2_in"), d - 3)
                for t in range(TT):
                    last = pe.transpose(ps[:, 4 + d % 4, t * P:(t + 1) * P], xtok[:, t, d * P:(d + 1) * P], ident[:])
                last.then_inc(s("xT2_ps"), 1)

            for d in range(DT):
                unit(U_O + d)
                wait(pe, s("x2_sum"), d - 3)
                if d == 3:
                    pe.wait_ge(s("mods2"), 4)
                project(pe, ps[:, d % 4, :], d % SLOTS, mhi, mlo).then_inc(w_used, 1)
                if d == 0:
                    pe.wait_ge(s("ada2_used"), 4 * DT)
                    pe.wait_ge(s("m_prod"), 2 * DT)
                    mod_rows(0)
                if d == 1:
                    pe.wait_ge(s("rows2_act"), 1)
                    mod_rows(4)
                if d == 2:
                    pe.wait_ge(s("rows2_dve"), 1)
                    for m in range(4 * DT):
                        last = pe.transpose(ps[:, 3, m:m + 1], rows2[:, m * P:(m + 1) * P], ident[0:1, 0:1])
                    last.then_inc(s("cols2_ps"), 1)
                    pe.wait_ge(s("xtok_loaded"), 16 * TT)
                    for n in range(3):
                        residual_in(n)
                if d >= 3:
                    residual_in(d)
            pe.wait_ge(s("x2_ssq"), DT)
            pe.matmul(ps[:, 4, :], ones[:], work[:, 2, :], start=True, stop=True).then_inc(s("x2stat_ps"), 1)

            def up(i):
                for jj in range(2):
                    j = 2 * i + jj
                    for n in range(2):
                        m = 2 * jj + n
                        pe.wait_ge(w_lo, U_UP + 4 * i + m + 1)
                        pe.wait_ge(s("up_gate" if n == 0 else "up_val"), 2 * j - 2)
                        project(pe, ps[:, m, :], m, hhi, hlo).then_inc(w_used, 1)

            for k in range(DT):
                pe.wait_ge(s("h2_lo"), k + 1)
                for m in range(3):
                    if k == 0:
                        unit(U_UP + m)
                    last = mm3(pe, ps[:, m, :], (tile_of(whi, m, k), tile_of(wlo, m, k)), (hhi[:, k, :], hlo[:, k, :]),
                               k == 0, k == DT - 1)
                    if k == DT - 1:
                        last.then_inc(w_used, 1)
            unit(U_UP + 3)
            project(pe, ps[:, 3, :], 3, hhi, hlo).then_inc(w_used, 1)
            with pe.Fori(1, FT // 2) as i:
                up(i)

            def down(k, slot, start=False):
                pe.wait_ge(w_lo, U_DOWN + k + 1)
                pe.wait_ge(s("f_lo"), k + 1)
                for n, m in enumerate((4, 5, 6, 7, 0, 1, 2, 3)):
                    if start and n == 4:
                        pe.wait_ge(s("up_val"), 2 * FT)
                    last = mm3(pe, ps[:, m, :], (tile_of(whi, slot, m), tile_of(wlo, slot, m)),
                               (at1(fhi, k), at1(flo, k)), start, False)
                last.then_inc(w_used, 1)

            for k in range(4):
                down(k, k, start=k == 0)
            with pe.Fori(1, (FT - 6) // 4) as i:
                for n in range(4):
                    down(4 * i + n, n)
            for k in range(FT - 6, FT - 4):
                down(k, k % SLOTS)

            def result(d):
                pe.wait_ge(s("y_t"), d + 1)
                for t in range(TT):
                    last = pe.transpose(ps[:, d, t * P:(t + 1) * P], yT[:, d, t * P:(t + 1) * P], ident[:])
                last.then_inc(s("y_ps"), 1)

            pe.wait_ge(w_lo, U_ALL)
            pe.wait_ge(s("f_lo"), FT)
            for m in range(DT):
                for k in range(FT - 4, FT):
                    last = mm3(pe, ps[:, m, :], (tile_of(whi, k % SLOTS, m), tile_of(wlo, k % SLOTS, m)),
                               (fhi[:, k, :], flo[:, k, :]), False, k == FT - 1)
                last.then_inc(s("d_ps"), 1)
                if m >= 1:
                    result(m - 1)
            pe.wait_ge(s("x3_ssq"), DT)
            for t in range(TT):
                last = pe.matmul(ps[:, 7, t:t + 1], work[:, 2, t * P:(t + 1) * P], ones[:, 0:1], start=True, stop=True)
            last.then_inc(s("x3stat_ps"), 1)
            pe.wait_ge(s("x3_rms"), 1)
            result(DT - 1)


_SHARED = ["x", "c", "ctx", "c_ctx", "w_ada", "b_ada", "norm1_g", "w_in", "q_norm_g", "kv_norm_g", "w_uq", "w_ukv",
           "conv_w", "conv_b", "w_attn_out", "w_conv_out", "w_o", "norm2_g", "w_up", "ffn_conv_w", "ffn_conv_b",
           "w_down", "final_g"]


def rope_table():
    t = np.arange(T)
    axis = ROPE // 2
    inv = np.float32(THETA) ** (-np.arange(0, axis, 2, dtype=np.float32) / np.float32(axis))
    table = np.zeros((2, 2, 2, axis // 2, T), np.float32)
    for a, at in enumerate((t // GRID_W, t % GRID_W)):
        ang = (inv[:, None] * at[None, :].astype(np.float32)).astype(np.float32)
        table[0, a] = np.cos(ang)
        table[1, a, 0] = -np.sin(ang)
        table[1, a, 1] = np.sin(ang)
    return table.reshape(2 * ROPE, T)


def kernel(**inputs):
    import concourse.bacc as bacc
    from concourse.bass_utils import run_bass_kernel_spmd

    nc = bacc.Bacc("TRN2", target_bir_lowering=False, num_devices=1)
    arrays, args = {}, []
    for name in _SHARED:
        a = np.ascontiguousarray(inputs[name])
        if name in ("x", "ctx") or (a.ndim > 1 and name != "c"):
            a = a.reshape(a.shape[1:])
        arrays[name + "_dram"] = a
    arrays["rope_dram"] = rope_table()
    for name, a in arrays.items():
        args.append(nc.dram_tensor(name, a.shape, mybir.dt.from_np(a.dtype), kind="ExternalInput").ap())
    args.append(nc.dram_tensor("out_dram", (T, D), F32, kind="ExternalOutput").ap())
    build(nc, *args)
    r = run_bass_kernel_spmd(nc, [arrays], core_ids=[0])
    return r.results[0]["out_dram"].reshape(1, T, D)
```

```python
from contextlib import ExitStack

import numpy as np

import concourse.bass as bass
from concourse import mybir

F32 = mybir.dt.float32
F32R = mybir.dt.float32r
ACT = mybir.ActivationFunctionType
ALU = mybir.AluOpType
AX = mybir.AxisListType

P = 128
D = 1024
T = 512
C = 256
K = T + C
GRID_W = 64
HEADS = 8
NOPE, ROPE, VDIM = 64, 32, 64
QK = NOPE + ROPE
QR, KVR = 384, 256
CONV = 512
FF = 2816
EPS = 1e-6
THETA = 10000.0
KV_END = KVR
KR_END = KV_END + ROPE
Q_END = KR_END + QR
CX_END = Q_END + CONV
CB_END = CX_END + CONV
CC_END = CB_END + CONV
GA_END = CC_END + D
DT = D // P
QT, KVT, CT, FT = QR // P, KVR // P, CONV // P, FF // P
TT, CTT, KT = T // P, C // P, K // P
SCALE = float(QK) ** -0.5
HALVES = ((0, T // 2), (T // 2, T))
SLOTS = 4
UNIT = 1024
BANK = 512

R_C, R_CC, R_BADA, R_N1, R_N2, R_FG = 0, 8, 16, 64, 72, 80
R_QG = 88
R_KVG = R_QG + QT
R_CB = R_KVG + KVT
R_CW = R_CB + CT
R_END0 = R_CW + 3 * CT
R_FW = P
R_FB = R_FW + 6 * FT
R_END = R_FB + 2 * FT

U_ADA = 0
U_Q = U_ADA + 2 * DT
U_KV = U_Q + QT
U_KR = U_KV + KVT
U_UQ = U_KR + 1
U_V = U_UQ + HEADS // 2
U_N = U_V + 1
U_CONV = U_N + 1
U_MERGE = U_CONV + 3 * CT
U_O = U_MERGE + 3 * DT
U_UP = U_O + DT
U_DOWN = U_UP + 2 * FT
U_ALL = U_DOWN + FT
Y_ACT, Y_DVE = (1, 4, 6), (0, 2, 3, 5, 7)
CONV_SPLITS = (9, 13, 17, 21)


def build(nc, x, c, ctx, c_ctx, w_ada, b_ada, norm1_g, w_in, q_norm_g, kv_norm_g, w_uq, w_ukv, conv_w,
          conv_b, w_attn_out, w_conv_out, w_o, norm2_g, w_up, ffn_conv_w, ffn_conv_b, w_down, final_g,
          rope_tab, out):
    stack = ExitStack()
    with stack:
        def sem(name):
            return stack.enter_context(nc.semaphore(name))

        def sb(name, shape, dt=F32, scope=stack):
            return scope.enter_context(nc.sbuf_tensor(name, shape, dt))

        raw = sb("raw", [P, SLOTS, UNIT])
        whi = sb("whi", [P, SLOTS, UNIT], F32R)
        wlo = sb("wlo", [P, SLOTS, UNIT], F32R)
        hhi = sb("hhi", [P, DT, T], F32R)
        hlo = sb("hlo", [P, DT, T], F32R)
        work = sb("work", [P, 6, T])
        tab = sb("tab", [P, T])
        ident = sb("ident", [P, P])
        ones = sb("ones", [P, P])
        eps = sb("eps", [P, 1])
        prm = sb("prm", [P, R_END])
        mod = sb("mod", [P, 6 * DT])
        modc = sb("modc", [P, 2 * DT])
        gain = sb("gain", [P, 3, DT])
        cvec = sb("cvec", [P, DT, 2])
        small = sb("small", [P, 32])

        early = ExitStack()
        xt = sb("xt", [P, KT, D], scope=early)
        rows1 = sb("rows1", [4, 2 * D], scope=early)
        chl = sb("chl", [P, DT, P], F32R, scope=early)
        sb("gap0", [P, 3584], scope=early)
        chi = sb("chi", [P, DT, C], F32R, scope=early)
        clo = sb("clo", [P, DT, C], F32R, scope=early)
        xnT = sb("xnT", [P, DT, K], scope=early)
        ht = sb("ht", [P, 2, K], scope=early)
        early.close()
        att = ExitStack()
        qhi = sb("qhi", [P, HEADS, T], F32R, scope=att)
        qlo = sb("qlo", [P, HEADS, T], F32R, scope=att)
        cq = ExitStack()
        cqhi = sb("cqhi", [P, QT, T], F32R, scope=cq)
        cqlo = sb("cqlo", [P, QT, T], F32R, scope=cq)
        krot = sb("krot", [P, K], scope=cq)
        krot2 = sb("krot2", [P, T], scope=cq)
        qtmp = sb("qtmp", [P, T], scope=cq)
        cq.close()
        pthi = sb("pthi", [P, KT, T], F32R, scope=att)
        ptlo = sb("ptlo", [P, KT, T], F32R, scope=att)
        ckhi = sb("ckhi", [P, KVT, K], F32R, scope=att)
        cklo = sb("cklo", [P, KVT, K], F32R, scope=att)
        khi = sb("khi", [P, 2, K], F32R, scope=att)
        klo = sb("klo", [P, 2, K], F32R, scope=att)
        vs = sb("vs", [P, KT, HEADS, 2 * VDIM], F32R, scope=att)
        pr = ExitStack()
        ckraw = sb("ckraw", [P, KVT, K], scope=pr)
        pr.close()
        prob = sb("prob", [P, 2, K], scope=att)
        att.close()
        mrg = ExitStack()
        sb("gap1", [P, 2 * HEADS * T], scope=mrg)
        zhi = sb("zhi", [P, CT, T], F32R, scope=mrg)
        zlo = sb("zlo", [P, CT, T], F32R, scope=mrg)
        mhi = sb("mhi", [P, DT, T], F32R, scope=mrg)
        mlo = sb("mlo", [P, DT, T], F32R, scope=mrg)
        ada2 = sb("ada2", [P, 2, D], scope=mrg)
        sb("gap2", [P, 1536], scope=mrg)
        x2 = ExitStack()
        x2T = sb("x2T", [P, DT, T], scope=x2)
        x2.close()
        adacc = sb("adacc", [P, 4 * D], scope=mrg)
        mrg.close()
        res = ExitStack()
        rows2 = sb("rows2", [1, 4 * D], scope=res)
        sb("gap3", [P, 4096], scope=res)
        xtok = sb("xtok", [P, TT, D], scope=res)
        res.close()
        ffn = ExitStack()
        fhi = sb("fhi", [P, FT, T], F32R, scope=ffn)
        flo = sb("flo", [P, FT, T], F32R, scope=ffn)
        ffn.close()
        fin = ExitStack()
        yo = sb("yo", [P, TT, D], scope=fin)
        yT = sb("yT", [P, DT, T], scope=fin)
        fin.close()

        ps = stack.enter_context(nc.psum_tensor("ps", [P, 8, BANK], F32))

        def wide(bank):
            return ps[:, bank:bank + 2, :].rearrange("p b n -> p (b n)")[:, 0:K]

        raw_loaded = [sem(f"raw_loaded{s}") for s in range(SLOTS)]
        w_hi, w_lo, w_used = sem("w_hi"), sem("w_lo"), sem("w_used")
        S = {}

        def s(name):
            if name not in S:
                S[name] = sem(name)
            return S[name]

        def wait(e, semaphore, value):
            if not (isinstance(value, int) and value <= 0):
                e.wait_ge(semaphore, value)

        def col(t, at):
            return t[:, bass.ds(at, 1)] if not isinstance(at, int) else t[:, at:at + 1]

        def at1(t, i):
            if isinstance(i, int):
                return t[:, i, :]
            return t[:, bass.ds(i, 1), :].rearrange("p a n -> p (a n)")

        def rows_of(w, k0, k1, c0, n):
            cols = w[:, c0:c0 + n] if isinstance(c0, int) else w[:, bass.ds(c0, n)]
            return cols.rearrange("(k p) n -> p k n", p=P)[:, k0:k1, :]

        def load(sp, u, slot, pieces):
            wait(sp, w_lo, u - SLOTS + 1)
            if not isinstance(u, int):
                sp.sem_inc(s("load_turn"), 1)
            for dst, src in pieces:
                sp.dma_start(dst, src).then_inc(raw_loaded[slot], 16)

        def column_tile(slot, w, c0, kt=DT):
            view = raw[:, slot, 0:kt * P].rearrange("p (k n) -> p k n", n=P)
            h = kt // 2
            return [(view[:, 0:h, :], rows_of(w, 0, h, c0, P)), (view[:, h:kt, :], rows_of(w, h, kt, c0, P))]

        def merge_tile(slot, d):
            view = raw[:, slot, :].rearrange("p (k n) -> p k n", n=P)
            return [(view[:, 0:CT, :], rows_of(w_attn_out, 0, CT, d * P, P)),
                    (view[:, CT:2 * CT, :], rows_of(w_conv_out, 0, CT, d * P, P))]

        def down_tile(slot, k):
            r = w_down[k * P:(k + 1) * P, :] if isinstance(k, int) else w_down[bass.ds(k * P, P), :]
            return [(raw[:, slot, 0:512], r[:, 0:512]), (raw[:, slot, 512:1024], r[:, 512:1024])]

        def arrived(e, u, slot):
            e.wait_ge(raw_loaded[slot], 32 * ((u - slot) // SLOTS + 1) if isinstance(u, int) else (u - slot) * 8 + 32)

        def plain(t, slot, n=UNIT):
            return [t[:, slot, 0:n]]

        def headed_raw(slot, g):
            v = raw[:, slot, 0:g * QK].rearrange("p (g n) -> p g n", n=QK)
            r = v[:, :, NOPE:QK].rearrange("p g (a h j) -> p g a h j", a=2, h=2)
            return [v, r[:, :, :, 1, :], r[:, :, :, 0, :]]

        def headed(t, slot, g):
            v = t[:, slot, 0:g * P].rearrange("p (g n) -> p g n", n=P)
            r = v[:, :, QK:P].rearrange("p g (a h j) -> p g a h j", a=2, h=2)
            return [v[:, :, 0:QK], r[:, :, :, 0, :], r[:, :, :, 1, :]]

        def views(u, slot):
            if isinstance(u, int) and u == U_KR:
                return headed_raw(slot, DT), headed(whi, slot, DT), headed(wlo, slot, DT)
            if isinstance(u, int) and U_UQ <= u < U_UQ + 4:
                return headed_raw(slot, 2 * QT), headed(whi, slot, 2 * QT), headed(wlo, slot, 2 * QT)
            return plain(raw, slot), plain(whi, slot), plain(wlo, slot)

        def split_hi(act, u, slot):
            arrived(act, u, slot)
            wait(act, w_used, u - SLOTS + 1)
            rv, hv, _ = views(u, slot)
            for n, (r, h) in enumerate(zip(rv, hv)):
                ins = nc.scalar.activation(h, r, ACT.Copy)
            ins.then_inc(w_hi, 1)

        def split_lo(e, u, slot, engine=None):
            e.wait_ge(w_hi, u + 1)
            rv, hv, lv = views(u, slot)
            for r, h, l in zip(rv, hv, lv):
                ins = (engine or nc.gpsimd).tensor_tensor(out=l, in0=r, in1=h.bitcast(F32), op=ALU.subtract)
            ins.then_inc(w_lo, 1)

        def used(e, u):
            e.wait_ge(w_used, u + 1)

        def query_ready(e, h):
            if h % 2 == 0:
                e.wait_ge(s("q_ps"), h // 2 + 1)
            else:
                used(e, U_UQ + h // 2)

        def keys_ready(e, pair, part):
            if (pair, part) == (HEADS // 2 - 1, 1):
                used(e, U_N)
            else:
                e.wait_ge(s("k_ps"), 2 * pair + part + 1)

        flat = work[:].rearrange("p a n -> p (a n)")
        sqk = [flat[:, m * K:(m + 1) * K] for m in range(2)]

        def qval(h):
            return (work[:, 3, :], qtmp[:])[h % 2]

        def probs(g):
            if g % 3 < 2:
                return prob[:, g % 3, :]
            return flat[:, 2 * T:2 * T + K]

        kraw = flat[:, 2 * T + K:2 * T + 2 * K]

        def neg_max(g):
            return small[:, 14 + g % 4:15 + g % 4]

        def exp_sum(g, n=1):
            return small[:, 18 + g % 8:18 + g % 8 + n]

        inv_sum = small[:, 8:8 + TT]
        q_rms = small[:, 4:4 + TT]
        q_scale = small[:, 26:26 + TT]

        def neg_bias(g):
            return small[:, g % 4:g % 4 + 1]

        diag = work[:, 5, :]

        G = flat[:, 0:4 * P].rearrange("p (g n) -> p g n", n=P)

        def tile_of(t, slot, k, n=P):
            return t[:, slot, k * n:(k + 1) * n]

        def mm3(pe, o, l, r, start, stop):
            pe.matmul(o, l[0], r[0], start=start, stop=False)
            pe.matmul(o, l[0], r[1], start=False, stop=False)
            return pe.matmul(o, l[1], r[0], start=False, stop=stop)

        def project(pe, o, slot, hi, lo, kt=DT, k0=0, start=True, stop=True):
            for k in range(kt):
                last = mm3(pe, o, (tile_of(whi, slot, k0 + k), tile_of(wlo, slot, k0 + k)),
                           (hi[:, k, :], lo[:, k, :]), start and k == 0, stop and k == kt - 1)
            return last

        def x3_add(dve, d):
            dve.wait_ge(s("x3_sq"), d + 1)
            if d == 0:
                nc.vector.tensor_copy(work[:, 2, :], work[:, 0, :]).then_inc(s("x3_ssq"), 1)
            else:
                dve.wait_ge(s("x3_ssq"), d)
                nc.vector.tensor_tensor(out=work[:, 2, :], in0=work[:, 2, :], in1=work[:, d % 2, :], op=ALU.add).then_inc(s("x3_ssq"), 1)

        block = stack.enter_context(nc.Block())

        @block.sync
        def _(sp):
            def rows_to(g, r0, a, n):
                sp.dma_start(G[r0:r0 + n, g, :], a).then_inc(s("prm_loaded" if g == 0 else "prm_ffn_loaded"), 16)

            fw = ffn_conv_w.rearrange("k (r n) -> (k r) n", n=P)
            small_loads = [
                (0, R_BADA - 16, b_ada.rearrange("(r n) -> r n", n=P), 48),
                (0, R_N1 - 16, norm1_g.rearrange("(r n) -> r n", n=P), DT),
                (0, R_N2 - 16, norm2_g.rearrange("(r n) -> r n", n=P), DT),
                (0, R_FG - 16, final_g.rearrange("(r n) -> r n", n=P), DT),
                (0, R_QG - 16, q_norm_g.rearrange("(r n) -> r n", n=P), QT),
                (0, R_KVG - 16, kv_norm_g.rearrange("(r n) -> r n", n=P), KVT),
                (0, R_CB - 16, conv_b.rearrange("(r n) -> r n", n=P), CT),
                (0, R_CW - 16, conv_w.rearrange("k (r n) -> (k r) n", n=P), 3 * CT),
                (1, 0, fw[0:P, :], P),
                (2, 0, fw[P:6 * FT, :], 6 * FT - P),
                (2, 6 * FT - P, ffn_conv_b.rearrange("(r n) -> r n", n=P), 2 * FT)]
            for u in range(U_ADA, U_Q):
                k, at = (u - U_ADA) // 2, (u - U_ADA) % 2 * D
                load(sp, u, u % SLOTS, [(raw[:, u % SLOTS, n:n + 512], w_ada[k * P:(k + 1) * P, at + n:at + n + 512])
                                        for n in (0, 512)])
                if u % 2 == 1 and u // 2 < KT:
                    t = u // 2
                    rows = x[t * P:(t + 1) * P, :] if t < TT else ctx[(t - TT) * P:(t - TT + 1) * P, :]
                    sp.dma_start(xt[:, t, :], rows).then_inc(s(f"x_loaded{t}"), 16)
                if u >= 5:
                    rows_to(*small_loads[u - 5])
            sp.dma_start(tab[64:P, :], rope_tab).then_inc(s("tab_loaded"), 16)
            for m in range(QT):
                u = U_Q + m
                load(sp, u, u % SLOTS, column_tile(u % SLOTS, w_in, KR_END + m * P))
            for m in range(KVT):
                u = U_KV + m
                load(sp, u, u % SLOTS, column_tile(u % SLOTS, w_in, m * P))
            kr = raw[:, U_KR % SLOTS, 0:DT * QK].rearrange("p (k n) -> p k n", n=QK)
            load(sp, U_KR, U_KR % SLOTS, [(kr[:, k:k + 4, :], rows_of(w_in, k, k + 4, KR_END - QK, QK)) for k in (0, 4)])
            for m in range(4):
                slot = (U_UQ + m) % SLOTS
                view = raw[:, slot, 0:2 * QT * QK].rearrange("p (k h n) -> p k h n", k=QT, n=QK)
                load(sp, U_UQ + m, slot, [(view[:, :, h, :], rows_of(w_uq, 0, QT, (2 * m + h) * QK, QK)) for h in (0, 1)])
            ukv = w_ukv.rearrange("(k p) (h n) -> p k h n", p=P, n=NOPE + VDIM)
            slot = U_V % SLOTS
            load(sp, U_V, slot, [(raw[:, slot, k * 512:(k + 1) * 512].rearrange("p (h n) -> p h n", n=VDIM),
                                  ukv[:, k, :, NOPE:]) for k in range(KVT)])
            slot = U_N % SLOTS
            load(sp, U_N, slot, [(raw[:, slot, k * 512:(k + 1) * 512].rearrange("p (h n) -> p h n", n=NOPE),
                                  ukv[:, k, :, 0:NOPE]) for k in range(KVT)])

            def load_ada2(n, k, g):
                wait(sp, s("ada2_used"), n - 1)
                if not isinstance(n, int):
                    sp.sem_inc(s("load_turn"), 1)
                rows = w_ada[k * P:(k + 1) * P, :] if isinstance(k, int) else w_ada[bass.ds(k * P, P), :]
                sp.dma_start(ada2[:, g % 2, :], rows[:, (2 + g) * D:(3 + g) * D]).then_inc(s(f"ada2_loaded{g % 2}"), 16)

            for j in range(CT):
                for n, end in enumerate((Q_END, CB_END, CX_END)):
                    u = U_CONV + 3 * j + n
                    load(sp, u, u % SLOTS, column_tile(u % SLOTS, w_in, end + j * P))
                    if (j, n) in ((2, 1), (3, 1)):
                        if j == 2:
                            sp.wait_ge(s("pv_ps"), 2 * HEADS)
                        for m in range(2):
                            load_ada2(2 * (j - 2) + m, 0, 2 * (j - 2) + m)

            def merge_loads(i):
                for n in range(12):
                    dd, what = n // 3, n % 3
                    d = 4 * i + dd
                    u = U_MERGE + 12 * i + n
                    slot = n % SLOTS
                    load(sp, u, slot, merge_tile(slot, d) if what == 2 else
                         column_tile(slot, w_in, (CC_END, GA_END)[what] + d * P))
                    load_ada2(4 + 12 * i + n, 1 + 3 * i + n // 4, n % 4)

            with sp.Fori(0, 2) as i:
                merge_loads(i)
            for d in range(SLOTS):
                load(sp, U_O + d, d, column_tile(d, w_o, d * P))
                load_ada2(4 * (DT - 1) + d, DT - 1, d)
            for d in range(SLOTS, DT):
                if d == DT - 1:
                    used(sp, U_O - 1)
                    for t in range(TT):
                        sp.dma_start(xtok[:, t, :], x[t * P:(t + 1) * P, :]).then_inc(s("xtok_loaded"), 16)
                load(sp, U_O + d, d - SLOTS, column_tile(d - SLOTS, w_o, d * P))
            with sp.Fori(0, FT // 2) as i:
                for n in range(4):
                    load(sp, U_UP + 4 * i + n, n, column_tile(n, w_up, (n % 2) * FF + (2 * i + n // 2) * P))
            with sp.Fori(0, FT // 4) as i:
                for n in range(4):
                    load(sp, U_DOWN + 4 * i + n, n, down_tile(n, 4 * i + n))
            for k in range(FT // 4 * 4, FT):
                load(sp, U_DOWN + k, k % 4, down_tile(k % 4, k))
            out_v = out.rearrange("(t p) d -> p t d", p=P)
            for n in range(DT // 2):
                lo, hi = 2 * n * P, 2 * (n + 1) * P
                sp.wait_ge(s("y_act"), TT * sum(d < 2 * n + 2 for d in Y_ACT))
                sp.wait_ge(s("y_dve"), sum(d < 2 * n + 2 for d in Y_DVE))
                sp.dma_start(out_v[:, :, lo:hi], yo[:, :, lo:hi]).then_inc(s("stored"), 16)
            sp.wait_ge(s("stored"), 16 * (DT // 2))

        @block.gpsimd
        def _(pool):
            nc.gpsimd.memset(ident[:], 0.0).then_inc(s("consts"), 1)
            nc.gpsimd.memset(ones[:], 1.0).then_inc(s("consts"), 1)
            nc.gpsimd.memset(eps[:], EPS).then_inc(s("consts"), 1)
            pool.wait_ge(s("consts"), 3)
            nc.gpsimd.affine_select(out=ident[:], in_=ident[:], compare_op=ALU.not_equal, fill=1.0, base=0,
                                    pattern=[[-1, P]], channel_multiplier=1).then_inc(s("consts"), 1)
            nc.gpsimd.memset(chl[:].bitcast(F32), 0.0).then_inc(s("chl_zero"), 1)
            pool.wait_ge(w_lo, U_Q + 1)
            split_lo(pool, U_Q + 1, (U_Q + 1) % SLOTS)
            pool.wait_ge(s("mods1"), 8)
            for n in range(2 * DT):
                k, (lo, hi, g, m) = n % DT, ((0, T, 0, mod), (T, K, 1, modc))[n // DT]
                wait(pool, s("h_lo"), n - 1)
                nc.gpsimd.tensor_scalar(ht[:, n % 2, lo:hi], xnT[:, k, lo:hi], gain[:, g, k:k + 1],
                                        m[:, k:k + 1], ALU.mult, ALU.add).then_inc(s("h_t"), 1)
                if n in (7, 11):
                    split_lo(pool, U_Q + 2 + (7, 11).index(n), (U_Q + 2 + (7, 11).index(n)) % SLOTS)
            for u in range(U_Q + 4, U_V):
                split_lo(pool, u, u % SLOTS)
            for h in range(HEADS):
                pool.wait_ge(s("q_hi"), h + 1)
                nc.gpsimd.tensor_tensor(out=qlo[0:QK, h, :], in0=qval(h)[0:QK, :], in1=qhi[0:QK, h, :].bitcast(F32),
                                        op=ALU.subtract).then_inc(s("q_lo"), 1)
                if h in (1, 3):
                    split_lo(pool, U_V + h // 2, (U_V + h // 2) % SLOTS)
            pool.wait_ge(s("q_lo"), HEADS)

            def keys_split(h):
                pool.wait_ge(s("k_raw"), h // 2 * 2 + 2)
                wait(pool, s("s_ps"), TT * (h - 1))
                src = kraw[h % 2 * NOPE:(h % 2 + 1) * NOPE, :]
                if h > 0:
                    nc.gpsimd.tensor_scalar(khi[0:NOPE, h % 2, :], src, 1.0, None, ALU.mult).then_inc(s("k_hi"), 1)
                if h % 2 == 0:
                    pool.wait_ge(s("k_hi"), h + 1)
                    nc.gpsimd.tensor_tensor(out=klo[0:NOPE, 0, :], in0=src, in1=khi[0:NOPE, 0, :].bitcast(F32),
                                            op=ALU.subtract).then_inc(s("k_lo_even"), 1)

            def diagonals(h):
                pool.wait_ge(s("rsum"), h + 1)
                wait(pool, s("r_ps"), h)
                nc.gpsimd.tensor_tensor(out=diag.rearrange("p (t n) -> p t n", n=P), in0=ident[:].unsqueeze(1).to_broadcast([P, TT, P]),
                                        in1=inv_sum.unsqueeze(2).to_broadcast([P, TT, P]), op=ALU.mult).then_inc(s("diag"), 1)

            def output_lo(h):
                r = slice((h % 2) * VDIM, (h % 2 + 1) * VDIM)
                pool.wait_ge(s("o_hi"), h + 1)
                nc.gpsimd.tensor_tensor(out=qlo[r, h // 2 * 2, :], in0=work[r, 1, :], in1=qhi[r, h // 2 * 2, :].bitcast(F32),
                                        op=ALU.subtract).then_inc(s("o_lo"), 1)

            keys_split(0)
            pool.wait_ge(s("k_lo_even"), 1)
            keys_split(1)
            pool.wait_ge(s("k_hi"), 2)
            for h in range(HEADS):
                diagonals(h)
                pool.wait_ge(s("diag"), h + 1)
                if h + 2 < HEADS:
                    keys_split(h + 2)
                    if h % 2 == 1:
                        pool.wait_ge(s("k_hi"), h + 3)
                    else:
                        pool.wait_ge(s("k_lo_even"), h // 2 + 2)
                if h >= 1:
                    output_lo(h - 1)
                    pool.wait_ge(s("o_lo"), h)
                if 2 <= h < 6:
                    split_lo(pool, U_CONV + h - 2, h - 2)
                    pool.wait_ge(w_lo, U_CONV + h - 1)
            output_lo(HEADS - 1)
            pool.wait_ge(s("o_lo"), HEADS)
            for u in range(U_CONV + 4, U_MERGE):
                split_lo(pool, u, u % SLOTS)
            with pool.Fori(0, (U_DOWN - U_MERGE) // 4) as i:
                for n in range(4):
                    split_lo(pool, U_MERGE + 4 * i + n, n)
            with pool.Fori(0, FT // 4) as i:
                for n in range(4):
                    split_lo(pool, U_DOWN + 4 * i + n, n)
            for k in range(FT // 4 * 4, FT):
                split_lo(pool, U_DOWN + k, k % 4)

        @block.scalar
        def _(act):
            for n, v in enumerate((c.rearrange("a (r n) -> (a r) n", n=P), c_ctx.rearrange("(r n) -> r n", n=P))):
                act.dma_start(G[n * DT:(n + 1) * DT, 3, :], v).then_inc(s("c_loaded"), 16)
            act.wait_ge(s("consts"), 4)
            nc.scalar.activation(small[:, 30:31], eps[:, 0:1], ACT.Silu).then_inc(s("table"), 1)
            act.wait_ge(s("c_ps"), 1)
            nc.scalar.activation(cvec[:].rearrange("p k s -> p s k"), ps[:, 7, 0:2 * DT].rearrange("p (s k) -> p s k", k=DT),
                                 ACT.Silu).then_inc(s("cvec"), 1)
            act.wait_ge(s("cvec"), 1)
            act.wait_ge(s("chl_zero"), 1)
            nc.scalar.activation(chl[:, :, 0:2], cvec[:], ACT.Copy).then_inc(s("chl_hi"), 1)

            def xT_copy(t):
                act.wait_ge(s("xT_ps"), t + 1)
                nc.scalar.activation(xnT[:, 4:8, t * P:(t + 1) * P], ps[:, 5 + 2 * (t % 2), :]
                                     .rearrange("p (k n) -> p k n", n=P), ACT.Copy).then_inc(s("xT_act"), 1)

            for u in range(U_ADA, U_Q):
                split_hi(act, u, u % SLOTS)
                if u % 2 == 1 and u // 2 < KT:
                    t = u // 2
                    act.wait_ge(s(f"x_loaded{t}"), 16)
                    wait(act, s("x_ssq"), t)
                    nc.scalar.activation(ht[:].rearrange("p a n -> p (a n)")[:, 0:D], xt[:, t, :], ACT.Square,
                                         accum_out=small[:, t:t + 1]).then_inc(s("x_ssq"), 1)
                    act.wait_ge(s("x_ssq"), t + 1)
                    nc.scalar.activation(small[:, 8 + t:9 + t], small[:, t:t + 1], ACT.Sqrt, bias=eps[:, 0:1],
                                         scale=1.0 / D).then_inc(s("x_rms"), 1)
                if u % 2 == 1 and 1 <= u // 2 <= KT:
                    xT_copy(u // 2 - 1)
            split_hi(act, U_Q, U_Q % SLOTS)
            split_hi(act, U_Q + 1, (U_Q + 1) % SLOTS)
            used(act, U_Q - 1)
            nc.scalar.activation(rows1[:, 0:D], ps[0:4, 0:2, :].rearrange("p b n -> p (b n)"), ACT.Copy).then_inc(s("rows1_act"), 1)
            split_hi(act, U_Q + 2, (U_Q + 2) % SLOTS)
            act.wait_ge(s("mods1"), 8)
            for n in range(2 * DT):
                k, (lo, hi, to, g, m) = n % DT, ((0, T, hhi, 0, mod), (T, K, chi, 1, modc))[n // DT]
                nc.scalar.activation(to[:, k, :], xnT[:, k, lo:hi], ACT.Identity, bias=m[:, k:k + 1],
                                     scale=gain[:, g, k:k + 1]).then_inc(s("h_hi"), 1)
                if n == DT - 1:
                    split_hi(act, U_KV, U_KV % SLOTS)

            def keys_raw(pair, part):
                lo, hi = ((0, T), (T, K))[part]
                keys_ready(act, pair, part)
                wait(act, s("k_lo_even"), pair)
                wait(act, s("k_lo_odd"), pair)
                nc.scalar.activation(kraw[:, lo:hi], ps[:, 6, 0:hi - lo], ACT.Copy).then_inc(s("k_raw"), 1)

            for m in range(QT):
                used(act, U_Q + m)
                nc.scalar.activation(work[:, 3 + m, :], ps[:, m, :], ACT.Square).then_inc(s("p_sq"), 1)
                nc.scalar.activation(cqhi[:, m, :], ps[:, m, :], ACT.Copy, scale=prm[:, R_QG + m:R_QG + m + 1]).then_inc(s("cq_hi"), 1)
                split_hi(act, U_KV + 1 + m, (U_KV + 1 + m) % SLOTS)
            act.wait_ge(s("qstat_ps"), 1)
            nc.scalar.activation(q_rms, ps[:, 3, 0:TT], ACT.Sqrt, bias=eps[:, 0:1], scale=1.0 / QR).then_inc(s("q_rms"), 1)
            for m in range(KVT):
                used(act, U_KV + m)
                nc.scalar.activation(sqk[m], wide(4 + 2 * m), ACT.Square).then_inc(s("p_sq"), 1)
                nc.scalar.activation(ckraw[:, m, :], wide(4 + 2 * m), ACT.Copy).then_inc(s("p_raw"), 1)
                split_hi(act, U_UQ + 1 + m, (U_UQ + 1 + m) % SLOTS)
            act.wait_ge(s("kstat_ps"), 1)
            nc.scalar.activation(sqk[1], wide(2), ACT.Sqrt, bias=eps[:, 0:1], scale=1.0 / KVR).then_inc(s("k_rms"), 1)
            nc.scalar.activation(small[:, 31:32], eps[:, 0:1], ACT.Exp).then_inc(s("table"), 1)
            split_hi(act, U_UQ + 3, (U_UQ + 3) % SLOTS)
            for h in range(HEADS):
                query_ready(act, h)
                wait(act, s("q_lo"), h - 1)
                nc.scalar.activation(qval(h)[0:NOPE, :], ps[0:NOPE, 4 + h % 4, :], ACT.Copy).then_inc(s("q_nope"), 1)
                act.wait_ge(s("q_rope"), 3 * h + 3)
                act.wait_ge(s("q_nope"), h + 1)
                nc.scalar.activation(qhi[0:QK, h, :], qval(h)[0:QK, :], ACT.Copy).then_inc(s("q_hi"), 1)
                if h in (1, 3):
                    split_hi(act, U_V + h // 2, (U_V + h // 2) % SLOTS)
                if h == 1:
                    for m in range(KVT):
                        act.wait_ge(s("ck_t"), m + 1)
                        nc.scalar.activation(ckhi[:, m, :], ckraw[:, m, :], ACT.Copy).then_inc(s("ck_hi"), 1)
            act.wait_ge(s("q_lo"), HEADS - 1)
            for kt in range(KT):
                if kt in (2, 3):
                    keys_raw(0, kt - 2)
                if kt == 3:
                    act.wait_ge(s("k_raw"), 2)
                    nc.scalar.activation(khi[0:NOPE, 0, :], kraw[0:NOPE, :], ACT.Copy).then_inc(s("k_hi"), 1)
                if kt < KT - 1:
                    act.wait_ge(s("v_ps"), kt + 1)
                else:
                    used(act, U_V)
                nc.scalar.activation(vs[:, kt, :, 0:VDIM], ps[:, kt % 4, :].rearrange("p (h n) -> p h n", n=VDIM),
                                     ACT.Copy).then_inc(s("v_hi"), 1)

            def exps(g):
                act.wait_ge(s("nbias"), g + 1)
                wait(act, s("t_ps"), g - 2)
                nc.scalar.activation(probs(g), wide(2 * (g % 2)), ACT.Exp, bias=neg_bias(g), scale=q_scale[:, g % TT:g % TT + 1],
                                     accum_out=exp_sum(g)).then_inc(s("p_exp"), 1)

            def output_part(h):
                r = slice((h % 2) * VDIM, (h % 2 + 1) * VDIM)
                act.wait_ge(s("pv_ps"), 2 * h + 2)
                wait(act, s("o_sum"), h)
                nc.scalar.activation(work[r, 0, :], ps[VDIM:P, 7, :], ACT.Copy).then_inc(s("o_part"), 1)

            def output_hi(h):
                r = slice((h % 2) * VDIM, (h % 2 + 1) * VDIM)
                act.wait_ge(s("o_val"), h + 1)
                nc.scalar.activation(qhi[r, h // 2 * 2, :], work[r, 1, :], ACT.Copy).then_inc(s("o_hi"), 1)

            exps(0)
            exps(1)
            for g in range(HEADS * TT):
                h, t = g // TT, g % TT
                new_keys = t == 3 and h % 2 == 0 and h + 2 < HEADS
                if new_keys:
                    keys_raw(h // 2 + 1, 0)
                act.wait_ge(s("t_ps0"), g + 1)
                wait(act, s("pv_ps"), g // 2 - 1)
                nc.scalar.activation(pthi[:, 0:4, t * P:(t + 1) * P], ps[:, 4, :].rearrange("p (k n) -> p k n", n=P),
                                     ACT.Copy).then_inc(s("pt_hi"), 1)
                act.wait_ge(s("t_ps"), g + 1)
                nc.scalar.activation(pthi[:, 4:KT, t * P:(t + 1) * P], ps[:, 5, 0:K - 4 * P].rearrange("p (k n) -> p k n", n=P),
                                     ACT.Copy).then_inc(s("pt_hi"), 1)
                if g + 2 < HEADS * TT:
                    exps(g + 2)
                if t == 1 and h >= 1:
                    output_part(h - 1)
                if t == 2 and h >= 1:
                    output_hi(h - 1)
                if new_keys:
                    keys_raw(h // 2 + 1, 1)
                if g in CONV_SPLITS:
                    n = CONV_SPLITS.index(g)
                    split_hi(act, U_CONV + n, n)
            output_part(HEADS - 1)
            output_hi(HEADS - 1)

            for j in range(CT):
                cx, y = work[:, 3 * (j % 2), :], work[:, 3 * (j % 2) + 2, :]
                used(act, U_CONV + 3 * j)
                wait(act, s("z_lo"), j - 1)
                if j == 0:
                    act.wait_ge(s("o_lo"), HEADS)
                nc.scalar.activation(cx, ps[:, 3 * (j % 2), :], ACT.Copy).then_inc(s("c_x"), 1)
                split_hi(act, U_CONV + 3 * j + 4, (3 * j + 4) % SLOTS)
                act.wait_ge(s("c_prod"), j + 1)
                nc.scalar.activation(y, work[:, 3 * (j % 2) + 1, :], ACT.Identity, bias=prm[:, R_CB + j:R_CB + j + 1],
                                     scale=prm[:, R_CW + CT + j:R_CW + CT + j + 1]).then_inc(s("c_mid"), 1)
                split_hi(act, U_CONV + 3 * j + 5, (3 * j + 5) % SLOTS)
                act.wait_ge(s("c_z"), j + 1)
                nc.scalar.activation(zhi[:, j, :], work[:, 3 * (j % 2), :], ACT.Copy).then_inc(s("z_hi"), 1)
                split_hi(act, U_CONV + 3 * j + 6, (3 * j + 6) % SLOTS)

            def merge_hi(i, first):
                for dd in range(4):
                    d = 4 * i + dd
                    b = 4 * (dd % 2)
                    for n in range(3):
                        m = 3 * dd + n
                        if n < 2:
                            used(act, U_MERGE + 3 * d + n)
                            if first and dd == 0:
                                act.wait_ge(s("z_lo"), CT)
                            if not (first and dd < 2):
                                act.wait_ge(s("m_lo"), d - 1)
                            nc.scalar.activation(work[:, 3 * (dd % 2) + n, :], ps[:, b + n, :], ACT.Sigmoid).then_inc(s("g_sig"), 1)
                        else:
                            act.wait_ge(s("m_sum"), d + 1)
                            nc.scalar.activation(at1(mhi, d), work[:, 3 * (dd % 2) + 2, :], ACT.Copy).then_inc(s("m_hi"), 1)
                        split_hi(act, U_MERGE + 12 * i + m + 4, m % SLOTS)

            merge_hi(0, True)
            with act.Fori(1, 2) as i:
                merge_hi(i, False)

            split_hi(act, U_O + 4, 0)
            act.wait_ge(s("rows2_ps"), 4)
            nc.scalar.activation(rows2[:, 0:2 * D], ps[0:1, 4:8, :].rearrange("p b n -> p (b n)"), ACT.Copy).then_inc(s("rows2_act"), 1)
            act.wait_ge(s("rows2_ps"), 8)
            nc.scalar.activation(small[:, 30:31], eps[:, 0:1], ACT.Sqrt).then_inc(s("table"), 1)
            for d in range(1, SLOTS):
                split_hi(act, U_O + 4 + d, d)
            def square2(d, lo, hi):
                act.wait_ge(s("x2_sum"), d + 1 + (lo > 0))
                nc.scalar.activation(work[:, d % 2, lo:hi], x2T[:, d, lo:hi], ACT.Square).then_inc(s("x2_sq"), 1)

            def rms2(n):
                lo, hi = HALVES[n]
                act.wait_ge(s("x2stat_ps"), n + 1)
                nc.scalar.activation(work[:, 3, lo:hi], ps[:, 4 + n, 0:hi - lo], ACT.Sqrt, bias=eps[:, 0:1], scale=1.0 / D).then_inc(s("x2_rms"), 1)

            for d in range(DT):
                act.wait_ge(s("xT2_ps"), d + 1)
                nc.scalar.activation(x2T[:, d, :], ps[:, 4 + d % 4, :], ACT.Copy).then_inc(s("x2_in"), 1)
                wait(act, s("x2_ssq"), d - 1)
                if d < DT - 1:
                    square2(d, 0, T)
                if SLOTS <= d < DT - 1:
                    split_hi(act, U_O + 4 + d, d % SLOTS)
            square2(DT - 1, *HALVES[0])
            rms2(0)
            for i in range(2 * DT):
                n, k = i // DT, i % DT
                lo, hi = HALVES[n]
                act.wait_ge(s("h2_t"), i + 1)
                nc.scalar.activation(hhi[:, k, lo:hi], work[:, k % 2, lo:hi], ACT.Identity,
                                     bias=mod[:, 3 * DT + k:3 * DT + k + 1]).then_inc(s("h2_hi"), 1)
                if i == 1:
                    square2(DT - 1, *HALVES[1])
                if i == 4:
                    rms2(1)
                if i == 5:
                    split_hi(act, U_UP + 3, 3)

            def up(i, first):
                for jj in range(2):
                    j = 2 * i + jj
                    for n in range(2):
                        used(act, U_UP + 2 * j + n)
                        if first and jj == 0:
                            act.wait_ge(s("h2_lo"), 2 * DT)
                        if not (first and jj < 2):
                            act.wait_ge(s("f_prod"), j - 1)
                        nc.scalar.activation(work[:, 3 * jj + n, :], ps[:, 2 * jj + n, :], ACT.Identity,
                                             bias=col(prm, R_FB + n * FT + j),
                                             scale=col(prm, R_FW + 2 * FT + n * FT + j)).then_inc(s("up_mid"), 1)
                        split_hi(act, U_UP + 4 * i + 2 * jj + n + 4, 2 * jj + n)
                    act.wait_ge(s("up_gate"), 2 * j + 2)
                    nc.scalar.activation(work[:, 3 * jj, :], work[:, 3 * jj, :], ACT.Silu).then_inc(s("up_silu"), 1)
                    act.wait_ge(s("f_prod"), j + 1)
                    nc.scalar.activation(at1(fhi, j), work[:, 3 * jj + 2, :], ACT.Copy).then_inc(s("f_hi"), 1)

            up(0, True)
            with act.Fori(1, FT // 2) as i:
                up(i, False)
            with act.Fori(0, (FT - 4) // 4) as i:
                for n in range(4):
                    split_hi(act, U_DOWN + 4 + 4 * i + n, n)
            for k in range(4 + (FT - 4) // 4 * 4, FT):
                split_hi(act, U_DOWN + k, k % 4)
            nc.scalar.activation(small[:, 31:32], eps[:, 0:1], ACT.Sqrt).then_inc(s("table"), 1)
            for d in range(DT):
                act.wait_ge(s("x3_sum"), d + 1)
                wait(act, s("x3_ssq"), d - 1)
                nc.scalar.activation(work[:, d % 2, :], x2T[:, d, :], ACT.Square).then_inc(s("x3_sq"), 1)
                nc.scalar.activation(yT[:, d, :], x2T[:, d, :], ACT.Copy, scale=prm[:, R_FG + d:R_FG + d + 1]).then_inc(s("y_t"), 1)
            act.wait_ge(s("x3stat_ps"), 1)
            nc.scalar.activation(small[:, 0:TT], ps[:, 7, 0:TT], ACT.Sqrt, bias=eps[:, 0:1], scale=1.0 / D).then_inc(s("x3_rms"), 1)
            for d in Y_ACT:
                act.wait_ge(s("x3_rinv"), 1)
                act.wait_ge(s("y_ps"), d + 1)
                for t in range(TT):
                    nc.scalar.activation(yo[:, t, d * P:(d + 1) * P], ps[:, d, t * P:(t + 1) * P], ACT.Copy,
                                         scale=small[:, 4 + t:5 + t]).then_inc(s("y_act"), 1)

        @block.vector
        def _(dve):
            dve.wait_ge(s("chl_hi"), 1)
            nc.vector.tensor_tensor(out=chl[:, :, 2:4], in0=cvec[:], in1=chl[:, :, 0:2].bitcast(F32), op=ALU.subtract).then_inc(s("chl_lo"), 1)

            def xT_copy(t):
                dve.wait_ge(s("xT_ps"), t + 1)
                nc.vector.tensor_copy(xnT[:, 0:4, t * P:(t + 1) * P], ps[:, 4 + 2 * (t % 2), :]
                                      .rearrange("p (k n) -> p k n", n=P)).then_inc(s("xT_dve"), 1)

            for u in range(U_ADA, U_Q):
                split_lo(dve, u, u % SLOTS, nc.vector)
                if u % 2 == 1 and u // 2 < KT:
                    t = u // 2
                    dve.wait_ge(s("x_rms"), t + 1)
                    nc.vector.reciprocal(small[:, 24 + t:25 + t], small[:, 8 + t:9 + t]).then_inc(s("x_rinv"), 1)
                    dve.wait_ge(s("x_rinv"), t + 1)
                    nc.vector.tensor_scalar(xt[:, t, :], xt[:, t, :], small[:, 24 + t:25 + t], None, ALU.mult).then_inc(s("x_norm"), 1)
                if u % 2 == 1 and 1 <= u // 2 <= KT:
                    xT_copy(u // 2 - 1)
            split_lo(dve, U_Q, U_Q % SLOTS, nc.vector)
            dve.wait_ge(s("prm_ps"), 1)
            nc.vector.tensor_copy(prm[:, 2 * DT:R_END0], ps[:, 7, 0:R_END0 - 2 * DT]).then_inc(s("prm"), 1)
            used(dve, U_Q - 1)
            nc.vector.tensor_copy(rows1[:, D:2 * D], ps[0:4, 2:4, :].rearrange("p b n -> p (b n)")).then_inc(s("rows1_dve"), 1)
            dve.wait_ge(s("cols1_ps"), 1)
            dve.wait_ge(s("prm"), 1)
            cols = ps[:, 4, 0:8 * DT].rearrange("p (m s) -> p s m", s=4)
            for n, m in enumerate((mod[:, 0:2 * DT], modc[:])):
                nc.vector.tensor_tensor(out=m, in0=cols[:, n, :], in1=prm[:, R_BADA:R_BADA + 2 * DT], op=ALU.add).then_inc(s("mods1"), 1)
            dve.wait_ge(s("mods1"), 2)
            for n, m in enumerate((mod[:, 0:2 * DT], modc[:])):
                nc.vector.tensor_tensor(out=m, in0=cols[:, 2 + n, :], in1=m, op=ALU.add).then_inc(s("mods1"), 1)
            dve.wait_ge(s("mods1"), 4)
            for g, m in ((0, mod), (1, modc)):
                nc.vector.scalar_tensor_tensor(out=gain[:, g, :], in0=m[:, DT:2 * DT], scalar=1.0, in1=prm[:, R_N1:R_N1 + DT],
                                               op0=ALU.add, op1=ALU.mult).then_inc(s("mods1"), 2)
            for n in range(2 * DT):
                k, (lo, hi, dst, src) = n % DT, ((0, T, hlo, hhi), (T, K, clo, chi))[n // DT]
                dve.wait_ge(s("h_t"), n + 1)
                dve.wait_ge(s("h_hi"), n + 1)
                nc.vector.tensor_tensor(out=dst[:, k, :], in0=ht[:, n % 2, lo:hi], in1=src[:, k, :].bitcast(F32),
                                        op=ALU.subtract).then_inc(s("h_lo"), 1)
            dve.wait_ge(s("prm_ffn_ps"), 1)
            nc.vector.tensor_copy(prm[:, R_FW:R_END], ps[:, 7, R_FW:R_END]).then_inc(s("prm_ffn"), 1)
            for m in range(QT):
                dve.wait_ge(s("cq_hi"), m + 1)
                nc.vector.scalar_tensor_tensor(out=cqlo[:, m, :], in0=ps[:, m, :], scalar=prm[:, R_QG + m:R_QG + m + 1],
                                               in1=cqhi[:, m, :].bitcast(F32), op0=ALU.mult, op1=ALU.subtract).then_inc(s("cq_lo"), 1)
                if m >= 1:
                    dve.wait_ge(s("p_sq"), m + 1)
                    wait(dve, s("q_sum"), m - 1)
                    nc.vector.tensor_tensor(out=work[:, 3, :], in0=work[:, 3, :], in1=work[:, 3 + m, :], op=ALU.add).then_inc(s("q_sum"), 1)
            dve.wait_ge(s("q_rms"), 1)
            nc.vector.reciprocal(q_scale, q_rms).then_inc(s("q_rinv"), 1)
            dve.wait_ge(s("q_rinv"), 1)
            nc.vector.tensor_scalar(q_scale, q_scale, SCALE, None, ALU.mult).then_inc(s("q_rinv"), 1)
            dve.wait_ge(s("p_sq"), QT + 2)
            nc.vector.tensor_tensor(out=sqk[0], in0=sqk[0], in1=sqk[1], op=ALU.add).then_inc(s("k_ssq"), 1)
            dve.wait_ge(s("k_rms"), 1)
            nc.vector.reciprocal(sqk[0], sqk[1]).then_inc(s("k_rinv"), 1)
            used(dve, U_KR)
            dve.wait_ge(s("tab_loaded"), 16)
            kr, tmp = krot[NOPE:QK, :], krot2[NOPE:QK, :]
            nc.vector.tensor_tensor(out=kr[:, 0:T], in0=ps[NOPE:QK, 0, :], in1=tab[NOPE:QK, :], op=ALU.mult).then_inc(s("kr"), 1)
            nc.vector.tensor_tensor(out=tmp, in0=ps[QK:P, 0, :], in1=tab[QK:P, :], op=ALU.mult).then_inc(s("kr"), 1)
            nc.vector.tensor_copy(kr[:, T:K], ps[NOPE:QK, 1, 0:C]).then_inc(s("kr"), 1)
            dve.wait_ge(s("kr"), 3)
            nc.vector.tensor_tensor(out=kr[:, 0:T], in0=kr[:, 0:T], in1=tmp, op=ALU.add).then_inc(s("kr"), 1)

            def rotary_key_split(b):
                dve.wait_ge(s("kr"), 4)
                nc.vector.tensor_copy(khi[NOPE:QK, b, :], kr).then_inc(s("kr"), 1)
                dve.wait_ge(s("kr"), 5 + 2 * b)
                nc.vector.tensor_tensor(out=klo[NOPE:QK, b, :], in0=kr, in1=khi[NOPE:QK, b, :].bitcast(F32),
                                        op=ALU.subtract).then_inc(s("kr"), 1)

            def value_lo(kt):
                dve.wait_ge(s("v_hi"), kt + 1)
                nc.vector.tensor_tensor(out=vs[:, kt, :, VDIM:], in0=ps[:, kt % 4, :].rearrange("p (h n) -> p h n", n=VDIM),
                                        in1=vs[:, kt, :, 0:VDIM].bitcast(F32), op=ALU.subtract).then_inc(s("v_lo"), 1)

            def keys_lo(h):
                dve.wait_ge(s("k_hi"), h + 1)
                nc.vector.tensor_tensor(out=klo[0:NOPE, 1, :], in0=kraw[NOPE:P, :], in1=khi[0:NOPE, 1, :].bitcast(F32),
                                        op=ALU.subtract).then_inc(s("k_lo_odd"), 1)

            for h in range(HEADS):
                r1, r2 = work[NOPE:QK, 4, :], work[NOPE:QK, 5, :]
                query_ready(dve, h)
                wait(dve, s("q_rope"), 3 * h)
                for n, (r, at) in enumerate(((r1, NOPE), (r2, QK))):
                    nc.vector.tensor_tensor(out=r, in0=ps[at:at + ROPE, 4 + h % 4, :], in1=tab[at:at + ROPE, :],
                                            op=ALU.mult).then_inc(s("q_rope"), 1)
                dve.wait_ge(s("q_rope"), 3 * h + 2)
                wait(dve, s("q_lo"), h - 1)
                nc.vector.tensor_tensor(out=qval(h)[NOPE:QK, :], in0=r1, in1=r2, op=ALU.add).then_inc(s("q_rope"), 1)
                if h < KVT:
                    dve.wait_ge(s("k_rinv"), 1)
                    nc.vector.scalar_tensor_tensor(out=ckraw[:, h, :], in0=ckraw[:, h, :], scalar=prm[:, R_KVG + h:R_KVG + h + 1],
                                                   in1=sqk[0], op0=ALU.mult, op1=ALU.mult).then_inc(s("ck_t"), 1)
                if h in (2, 3):
                    m = h - 2
                    dve.wait_ge(s("ck_hi"), m + 1)
                    nc.vector.tensor_tensor(out=cklo[:, m, :], in0=ckraw[:, m, :], in1=ckhi[:, m, :].bitcast(F32),
                                            op=ALU.subtract).then_inc(s("ck_lo"), 1)
            for b in range(2):
                rotary_key_split(b)
            for kt in range(KT):
                value_lo(kt)

            def maxima(g):
                dve.wait_ge(s("s_ps"), g + 1)
                wait(dve, s("p_exp"), g - 3)
                nc.vector.reduce_max(neg_max(g), wide(2 * (g % 2)), AX.X, negate=True).then_inc(s("nmax"), 1)
                dve.wait_ge(s("nmax"), g + 1)
                nc.vector.tensor_tensor(out=neg_bias(g), in0=neg_max(g), in1=q_scale[:, g % TT:g % TT + 1], op=ALU.mult).then_inc(s("nbias"), 1)

            def inverse(h):
                dve.wait_ge(s("p_exp"), TT * (h + 1))
                wait(dve, s("diag"), h)
                nc.vector.reciprocal(inv_sum, exp_sum(TT * h, TT)).then_inc(s("rsum"), 1)

            def output_value(h):
                r = slice((h % 2) * VDIM, (h % 2 + 1) * VDIM)
                dve.wait_ge(s("o_part"), h + 1)
                wait(dve, s("o_lo"), h)
                nc.vector.tensor_tensor(out=work[r, 1, :], in0=ps[0:VDIM, 7, :], in1=work[r, 0, :], op=ALU.add).then_inc(s("o_sum"), 1)
                dve.wait_ge(s("o_sum"), h + 1)
                dve.wait_ge(s("r_ps"), h + 1)
                nc.vector.tensor_tensor(out=work[r, 1, :], in0=ps[r, 6, :], in1=work[r, 1, :], op=ALU.mult).then_inc(s("o_val"), 1)

            maxima(0)
            maxima(1)
            for g in range(HEADS * TT):
                h, t = g // TT, g % TT
                if g + 2 < HEADS * TT:
                    maxima(g + 2)
                if t == 2:
                    inverse(h)
                dve.wait_ge(s("pt_hi"), 2 * g + 1)
                nc.vector.tensor_tensor(out=ptlo[:, 0:4, t * P:(t + 1) * P], in0=ps[:, 4, :].rearrange("p (k n) -> p k n", n=P),
                                        in1=pthi[:, 0:4, t * P:(t + 1) * P].bitcast(F32), op=ALU.subtract).then_inc(s("pt_lo0"), 1)
                dve.wait_ge(s("pt_hi"), 2 * g + 2)
                nc.vector.tensor_tensor(out=ptlo[:, 4:KT, t * P:(t + 1) * P],
                                        in0=ps[:, 5, 0:K - 4 * P].rearrange("p (k n) -> p k n", n=P),
                                        in1=pthi[:, 4:KT, t * P:(t + 1) * P].bitcast(F32), op=ALU.subtract).then_inc(s("pt_lo"), 1)
                if t == 0 and h % 2 == 0:
                    keys_lo(h + 1)
                if t == 1 and h >= 1:
                    output_value(h - 1)
            output_value(HEADS - 1)

            def ada2_add(n, k, g):
                gg = g * D
                if isinstance(n, int):
                    dve.wait_ge(s(f"ada2_loaded{g % 2}"), 16 * (n // 2 + 1))
                else:
                    dve.wait_ge(s(f"ada2_loaded{g % 2}"), (n - g % 2) * 8 + 16)
                cv = cvec[:, k, 0:1] if isinstance(k, int) else cvec[:, bass.ds(k, 1), 0:1].rearrange("p a b -> p (a b)")
                if isinstance(k, int) and k == 0:
                    nc.vector.tensor_scalar(adacc[:, gg:gg + D], ada2[:, g % 2, :], cv, None, ALU.mult).then_inc(s("ada2_used"), 1)
                else:
                    dve.wait_ge(s("ada2_used"), n - 3)
                    nc.vector.scalar_tensor_tensor(out=adacc[:, gg:gg + D], in0=ada2[:, g % 2, :], scalar=cv,
                                                   in1=adacc[:, gg:gg + D], op0=ALU.mult, op1=ALU.add).then_inc(s("ada2_used"), 1)

            for j in range(CT):
                b = 3 * (j % 2)
                cx, prod, y = (work[:, b + n, :] for n in range(3))
                used(dve, U_CONV + 3 * j + 1)
                dve.wait_ge(s("c_x"), j + 1)
                nc.vector.tensor_tensor(out=prod, in0=ps[:, b + 1, :], in1=cx, op=ALU.mult).then_inc(s("c_prod"), 1)
                dve.wait_ge(s("c_mid"), j + 1)
                nc.vector.scalar_tensor_tensor(out=y[:, 1:T], in0=prod[:, 0:T - 1], scalar=prm[:, R_CW + j:R_CW + j + 1],
                                               in1=y[:, 1:T], op0=ALU.mult, op1=ALU.add).then_inc(s("c_tap"), 1)
                dve.wait_ge(s("c_tap"), 2 * j + 1)
                nc.vector.scalar_tensor_tensor(out=y[:, 0:T - 1], in0=prod[:, 1:T], scalar=prm[:, R_CW + 2 * CT + j:R_CW + 2 * CT + j + 1],
                                               in1=y[:, 0:T - 1], op0=ALU.mult, op1=ALU.add).then_inc(s("c_tap"), 1)
                dve.wait_ge(s("c_tap"), 2 * j + 2)
                used(dve, U_CONV + 3 * j + 2)
                nc.vector.tensor_tensor(out=cx, in0=ps[:, b + 2, :], in1=y, op=ALU.mult).then_inc(s("c_z"), 1)
                dve.wait_ge(s("z_hi"), j + 1)
                nc.vector.tensor_tensor(out=zlo[:, j, :], in0=cx, in1=zhi[:, j, :].bitcast(F32), op=ALU.subtract).then_inc(s("z_lo"), 1)
                if j in (1, 3):
                    for m in range(4):
                        ada2_add(4 * (j // 2) + m, j // 2, m)

            def merge_lo(i, first):
                for dd in range(4):
                    d = 4 * i + dd
                    b, w = 4 * (dd % 2), 3 * (dd % 2)
                    for m in range(3):
                        nn = 3 * dd + m
                        ada2_add(8 + 12 * i + nn, 2 + 3 * i + nn // 4, nn % 4)
                    for n in range(2):
                        used(dve, U_MERGE + 3 * d + 2)
                        dve.wait_ge(s("g_sig"), 2 * d + n + 1)
                        nc.vector.tensor_tensor(out=work[:, w + n, :], in0=ps[:, b + 2 + n, :], in1=work[:, w + n, :],
                                                op=ALU.mult).then_inc(s("m_prod"), 1)
                    dve.wait_ge(s("m_prod"), 2 * d + 2)
                    if not (first and dd < 2):
                        dve.wait_ge(s("m_lo"), d - 1)
                    nc.vector.tensor_tensor(out=work[:, w + 2, :], in0=work[:, w, :], in1=work[:, w + 1, :],
                                            op=ALU.add).then_inc(s("m_sum"), 1)
                    dve.wait_ge(s("m_hi"), d + 1)
                    nc.vector.tensor_tensor(out=at1(mlo, d), in0=work[:, w + 2, :], in1=at1(mhi, d).bitcast(F32),
                                            op=ALU.subtract).then_inc(s("m_lo"), 1)

            merge_lo(0, True)
            with dve.Fori(1, 2) as i:
                merge_lo(i, False)

            dve.wait_ge(s("rows2_ps"), 8)
            nc.vector.tensor_copy(rows2[:, 2 * D:4 * D], ps[0:1, 4:8, :].rearrange("p b n -> p (b n)")).then_inc(s("rows2_dve"), 1)
            dve.wait_ge(s("cols2_ps"), 1)
            nc.vector.tensor_tensor(out=mod[:, 2 * DT:6 * DT], in0=ps[:, 7, 0:4 * DT], in1=prm[:, R_BADA + 2 * DT:R_BADA + 6 * DT],
                                    op=ALU.add).then_inc(s("mods2"), 4)
            dve.wait_ge(s("mods2"), 4)
            nc.vector.scalar_tensor_tensor(out=gain[:, 2, :], in0=mod[:, 4 * DT:5 * DT], scalar=1.0, in1=prm[:, R_N2:R_N2 + DT],
                                           op0=ALU.add, op1=ALU.mult).then_inc(s("mods2"), 1)
            def residual(d, lo, hi):
                dve.wait_ge(s("x2_in"), d + 1)
                if d == DT - 1 and lo == 0:
                    dve.wait_ge(s("last_half_ps"), 1)
                else:
                    used(dve, U_O + d)
                src = ps[:, 6, 0:hi - lo] if lo > 0 else ps[:, d % 4, lo:hi]
                nc.vector.scalar_tensor_tensor(out=x2T[:, d, lo:hi], in0=src, scalar=mod[:, 2 * DT + d:2 * DT + d + 1],
                                               in1=x2T[:, d, lo:hi], op0=ALU.mult, op1=ALU.add).then_inc(s("x2_sum"), 1)

            def squares_sum(d, lo, hi):
                dve.wait_ge(s("x2_sq"), d + 1 + (lo > 0))
                if d == 0:
                    nc.vector.tensor_copy(work[:, 2, :], work[:, 0, :]).then_inc(s("x2_ssq"), 1)
                else:
                    dve.wait_ge(s("x2_ssq"), d)
                    nc.vector.tensor_tensor(out=work[:, 2, lo:hi], in0=work[:, 2, lo:hi], in1=work[:, d % 2, lo:hi],
                                            op=ALU.add).then_inc(s("x2_ssq"), 1)

            for d in range(DT):
                if d < DT - 1:
                    residual(d, 0, T)
                    squares_sum(d, 0, T)
            residual(DT - 1, *HALVES[0])
            squares_sum(DT - 1, *HALVES[0])

            def inverse_rms2(n):
                lo, hi = HALVES[n]
                dve.wait_ge(s("x2_rms"), n + 1)
                nc.vector.reciprocal(work[:, 4, lo:hi], work[:, 3, lo:hi]).then_inc(s("x2_rinv"), 1)

            def h2_t(n, k):
                lo, hi = HALVES[n]
                if k == 0:
                    dve.wait_ge(s("x2_rinv"), n + 1)
                wait(dve, s("h2_lo"), n * DT + k - 1)
                nc.vector.scalar_tensor_tensor(out=work[:, k % 2, lo:hi], in0=x2T[:, k, lo:hi], scalar=gain[:, 2, k:k + 1],
                                               in1=work[:, 4, lo:hi], op0=ALU.mult, op1=ALU.mult).then_inc(s("h2_t"), 1)

            def h2_lo(n, k):
                lo, hi = HALVES[n]
                dve.wait_ge(s("h2_hi"), n * DT + k + 1)
                nc.vector.scalar_tensor_tensor(out=hlo[:, k, lo:hi], in0=work[:, k % 2, lo:hi], scalar=mod[:, 3 * DT + k:3 * DT + k + 1],
                                               in1=hhi[:, k, lo:hi].bitcast(F32), op0=ALU.add, op1=ALU.subtract).then_inc(s("h2_lo"), 1)

            inverse_rms2(0)
            h2_t(0, 0)
            for i in range(2 * DT):
                if i + 1 < 2 * DT:
                    h2_t((i + 1) // DT, (i + 1) % DT)
                h2_lo(i // DT, i % DT)
                if i == 0:
                    residual(DT - 1, *HALVES[1])
                if i == 1:
                    squares_sum(DT - 1, *HALVES[1])
                if i == 5:
                    inverse_rms2(1)

            def up(i, first):
                for jj in range(2):
                    j = 2 * i + jj
                    for n in range(2):
                        u, p = work[:, 3 * jj + n, :], ps[:, 2 * jj + n, :]
                        dve.wait_ge(s("up_mid"), 2 * j + n + 1)
                        nc.vector.scalar_tensor_tensor(out=u[:, 1:T], in0=p[:, 0:T - 1], scalar=col(prm, R_FW + n * FT + j),
                                                       in1=u[:, 1:T], op0=ALU.mult, op1=ALU.add).then_inc(s("up_gate" if n == 0 else "up_val"), 1)
                        dve.wait_ge(s("up_gate" if n == 0 else "up_val"), 2 * j + 1)
                        nc.vector.scalar_tensor_tensor(out=u[:, 0:T - 1], in0=p[:, 1:T], scalar=col(prm, R_FW + 4 * FT + n * FT + j),
                                                       in1=u[:, 0:T - 1], op0=ALU.mult, op1=ALU.add).then_inc(s("up_gate" if n == 0 else "up_val"), 1)
                    dve.wait_ge(s("up_val"), 2 * j + 2)
                    dve.wait_ge(s("up_silu"), j + 1)
                    if not (first and jj < 2):
                        dve.wait_ge(s("f_lo"), j - 1)
                    nc.vector.tensor_tensor(out=work[:, 3 * jj + 2, :], in0=work[:, 3 * jj, :], in1=work[:, 3 * jj + 1, :],
                                            op=ALU.mult).then_inc(s("f_prod"), 1)
                    dve.wait_ge(s("f_hi"), j + 1)
                    nc.vector.tensor_tensor(out=at1(flo, j), in0=work[:, 3 * jj + 2, :], in1=at1(fhi, j).bitcast(F32),
                                            op=ALU.subtract).then_inc(s("f_lo"), 1)

            up(0, True)
            with dve.Fori(1, FT // 2) as i:
                up(i, False)
            for d in range(DT):
                if d == DT - 1:
                    x3_add(dve, d - 1)
                dve.wait_ge(s("d_ps"), d + 1)
                nc.vector.scalar_tensor_tensor(out=x2T[:, d, :], in0=ps[:, d, :], scalar=mod[:, 5 * DT + d:5 * DT + d + 1],
                                               in1=x2T[:, d, :], op0=ALU.mult, op1=ALU.add).then_inc(s("x3_sum"), 1)
                if 1 <= d < DT - 1:
                    x3_add(dve, d - 1)
            dve.wait_ge(s("x3_rms"), 1)
            nc.vector.reciprocal(small[:, 4:4 + TT], small[:, 0:TT]).then_inc(s("x3_rinv"), 1)
            dve.wait_ge(s("x3_rinv"), 1)
            inv = small[:, 4:4 + TT].unsqueeze(2).to_broadcast([P, TT, P])
            for d in Y_DVE:
                dve.wait_ge(s("y_ps"), d + 1)
                nc.vector.tensor_tensor(out=yo[:, :, d * P:(d + 1) * P], in0=ps[:, d, :].rearrange("p (t n) -> p t n", n=P),
                                        in1=inv, op=ALU.mult).then_inc(s("y_dve"), 1)

        @block.tensor
        def _(pe):
            pe.wait_ge(s("consts"), 4)
            pe.wait_ge(s("c_loaded"), 32)
            pe.transpose(ps[:, 7, 0:2 * DT], G[0:2 * DT, 3, :], ident[0:2 * DT, 0:2 * DT]).then_inc(s("c_ps"), 1)
            pe.wait_ge(s("chl_lo"), 1)

            def unit(u):
                pe.wait_ge(w_lo, u + 1)

            for u in range(U_ADA, U_Q):
                k, half = (u - U_ADA) // 2, (u - U_ADA) % 2
                unit(u)
                for b in range(2):
                    for w in (whi, wlo):
                        last = pe.matmul(ps[:, 2 * half + b, :], chl[:, k, :], tile_of(w, u % SLOTS, b, 512),
                                         start=k == 0 and w is whi, stop=k == DT - 1 and w is wlo)
                last.then_inc(w_used, 1)
                t = u // 2
                if u % 2 == 1 and t < KT:
                    pe.wait_ge(s("x_norm"), t + 1)
                    wait(pe, s("xT_dve"), t - 1)
                    wait(pe, s("xT_act"), t - 1)
                    for m in range(DT):
                        last = pe.transpose(ps[:, 4 + 2 * (t % 2) + m // 4, (m % 4) * P:(m % 4 + 1) * P],
                                            xt[:, t, m * P:(m + 1) * P], ident[:])
                    last.then_inc(s("xT_ps"), 1)
                if u == U_Q - 2:
                    pe.wait_ge(s("prm_loaded"), 16 * 8)
                    pe.wait_ge(s("xT_act"), KT)
                    n = R_END0 - 2 * DT
                    pe.transpose(ps[:, 7, 0:n], G[0:n, 0, :], ident[0:n, 0:n]).then_inc(s("prm_ps"), 1)
            pe.wait_ge(s("rows1_act"), 1)
            pe.wait_ge(s("rows1_dve"), 1)
            pe.wait_ge(s("xT_dve"), KT)
            for m in range(2 * DT):
                last = pe.transpose(ps[:, 4, 4 * m:4 * m + 4], rows1[:, m * P:(m + 1) * P], ident[0:4, 0:4])
            last.then_inc(s("cols1_ps"), 1)
            pe.wait_ge(s("prm"), 1)
            pe.wait_ge(s("prm_ffn_loaded"), 16 * 3)
            pe.transpose(ps[:, 7, P:2 * P], G[:, 1, :], ident[:])
            n = R_END - 2 * P
            pe.transpose(ps[:, 7, 2 * P:R_END], G[0:n, 2, :], ident[0:n, 0:n]).then_inc(s("prm_ffn_ps"), 1)

            for m in range(QT):
                u = U_Q + m
                unit(u)
                for k in range(DT):
                    if m == 0:
                        pe.wait_ge(s("h_lo"), k + 1)
                    last = mm3(pe, ps[:, m, :], (tile_of(whi, u % SLOTS, k), tile_of(wlo, u % SLOTS, k)),
                               (hhi[:, k, :], hlo[:, k, :]), k == 0, k == DT - 1)
                last.then_inc(w_used, 1)
            for n, u in enumerate((U_KV, U_KV + 1, U_KR)):
                bank = (4, 6, 0)[n]
                unit(u)
                if n == 0:
                    pe.wait_ge(s("h_lo"), 2 * DT)
                if n == 1:
                    pe.wait_ge(s("prm_ffn"), 1)
                    pe.wait_ge(s("q_sum"), QT - 1)
                    for t in range(TT):
                        last = pe.matmul(ps[:, 3, t:t + 1], work[:, 3, t * P:(t + 1) * P], ones[:, 0:1], start=True, stop=True)
                    last.then_inc(s("qstat_ps"), 1)
                if n == 2:
                    pe.wait_ge(s("cq_lo"), QT)
                project(pe, ps[:, bank + 1, 0:C], u % SLOTS, chi, clo)
                if n == 2:
                    pe.wait_ge(s("k_ssq"), 1)
                    pe.wait_ge(s("q_rms"), 1)
                    pe.matmul(ps[:, 3, 0:C], ones[:], sqk[0][:, T:K], start=True, stop=True)
                    pe.matmul(ps[:, 2, :], ones[:], sqk[0][:, 0:T], start=True, stop=True).then_inc(s("kstat_ps"), 1)
                project(pe, ps[:, bank, :], u % SLOTS, hhi, hlo).then_inc(w_used, 1)
            pe.wait_ge(s("p_raw"), KVT)
            for h in range(HEADS):
                unit(U_UQ + h // 2)
                wait(pe, s("q_rope"), 3 * (h - 3))
                wait(pe, s("q_nope"), h - 3)
                slot = (U_UQ + h // 2) % SLOTS
                for k in range(QT):
                    w = tuple(t[:, slot, (2 * k + h % 2) * P:(2 * k + h % 2 + 1) * P] for t in (whi, wlo))
                    last = mm3(pe, ps[:, 4 + h % 4, :], w, (cqhi[:, k, :], cqlo[:, k, :]), k == 0, k == QT - 1)
                last.then_inc(s("q_ps") if h % 2 == 0 else w_used, 1)

            def keys(pair, part):
                lo, hi = ((0, T), (T, K))[part]
                slot = U_N % SLOTS
                wait(pe, s("k_raw"), 2 * pair + part)
                wait(pe, s("o_val"), 2 * pair - 2)
                for k in range(KVT):
                    w = tuple(t[:, slot, k * 512 + pair * P:k * 512 + (pair + 1) * P] for t in (whi, wlo))
                    last = mm3(pe, ps[:, 6, 0:hi - lo], w, (ckhi[:, k, lo:hi], cklo[:, k, lo:hi]), k == 0, k == KVT - 1)
                last.then_inc(w_used if (pair, part) == (HEADS // 2 - 1, 1) else s("k_ps"), 1)

            pe.wait_ge(s("ck_lo"), KVT)
            pe.wait_ge(s("k_rms"), 1)
            pe.wait_ge(s("kr"), 4)
            unit(U_V)

            def values(kt):
                slot = U_V % SLOTS
                wait(pe, s("v_lo"), kt - 3)
                for k in range(KVT):
                    last = mm3(pe, ps[:, kt % 4, :], (ckhi[:, k, kt * P:(kt + 1) * P], cklo[:, k, kt * P:(kt + 1) * P]),
                               (tile_of(whi, slot, k, 512), tile_of(wlo, slot, k, 512)), k == 0, k == KVT - 1)
                last.then_inc(s("v_ps") if kt < KT - 1 else w_used, 1)

            values(0)
            values(1)
            pe.wait_ge(s("q_rope"), 3 * (HEADS - 1))
            pe.wait_ge(s("q_nope"), HEADS - 1)
            unit(U_N)
            keys(0, 0)
            values(2)
            keys(0, 1)
            for kt in range(3, KT):
                values(kt)

            def scores(g):
                h, t = g // TT, g % TT
                wait(pe, s("p_exp"), g - 1)
                if g == 0:
                    pe.wait_ge(s("q_lo"), HEADS)
                    pe.wait_ge(s("v_lo"), KT)
                    pe.wait_ge(s("kr"), 8)
                pe.wait_ge(s(("k_lo_even", "k_lo_odd")[h % 2]), h // 2 + 1)
                q = tuple(x_[0:QK, h, t * P:(t + 1) * P] for x_ in (qhi, qlo))
                for bank, lo, hi in ((1, T, K), (0, 0, T)):
                    last = mm3(pe, ps[:, 2 * (g % 2) + bank, 0:hi - lo], q,
                               (khi[0:QK, h % 2, lo:hi], klo[0:QK, h % 2, lo:hi]), True, True)
                last.then_inc(s("s_ps"), 1)

            def transposes(g):
                pe.wait_ge(s("p_exp"), g + 1)
                for half, lo, hi in ((0, 0, 4), (1, 4, KT)):
                    wait(pe, s("pt_lo" if half else "pt_lo0"), g)
                    for kt in range(lo, hi):
                        last = pe.transpose(ps[:, 4 + half, (kt - lo) * P:(kt - lo + 1) * P], probs(g)[:, kt * P:(kt + 1) * P], ident[:])
                    last.then_inc(s("t_ps" if half else "t_ps0"), 1)

            def output(h, half, part):
                pe.wait_ge(s("pt_lo"), TT * h + 2 * half + 2)
                wait(pe, s("o_val"), h)
                q = slice(half * 2 * P, (half + 1) * 2 * P)
                for kt in range(3 * part, 3 * part + 3):
                    for n, p_ in enumerate((pthi, ptlo)):
                        last = pe.matmul(ps[:, 7, q], vs[:, kt, h, :], p_[:, kt, q], start=kt == 0 and n == 0,
                                         stop=kt == KT - 1 and n == 1)
                if part == 1:
                    last.then_inc(s("pv_ps"), 1)

            def row_factors(h):
                pe.wait_ge(s("k_raw"), min(2 * (h // 2) + 4, HEADS))
                pe.wait_ge(s("diag"), h + 1)
                pe.matmul(ps[:, 6, :], ones[:], diag, start=True, stop=True).then_inc(s("r_ps"), 1)

            scores(0)
            scores(1)
            for g in range(HEADS * TT):
                h, t = g // TT, g % TT
                if g + 2 < HEADS * TT:
                    scores(g + 2)
                new_keys = t == 3 and h % 2 == 0 and h + 2 < HEADS
                if new_keys:
                    keys(h // 2 + 1, 0)
                elif t == 3:
                    output(h, 0, 0)
                if t == 0 and h >= 1:
                    output(h - 1, 0, 1)
                transposes(g)
                if t == 0 and h >= 1:
                    output(h - 1, 1, 0)
                if t == 1 and h >= 1:
                    output(h - 1, 1, 1)
                    row_factors(h - 1)
                if new_keys:
                    output(h, 0, 0)
                    keys(h // 2 + 1, 1)
            output(HEADS - 1, 0, 1)
            for part in range(2):
                output(HEADS - 1, 1, part)
            row_factors(HEADS - 1)

            for j in range(CT):
                for n in range(3):
                    u = U_CONV + 3 * j + n
                    unit(u)
                    wait(pe, s("c_z"), j - 1)
                    project(pe, ps[:, 3 * (j % 2) + n, :], u % SLOTS, hhi, hlo).then_inc(w_used, 1)

            def merge(i, first):
                for dd in range(4):
                    d, b = 4 * i + dd, 4 * (dd % 2)
                    if first and dd == 0:
                        pe.wait_ge(s("c_z"), CT - 1)
                    if not (first and dd < 2):
                        pe.wait_ge(s("m_prod"), 2 * d - 2)
                    for n in range(2):
                        m = 3 * dd + n
                        pe.wait_ge(w_lo, U_MERGE + 12 * i + m + 1)
                        project(pe, ps[:, b + n, :], m % SLOTS, hhi, hlo).then_inc(w_used, 1)
                    m = 3 * dd + 2
                    slot = m % SLOTS
                    pe.wait_ge(w_lo, U_MERGE + 12 * i + m + 1)
                    if first and dd == 0:
                        pe.wait_ge(s("z_lo"), CT)
                        pe.wait_ge(s("o_lo"), HEADS)
                    for k in range(CT):
                        mm3(pe, ps[:, b + 2, :], (tile_of(whi, slot, k), tile_of(wlo, slot, k)),
                            (qhi[:, 2 * k, :], qlo[:, 2 * k, :]), k == 0, k == CT - 1)
                    project(pe, ps[:, b + 3, :], slot, zhi, zlo, kt=CT, k0=CT).then_inc(w_used, 1)

            merge(0, True)
            with pe.Fori(1, 2) as i:
                merge(i, False)

            def mod_rows(b0):
                for b in range(b0, b0 + 4):
                    pe.matmul(ps[0:1, 4 + b % 4, :], ones[:, 0:1], adacc[:, b * 512:(b + 1) * 512], start=True, stop=True).then_inc(s("rows2_ps"), 1)

            def norm2_stat(n):
                lo, hi = HALVES[n]
                pe.wait_ge(s("x2_ssq"), DT + n)
                pe.matmul(ps[:, 4 + n, 0:hi - lo], ones[:], work[:, 2, lo:hi], start=True, stop=True).then_inc(s("x2stat_ps"), 1)

            def residual_in(d):
                wait(pe, s("x2_in"), d - 3)
                for t in range(TT):
                    last = pe.transpose(ps[:, 4 + d % 4, t * P:(t + 1) * P], xtok[:, t, d * P:(d + 1) * P], ident[:])
                last.then_inc(s("xT2_ps"), 1)

            for d in range(DT):
                unit(U_O + d)
                wait(pe, s("x2_sum"), d - 3)
                if d == 0:
                    pe.wait_ge(s("m_lo"), DT - 1)
                    pe.wait_ge(s("m_prod"), 2 * DT - 2)
                    project(pe, ps[:, 0, :], 0, mhi, mlo, kt=DT - 1, stop=False)
                    pe.wait_ge(s("m_lo"), DT)
                    mm3(pe, ps[:, 0, :], (tile_of(whi, 0, DT - 1), tile_of(wlo, 0, DT - 1)), (mhi[:, DT - 1, :], mlo[:, DT - 1, :]),
                        False, True).then_inc(w_used, 1)
                    pe.wait_ge(s("ada2_used"), 4 * DT)
                    mod_rows(0)
                elif d == DT - 1:
                    residual_in(d)
                    for n, (lo, hi) in enumerate(HALVES):
                        if n == 1:
                            pe.wait_ge(s("x2_in"), 7)
                        for k in range(DT):
                            if (n, k) == (1, DT // 2 + 1):
                                norm2_stat(0)
                            last = mm3(pe, ps[:, (3, 6)[n], 0:hi - lo], (tile_of(whi, d % SLOTS, k), tile_of(wlo, d % SLOTS, k)),
                                       (mhi[:, k, lo:hi], mlo[:, k, lo:hi]), k == 0, k == DT - 1)
                        last.then_inc(s("last_half_ps") if n == 0 else w_used, 1)
                else:
                    if d >= 4:
                        residual_in(d)
                    project(pe, ps[:, d % 4, :], d % SLOTS, mhi, mlo).then_inc(w_used, 1)
                if d == 1:
                    pe.wait_ge(s("rows2_act"), 1)
                    mod_rows(4)
                if d == 3:
                    pe.wait_ge(s("xtok_loaded"), 16 * TT)
                    pe.wait_ge(s("rows2_dve"), 1)
                    for m in range(4 * DT):
                        last = pe.transpose(ps[:, 7, m:m + 1], rows2[:, m * P:(m + 1) * P], ident[0:1, 0:1])
                    last.then_inc(s("cols2_ps"), 1)
                    for n in range(3):
                        residual_in(n)
                    pe.wait_ge(s("mods2"), 4)
                    residual_in(3)
            def up(i):
                for jj in range(2):
                    j = 2 * i + jj
                    for n in range(2):
                        m = 2 * jj + n
                        pe.wait_ge(w_lo, U_UP + 4 * i + m + 1)
                        pe.wait_ge(s("up_gate" if n == 0 else "up_val"), 2 * j - 2)
                        project(pe, ps[:, m, :], m, hhi, hlo).then_inc(w_used, 1)

            for n, (lo, hi) in enumerate(HALVES):
                for k in range(DT):
                    if (n, k) == (0, 2):
                        norm2_stat(1)
                    pe.wait_ge(s("h2_lo"), n * DT + k + 1)
                    for m in range(3):
                        if k == 0:
                            unit(U_UP + m)
                        last = mm3(pe, ps[:, m, lo:hi], (tile_of(whi, m, k), tile_of(wlo, m, k)), (hhi[:, k, lo:hi], hlo[:, k, lo:hi]),
                                   k == 0, k == DT - 1)
                        if (n, k) == (1, DT - 1):
                            last.then_inc(w_used, 1)
            unit(U_UP + 3)
            project(pe, ps[:, 3, :], 3, hhi, hlo).then_inc(w_used, 1)
            with pe.Fori(1, FT // 2) as i:
                up(i)

            def down(k, slot, start=False):
                pe.wait_ge(w_lo, U_DOWN + k + 1)
                pe.wait_ge(s("f_lo"), k + 1)
                for n, m in enumerate((4, 5, 6, 7, 0, 1, 2, 3)):
                    if start and n == 4:
                        pe.wait_ge(s("up_val"), 2 * FT)
                    last = mm3(pe, ps[:, m, :], (tile_of(whi, slot, m), tile_of(wlo, slot, m)),
                               (at1(fhi, k), at1(flo, k)), start, False)
                last.then_inc(w_used, 1)

            for k in range(4):
                down(k, k, start=k == 0)
            with pe.Fori(1, (FT - 6) // 4) as i:
                for n in range(4):
                    down(4 * i + n, n)
            for k in range(FT - 6, FT - 3):
                down(k, k % SLOTS)

            def result(d):
                pe.wait_ge(s("y_t"), d + 1)
                for t in range(TT):
                    last = pe.transpose(ps[:, d, t * P:(t + 1) * P], yT[:, d, t * P:(t + 1) * P], ident[:])
                last.then_inc(s("y_ps"), 1)

            pe.wait_ge(w_lo, U_ALL)
            pe.wait_ge(s("f_lo"), FT)
            for m in range(DT):
                for k in range(FT - 3, FT):
                    last = mm3(pe, ps[:, m, :], (tile_of(whi, k % SLOTS, m), tile_of(wlo, k % SLOTS, m)),
                               (fhi[:, k, :], flo[:, k, :]), False, k == FT - 1)
                last.then_inc(s("d_ps"), 1)
                if m >= 1:
                    result(m - 1)
            pe.wait_ge(s("x3_ssq"), DT - 1)
            pe.wait_ge(s("x3_sum"), DT)
            for t in range(TT):
                pe.matmul(ps[:, 7, t:t + 1], work[:, 2, t * P:(t + 1) * P], ones[:, 0:1], start=t == 0, stop=False)
            pe.wait_ge(s("x3_sq"), DT)
            for t in range(TT):
                last = pe.matmul(ps[:, 7, t:t + 1], work[:, (DT - 1) % 2, t * P:(t + 1) * P], ones[:, 0:1], start=False, stop=t == TT - 1)
            last.then_inc(s("x3stat_ps"), 1)
            pe.wait_ge(s("x3_rms"), 1)
            result(DT - 1)


_SHARED = ["x", "c", "ctx", "c_ctx", "w_ada", "b_ada", "norm1_g", "w_in", "q_norm_g", "kv_norm_g", "w_uq", "w_ukv",
           "conv_w", "conv_b", "w_attn_out", "w_conv_out", "w_o", "norm2_g", "w_up", "ffn_conv_w", "ffn_conv_b",
           "w_down", "final_g"]


def rope_table():
    t = np.arange(T)
    axis = ROPE // 2
    inv = np.float32(THETA) ** (-np.arange(0, axis, 2, dtype=np.float32) / np.float32(axis))
    table = np.zeros((2, 2, 2, axis // 2, T), np.float32)
    for a, at in enumerate((t // GRID_W, t % GRID_W)):
        ang = (inv[:, None] * at[None, :].astype(np.float32)).astype(np.float32)
        table[0, a] = np.cos(ang)
        table[1, a, 0] = -np.sin(ang)
        table[1, a, 1] = np.sin(ang)
    return table.reshape(2 * ROPE, T)


def kernel(**inputs):
    import concourse.bacc as bacc
    from concourse.bass_utils import run_bass_kernel_spmd

    nc = bacc.Bacc("TRN2", target_bir_lowering=False, num_devices=1)
    arrays, args = {}, []
    for name in _SHARED:
        a = np.ascontiguousarray(inputs[name])
        if name in ("x", "ctx") or (a.ndim > 1 and name != "c"):
            a = a.reshape(a.shape[1:])
        arrays[name + "_dram"] = a
    arrays["rope_dram"] = rope_table()
    for name, a in arrays.items():
        args.append(nc.dram_tensor(name, a.shape, mybir.dt.from_np(a.dtype), kind="ExternalInput").ap())
    args.append(nc.dram_tensor("out_dram", (T, D), F32, kind="ExternalOutput").ap())
    build(nc, *args)
    r = run_bass_kernel_spmd(nc, [arrays], core_ids=[0])
    return r.results[0]["out_dram"].reshape(1, T, D)
```
